# Optimizing a Trainium2 kernel written in Bass

```python
import jax, jax.numpy as jnp
from jax import lax
import numpy as np

D_MODEL = 2048
BATCH = 1
SEQ = 256
DEPTH = 2

GRID_W = 64
CTX_LEN = 256
N_MIXERS = 2
N_POOL_LAYERS = (DEPTH + N_MIXERS - 1) // N_MIXERS
N_ATTN_LAYERS = DEPTH // N_MIXERS
POOL_WINDOWS = (2, 4, 8, 16)
N_POOL_GROUPS = len(POOL_WINDOWS)
POOL_GROUP_DIM = D_MODEL // N_POOL_GROUPS
HEAD_DIM = 64
N_HEADS = D_MODEL // HEAD_DIM
N_KV_HEADS = N_HEADS // 8
GQA_GROUP = N_HEADS // N_KV_HEADS
ATTN_DIM = N_HEADS * HEAD_DIM
KV_DIM = N_KV_HEADS * HEAD_DIM
WINDOW = 128
Q_BLOCK = 128
KEY_SPAN = Q_BLOCK + 2 * WINDOW
AXIS_ROPE_DIM = HEAD_DIM // 2
ROPE_BASE = 10000.0
D_FF = -(-8 * D_MODEL // (3 * 256)) * 256
RMS_EPS = 1e-6
NEG_INF = -1e30

kernel_name = 'hybrid_pool_swa_dit_trunk'

def rms_norm(x, g):
    xf = x.astype(jnp.float32)
    y = xf * lax.rsqrt(jnp.mean(xf * xf, axis=-1, keepdims=True) + RMS_EPS)
    return (y * g.astype(jnp.float32)).astype(x.dtype)

def modulate(x, shift, scale):
    return x * (1 + scale) + shift

def axial_rope_tables(L):
    rows_n = L // GRID_W
    row = jnp.repeat(jnp.arange(rows_n), GRID_W).astype(jnp.float32)
    col = jnp.tile(jnp.arange(GRID_W), rows_n).astype(jnp.float32)
    inv = 1.0 / (ROPE_BASE ** (jnp.arange(0, AXIS_ROPE_DIM, 2, dtype=jnp.float32) / AXIS_ROPE_DIM))
    ang_r = row[:, None] * inv[None, :]
    ang_c = col[:, None] * inv[None, :]
    ang = jnp.concatenate([ang_r, ang_r, ang_c, ang_c], axis=-1)
    return jnp.cos(ang), jnp.sin(ang)

def _rotate_half(x):
    x1, x2 = jnp.split(x, 2, axis=-1)
    return jnp.concatenate([-x2, x1], axis=-1)

def apply_axial_rope(x, cos, sin):
    L = x.shape[1]
    bshape = (L,) + (1,) * (x.ndim - 3) + (HEAD_DIM,)
    xf = x.astype(jnp.float32)
    rot = jnp.concatenate([_rotate_half(xf[..., :AXIS_ROPE_DIM]), _rotate_half(xf[..., AXIS_ROPE_DIM:])], axis=-1)
    return (xf * cos.reshape(bshape) + rot * sin.reshape(bshape)).astype(x.dtype)

def multiscale_pool_mixer(h, w_pool, pool_scale):
    B, L, _ = h.shape
    hf = h.astype(jnp.float32)
    cs = jnp.concatenate([jnp.zeros((B, 1, D_MODEL), jnp.float32), jnp.cumsum(hf, axis=1)], axis=1)
    t = jnp.arange(L)
    parts = []
    for g, w in enumerate(POOL_WINDOWS):
        lo = jnp.clip(t - w // 2, 0, L)
        hi = jnp.clip(t + w // 2, 0, L)
        sl = slice(g * POOL_GROUP_DIM, (g + 1) * POOL_GROUP_DIM)
        csg = cs[..., sl]
        mean = (csg[:, hi] - csg[:, lo]) / (hi - lo).astype(jnp.float32)[None, :, None]
        parts.append(mean - hf[..., sl])
    p = jnp.stack(parts, axis=2)
    y = jnp.einsum('blgc,gcd->blgd', p, w_pool.astype(jnp.float32)).reshape(B, L, D_MODEL)
    return (y * pool_scale.astype(jnp.float32)).astype(h.dtype)

def _split_qkv(t, w_qkv):
    B, n, _ = t.shape
    qkv = t @ w_qkv
    q = qkv[..., :ATTN_DIM].reshape(B, n, N_KV_HEADS, GQA_GROUP, HEAD_DIM)
    k = qkv[..., ATTN_DIM:ATTN_DIM + KV_DIM].reshape(B, n, N_KV_HEADS, HEAD_DIM)
    v = qkv[..., ATTN_DIM + KV_DIM:].reshape(B, n, N_KV_HEADS, HEAD_DIM)
    return q, k, v

def windowed_gqa_mixer(h, hc, w_qkv, w_o, sinks, cos, sin, with_ctx_out):
    B, L, _ = h.shape
    Lc = hc.shape[1]
    scale = HEAD_DIM ** -0.5
    q, k, v = _split_qkv(h, w_qkv)
    qc, kc, vc = _split_qkv(hc, w_qkv)
    q = apply_axial_rope(q, cos, sin) * scale
    k = apply_axial_rope(k, cos, sin)
    qc = qc * scale
    pad = ((0, 0), (WINDOW, WINDOW), (0, 0), (0, 0))
    kp = jnp.pad(k, pad)
    vp = jnp.pad(v, pad)
    sink = sinks.astype(jnp.float32).reshape(1, N_KV_HEADS, GQA_GROUP, 1, 1)

    def attend_block(b):
        start = b * Q_BLOCK
        qb = lax.dynamic_slice_in_dim(q, start, Q_BLOCK, axis=1)
        kb = lax.dynamic_slice_in_dim(kp, start, KEY_SPAN, axis=1)
        vb = lax.dynamic_slice_in_dim(vp, start, KEY_SPAN, axis=1)
        s_loc = jnp.einsum('bqhgd,bkhd->bhgqk', qb, kb, preferred_element_type=jnp.float32)
        qpos = start + jnp.arange(Q_BLOCK)
        kpos = start - WINDOW + jnp.arange(KEY_SPAN)
        valid = (jnp.abs(qpos[:, None] - kpos[None, :]) <= WINDOW) & (kpos >= 0)[None, :] & (kpos < L)[None, :]
        s_loc = jnp.where(valid, s_loc, NEG_INF)
        s_ctx = jnp.einsum('bqhgd,bkhd->bhgqk', qb, kc, preferred_element_type=jnp.float32)
        s_snk = jnp.broadcast_to(sink, s_loc.shape[:-1] + (1,))
        p = jax.nn.softmax(jnp.concatenate([s_loc, s_ctx, s_snk], axis=-1), axis=-1)
        o = (jnp.einsum('bhgqk,bkhd->bqhgd', p[..., :KEY_SPAN].astype(v.dtype), vb)
             + jnp.einsum('bhgqk,bkhd->bqhgd', p[..., KEY_SPAN:KEY_SPAN + Lc].astype(v.dtype), vc))
        return o

    o = lax.map(attend_block, jnp.arange(L // Q_BLOCK))
    o = jnp.moveaxis(o, 0, 1).reshape(B, L, ATTN_DIM)
    y = o @ w_o
    if not with_ctx_out:
        return y, None
    s = jnp.einsum('bqhgd,bkhd->bhgqk', qc, kc, preferred_element_type=jnp.float32)
    s_snk = jnp.broadcast_to(sink, s.shape[:-1] + (1,))
    p = jax.nn.softmax(jnp.concatenate([s, s_snk], axis=-1), axis=-1)
    oc = jnp.einsum('bhgqk,bkhd->bqhgd', p[..., :Lc].astype(vc.dtype), vc).reshape(B, Lc, ATTN_DIM)
    return y, oc @ w_o

def swiglu(h, w_gate_up, w_down):
    gu = h @ w_gate_up
    return (jax.nn.silu(gu[..., :D_FF]) * gu[..., D_FF:]) @ w_down

def setup_inputs(seed: int = 0) -> dict:
    key = jax.random.key(seed)
    ks = jax.random.split(key, 17)
    nrm = jax.random.normal
    f32 = jnp.float32
    return {
        'x': nrm(ks[0], (BATCH, SEQ, D_MODEL), f32),
        'c': nrm(ks[1], (BATCH, D_MODEL), f32),
        'ctx': nrm(ks[2], (BATCH, CTX_LEN, D_MODEL), f32),
        'c_ctx': nrm(ks[3], (D_MODEL,), f32),
        'w_ada': nrm(ks[4], (DEPTH, D_MODEL, 6 * D_MODEL), f32) * (0.5 * D_MODEL ** -0.5),
        'b_ada': 0.02 * nrm(ks[5], (DEPTH, 6 * D_MODEL), f32),
        'norm_pre_mix': 1.0 + 0.05 * nrm(ks[6], (DEPTH, D_MODEL), f32),
        'norm_post_mix': 1.0 + 0.05 * nrm(ks[7], (DEPTH, D_MODEL), f32),
        'norm_pre_ffn': 1.0 + 0.05 * nrm(ks[8], (DEPTH, D_MODEL), f32),
        'norm_post_ffn': 1.0 + 0.05 * nrm(ks[9], (DEPTH, D_MODEL), f32),
        'w_pool': nrm(ks[10], (N_POOL_LAYERS, N_POOL_GROUPS, POOL_GROUP_DIM, POOL_GROUP_DIM), f32) * POOL_GROUP_DIM ** -0.5,
        'pool_scale': 1.0 + 0.05 * nrm(ks[11], (N_POOL_LAYERS, D_MODEL), f32),
        'w_qkv': nrm(ks[12], (N_ATTN_LAYERS, D_MODEL, ATTN_DIM + 2 * KV_DIM), f32) * D_MODEL ** -0.5,
        'w_o': nrm(ks[13], (N_ATTN_LAYERS, ATTN_DIM, D_MODEL), f32) * ATTN_DIM ** -0.5,
        'attn_sinks': 0.5 * nrm(ks[14], (N_ATTN_LAYERS, N_HEADS), f32),
        'w_gate_up': nrm(ks[15], (DEPTH, D_MODEL, 2 * D_FF), f32) * D_MODEL ** -0.5,
        'w_down': nrm(ks[16], (DEPTH, D_FF, D_MODEL), f32) * D_FF ** -0.5,
    }

def reference(x, c, ctx, c_ctx, w_ada, b_ada, norm_pre_mix, norm_post_mix, norm_pre_ffn, norm_post_ffn,
              w_pool, pool_scale, w_qkv, w_o, attn_sinks, w_gate_up, w_down):
    L = x.shape[1]
    cos, sin = axial_rope_tables(L)
    silu_c = jax.nn.silu(c)
    silu_cc = jax.nn.silu(c_ctx)
    for i in range(DEPTH):
        last = i == DEPTH - 1
        ada = silu_c @ w_ada[i] + b_ada[i]
        sh1, sc1, g1, sh2, sc2, g2 = jnp.split(ada[:, None, :], 6, axis=-1)
        ada_c = silu_cc @ w_ada[i] + b_ada[i]
        csh1, csc1, cg1, csh2, csc2, cg2 = jnp.split(ada_c, 6, axis=-1)

        h = modulate(rms_norm(x, norm_pre_mix[i]), sh1, sc1)
        hc = modulate(rms_norm(ctx, norm_pre_mix[i]), csh1, csc1)
        j = i // N_MIXERS
        if i % N_MIXERS == 0:
            y = multiscale_pool_mixer(h, w_pool[j], pool_scale[j])
            yc = None if last else multiscale_pool_mixer(hc, w_pool[j], pool_scale[j])
        else:
            y, yc = windowed_gqa_mixer(h, hc, w_qkv[j], w_o[j], attn_sinks[j], cos, sin, not last)
        x = x + g1 * rms_norm(y, norm_post_mix[i])
        if not last:
            ctx = ctx + cg1 * rms_norm(yc, norm_post_mix[i])

        h = modulate(rms_norm(x, norm_pre_ffn[i]), sh2, sc2)
        x = x + g2 * rms_norm(swiglu(h, w_gate_up[i], w_down[i]), norm_post_ffn[i])
        if not last:
            hc = modulate(rms_norm(ctx, norm_pre_ffn[i]), csh2, csc2)
            ctx = ctx + cg2 * rms_norm(swiglu(hc, w_gate_up[i], w_down[i]), norm_post_ffn[i])
    return x


_drawn_inputs = setup_inputs


def setup_inputs(seed=0):
    import zlib

    import numpy as np

    out = dict(_drawn_inputs(seed))
    spreads = {}
    factors = {'norm_pre_mix': 2.878, 'norm_post_ffn': 2.923, 'pool_scale': 3.653, 'attn_sinks': 64.0}
    for name, (base, spread) in spreads.items():
        noise = np.random.default_rng([zlib.crc32(name.encode()), seed]).standard_normal(out[name].shape)
        drawn = base * np.exp(spread * noise) if base else spread * noise
        out[name] = __import__('jax').numpy.asarray(drawn.astype(out[name].dtype))
    for name, factor in factors.items():
        out[name] = (out[name] * factor).astype(out[name].dtype)
    return out
```

```python
from contextlib import ExitStack

import concourse.bass as bass
from concourse import mybir

F32 = mybir.dt.float32
F32R = mybir.dt.float32r
ALU = mybir.AluOpType
ACT = mybir.ActivationFunctionType

P = 128
D = 2048
DT = D // P
SEQ = 256
TOK = 2 * SEQ
D_FF = 5632
FT = D_FF // P
CHUNKS = FT // 2
HEAD = 64
N_HEADS = D // HEAD
N_KV = N_HEADS // 8
KV = N_KV * HEAD
WINDOWS = (2, 4, 8, 16)
PAD = max(WINDOWS) // 2
EPS = 1e-6
Q_SCALE = HEAD ** -0.5
MASKED = -1e30

UNIT = 2048
PIECE = UNIT // 2
RAW = 4
RING = 4
ADA_CHUNKS = 6 * D // 512
ADA_EARLY = 20
ADA_BESIDE = CHUNKS - 1
ADA_GAP1 = 4
ADA_GAP2 = 3
assert ADA_EARLY + ADA_BESIDE + ADA_GAP1 + ADA_GAP2 == 2 * ADA_CHUNKS
Q_TILES = D // P
U_FFN0 = 4 * ADA_EARLY + 4
U_GAP1 = U_FFN0 + 3 * FT + 4 * ADA_BESIDE
U_QKV = U_GAP1 + 4 * ADA_GAP1
U_OUT = U_QKV + 4 + Q_TILES
U_GAP2 = U_OUT + DT
U_FFN1 = U_GAP2 + 4 * ADA_GAP2
UNITS = U_FFN1 + 3 * FT
S_FFN0 = 2 * U_FFN0
S_QKV = S_FFN0 + 6 * FT
S_OUT = S_QKV + 2 * (4 + Q_TILES)
S_FFN1 = S_OUT + 2 * DT


def early_order():
    order = []
    for g in range(4):
        order += [("ada", 8 + 2 * g)]
        if g:
            order += [("pool_out", g - 1)]
        order += [("mix", 4 * g), ("mix", 4 * g + 1), ("ada", 9 + 2 * g),
                  ("mix", 4 * g + 2), ("mix", 4 * g + 3), ("pool", g)]
    order += [("ada", 16), ("pool_out", 3), ("post_rstd", 0), ("ada", 17)]
    order += [("update", dt) for dt in range(8)] + [("ada", 18)]
    order += [("update", dt) for dt in range(8, 16)] + [("ada", 19), ("ada_flush", 19)]
    return order


def early_pieces():
    at = {("ada", j): 8 * j for j in range(8)}
    s = 64
    for item in early_order():
        if item[0] in ("ada", "pool"):
            at[item] = s
            s += 8 if item[0] == "ada" else 2
    assert s == S_FFN0
    return at


def build_trunk(nc, stream, x_in, cond, ada_bias, gains, pool_gain, inv_counts, rope, rotation, identity,
                pairs, mask, sinks, out):
    ctx = ExitStack()
    with ctx:
        base = 16512
        RESID, HB, GB, RAWB = 0, 32768, 98304, 114688
        SPLITB, EXTRA = RAWB + RAW * UNIT * 4, RAWB + RAW * UNIT * 4 + 2 * RING * PIECE * 4
        extra = [EXTRA]

        def at(name, shape, offset, dt=F32):
            return nc.alloc_sbuf_tensor_at(name, shape, dt, offset=base + offset)

        def small(name, shape, dt=F32):
            size = 4
            for n in shape[1:]:
                size *= n
            t = at(name, shape, extra[0], dt)
            extra[0] += -(-size // 32) * 32
            assert base + extra[0] <= 229368
            return t

        resid = at("resid", [P, DT, TOK], RESID)
        side = resid[:, :, SEQ:TOK]
        h_hi = at("h_hi", [P, DT, TOK], HB, F32R)
        h_lo = at("h_lo", [P, DT, TOK], HB + 32768, F32R)
        pooled_hi = [at(f"pooled_hi{i}", [P, 4, TOK], HB + 8192 * i, F32R) for i in range(2)]
        pooled_lo = [at(f"pooled_lo{i}", [P, 4, TOK], HB + 16384 + 8192 * i, F32R) for i in range(2)]
        pool_y = at("pool_y", [P, DT, TOK], HB + 32768)
        saved = at("saved", [P, DT, TOK], HB)
        o_hi = at("o_hi", [P, DT, SEQ], HB, F32R)
        o_lo = at("o_lo", [P, DT, SEQ], HB + 16384, F32R)
        key_hi = at("key_hi", [P, 2, TOK], HB + 32768, F32R)
        key_lo = at("key_lo", [P, 2, TOK], HB + 36864, F32R)
        val_hi = at("val_hi", [P, 4, P], HB + 40960, F32R)
        val_lo = at("val_lo", [P, 4, P], HB + 43008, F32R)
        q_hi = [at(f"q_hi{i}", [P, 2, P], HB + 45056 + 1024 * i, F32R) for i in range(2)]
        q_lo = [at(f"q_lo{i}", [P, 2, P], HB + 47104 + 1024 * i, F32R) for i in range(2)]
        probs = at("probs", [P, 4, TOK], HB + 49152)
        pt_hi = at("pt_hi", [P, 4, 4, P], HB + 57344, F32R)
        h1_hi = at("h1_hi", [P, DT, SEQ], HB, F32R)
        h1_lo = at("h1_lo", [P, DT, SEQ], HB + 16384, F32R)
        counts = at("counts", [P, 4, SEQ], GB)
        padded = [at(f"padded{i}", [P, 2, SEQ + 2 * PAD], GB + 4096 + 2176 * i) for i in range(2)]
        window = [at(f"window{i}", [P, 2, SEQ + 2 * PAD], GB + 8448 + 2176 * i) for i in range(2)]
        g_hi = at("g_hi", [P, 4, TOK], GB, F32R)
        g_lo = at("g_lo", [P, 4, TOK], GB + 8192, F32R)
        k32 = at("k32", [P, 2, TOK], GB)
        v32 = at("v32", [P, 4, KV], GB + 4096)
        pt_lo = at("pt_lo", [P, 4, 4, P], GB + 8192, F32R)

        raw = [at(f"raw{i}", [P, UNIT], RAWB + i * UNIT * 4) for i in range(RAW)]
        w_hi = [at(f"w_hi{i}", [P, PIECE], SPLITB + i * PIECE * 4, F32R) for i in range(RING)]
        w_lo = [at(f"w_lo{i}", [P, PIECE], SPLITB + (RING + i) * PIECE * 4, F32R) for i in range(RING)]

        work = [small(f"work{i}", [P, TOK]) for i in range(4)]
        rstd = small("rstd", [P, TOK])
        ada_rows = small("ada_rows", [P, 4, 512])
        ada_acc = ada_rows[:, 0:2, :]
        squares = ada_rows[:, 2:4, :]
        mask_sb = small("mask_sb", [P, 2, TOK])
        rope_sb = small("rope_sb", [P, 2, SEQ])
        rot_sb = small("rot_sb", [P, P])
        ident = small("ident", [P, P])
        ones = small("ones", [P, P])
        bias_sb = small("bias_sb", [P, 12 * DT, 2])
        ada = small("ada", [P, 12 * DT, 2])
        gains_sb = small("gains_sb", [P, 8, DT, 2])
        coef = small("coef", [P, 8, DT, 2])
        pool_gain_sb = small("pool_gain_sb", [P, DT])
        sinks_sb = small("sinks_sb", [P, N_HEADS])
        cond_sb = small("cond_sb", [P, DT, 2])
        csilu = small("csilu", [P, DT, 2])
        cparts = small("cparts", [P, DT, 2, 2], F32R)
        pairs_sb = small("pairs_sb", [4, 2])
        eps_sb = small("eps_sb", [P, 1])
        row_max = small("row_max", [P, 4])
        top = small("top", [P, 4])
        neg_top = small("neg_top", [P, 4])
        sink_gap = small("sink_gap", [P, 4])
        sink_exp = small("sink_exp", [P, 4])
        row_sum = small("row_sum", [P, 4])
        denom = small("denom", [P, 4])
        inv_denom = small("inv_denom", [P, 4])

        banks = [ctx.enter_context(nc.psum_tensor(f"bank{i}", [P, 512], F32)) for i in range(8)]
        spill = nc.dram_tensor("spill", (P, DT * TOK), F32).ap()

        def sem(name):
            return ctx.enter_context(nc.semaphore(name))

        raw_landed = [sem(f"raw_landed{i}") for i in range(RAW)]
        x_landed = sem("x_landed")
        cond_landed = sem("cond_landed")
        consts_landed = sem("consts_landed")
        counts_landed = sem("counts_landed")
        consts_set = sem("consts_set")
        padding_set = sem("padding_set")
        hi_done = sem("hi_done")
        lo_done = sem("lo_done")
        piece_used = sem("piece_used")
        cond_ready = sem("cond_ready")
        csilu_ready = sem("csilu_ready")
        rows_copied = sem("rows_copied")
        cols_done = sem("cols_done")
        ada_added = sem("ada_added")
        mac_done = sem("mac_done")
        gap_used = sem("gap_used")
        coef_ready = sem("coef_ready")
        squared = sem("squared")
        summed = sem("summed")
        std_ready = sem("std_ready")
        rstd_ready = sem("rstd_ready")
        scaled = sem("scaled")
        updated = sem("updated")
        mod_hi = sem("mod_hi")
        mod_lo = sem("mod_lo")
        shifted = sem("shifted")
        window_step = sem("window_step")
        diffed = sem("diffed")
        pooled_hi_done = sem("pooled_hi_done")
        pooled_lo_done = sem("pooled_lo_done")
        spilled = sem("spilled")
        reloaded = sem("reloaded")
        cleared = sem("cleared")
        gate_on = [sem("gate_on0"), sem("gate_on1")]
        product = [sem("product0"), sem("product1")]
        g_hi_done = [sem("g_hi_done0"), sem("g_hi_done1")]
        g_lo_done = [sem("g_lo_done0"), sem("g_lo_done1")]
        down_part = [sem("down_part0"), sem("down_part1")]
        y_added = [sem("y_added0"), sem("y_added1")]
        k_copied = sem("k_copied")
        k_turned = sem("k_turned")
        k_rope = sem("k_rope")
        k_ready = sem("k_ready")
        v_copied = sem("v_copied")
        q_copied = sem("q_copied")
        q_turned = sem("q_turned")
        q_rope = sem("q_rope")
        q_ready = sem("q_ready")
        kv_hi = sem("kv_hi")
        kv_lo = sem("kv_lo")
        qs_hi = sem("qs_hi")
        qs_lo = sem("qs_lo")
        scores = sem("scores")
        masked = sem("masked")
        small_step = sem("small_step")
        sink_step = sem("sink_step")
        weighed = sem("weighed")
        diag_ready = sem("diag_ready")
        turned = sem("turned")
        pt_hi_done = sem("pt_hi_done")
        pt_lo_done = sem("pt_lo_done")
        attended = sem("attended")
        o_copied = sem("o_copied")
        o_hi_done = sem("o_hi_done")
        o_lo_done = sem("o_lo_done")
        proj_copied = sem("proj_copied")
        stored = sem("stored")

        block = ctx.enter_context(nc.Block())
        early = early_order()
        first_piece = early_pieces()

        def is_first(t):
            return isinstance(t, int) and t == 0

        def repeat(eng, n, body):
            body(0)
            with eng.Fori(1, n, 1) as t:
                body(t)

        SQ_X0, SQ_Y0, SQ_X1, SQ_Y2, SQ_X2, SQ_Y3, SQ_X3, SQ_Y4 = (16 * i for i in range(8))
        SC_MIX, SC_U1, SC_M1, SC_U2, SC_M2, SC_U3, SC_M3, SC_U4 = (16 * i for i in range(8))

        def ffn_units(layer):
            if layer == 0:
                return U_FFN0 + 6, 10, (0, 2, 4, 6, 8, 9), (1, 3, 5, 7)
            return U_FFN1 + 6, 6, (0, 1, 2, 3, 4, 5), ()

        def split_piece(eng, part, s, u):
            s0, s_step, t = s
            u0, u_step, _ = u
            slot, half = s0 % RING, s0 % 2
            src = raw[u0 % RAW][:, half * PIECE:(half + 1) * PIECE]
            if part == "hi":
                eng.wait_ge(raw_landed[u0 % RAW], 16 * (u0 // RAW + 1) + t * (4 * u_step))
                if s0 >= RING or not is_first(t):
                    eng.wait_ge(piece_used, s0 - RING + 1 + t * s_step)
                eng.activation(w_hi[slot][:], src, ACT.Copy).then_inc(hi_done, 1)
            else:
                eng.wait_ge(hi_done, s0 + 1 + t * s_step)
                eng.tensor_tensor(w_lo[slot][:], src, w_hi[slot][:].bitcast(F32), ALU.subtract).then_inc(lo_done, 1)

        def split_run(eng, part, s, u, n):
            for i in range(n):
                split_piece(eng, part, (s + i, 0, 0), (u + i // 2, 0, 0))

        def consumed(v):
            if v < U_FFN0 + 6:
                return lo_done, 2 * (v + 1)
            if v < U_GAP1:
                c, k = divmod(v - U_FFN0 - 6, 10)
                if k in (1, 3, 5, 7):
                    return mac_done, 32 * c + 8 * ((k + 1) // 2)
                return lo_done, S_FFN0 + 12 + 12 * c + 2 * ((0, 2, 4, 6, 8, 9).index(k) + 1)
            if v < U_QKV:
                return gap_used, v - U_GAP1 + 1
            if v < U_GAP2:
                return lo_done, S_QKV + 2 * (v - U_QKV + 1)
            if v < U_FFN1:
                return gap_used, 4 * ADA_GAP1 + v - U_GAP2 + 1
            return lo_done, S_FFN1 + 2 * (v - U_FFN1 + 1)

        @block.sync
        def _(sp):
            def load(u0, u_step, t):
                if u0 >= RAW:
                    which, value = consumed(u0 - RAW)
                    later = consumed(u0 - RAW + u_step)[1] - value if u_step else 0
                    sp.wait_ge(which, value + t * later)
                src = stream[u0] if isinstance(t, int) and t == 0 else stream[bass.ds(t * u_step + u0, 1)]
                sp.dma_start(raw[u0 % RAW][:], src).then_inc(raw_landed[u0 % RAW], 16)

            def load_range(lo, hi, step):
                turns = (hi - lo) // step
                if turns > 1:
                    with sp.Fori(0, turns, 1) as t:
                        for i in range(step):
                            load(lo + i, step, t)
                    lo += turns * step
                for u in range(lo, hi):
                    load(u, 0, 0)

            for u in range(RAW):
                load(u, 0, 0)
            load_range(RAW, U_FFN0 + 6 + RAW, RAW)
            load_range(U_FFN0 + 6 + RAW, U_FFN0 + 6 + RAW + 20 * (CHUNKS // 2 - 1), 20)
            load_range(U_FFN0 + 6 + RAW + 20 * (CHUNKS // 2 - 1), U_GAP1 + RAW, UNITS)
            for lo, hi in ((U_GAP1, U_QKV), (U_QKV, U_GAP2), (U_GAP2, U_FFN1), (U_FFN1, UNITS - RAW)):
                load_range(lo + RAW, hi + RAW, RAW)
            sp.wait_ge(stored, 32)

        def stream_slices(tokens):
            return [(v, slice(v * SEQ, (v + 1) * SEQ)) for v in range(tokens // SEQ)]

        LAT = slice(0, SEQ)

        class Norm:
            def __init__(self, tokens, coef_row, shift_row, scaled0, mod0, std0):
                self.tokens, self.coef_row, self.shift_row = tokens, coef_row, shift_row
                self.scaled0, self.mod0, self.std0 = scaled0, mod0, std0

        POST = [Norm(TOK, 1, None, SC_U1, None, 1), Norm(TOK, 3, None, SC_U2, None, 3),
                Norm(SEQ, 5, None, SC_U3, None, 5), Norm(SEQ, 7, None, SC_U4, None, 7)]
        PRE = [Norm(TOK, 0, 0, SC_MIX, None, 0), Norm(TOK, 2, 3 * DT, SC_M1, 0, 2),
               Norm(TOK, 4, 6 * DT, SC_M2, 16, 4), Norm(SEQ, 6, 9 * DT, SC_M3, 32, 6)]

        @block.scalar
        def _(act):
            def square(n, src, tokens, scale=None):
                if n >= 2:
                    act.wait_ge(summed, n - 1)
                kw = {} if scale is None else {"scale": scale}
                act.activation(squares[:, n % 2, 0:tokens], src, ACT.Square, **kw).then_inc(squared, 1)

            def std(norm, bank, sq_end):
                act.wait_ge(summed, sq_end)
                if norm.scaled0:
                    act.wait_ge(scaled, norm.scaled0)
                act.activation(rstd[:, 0:norm.tokens], banks[bank][:, 0:norm.tokens], ACT.Sqrt,
                               scale=1.0 / D, bias=eps_sb[:]).then_inc(std_ready, 1)

            def modulate_hi(norm, dt, hi):
                act.wait_ge(scaled, norm.scaled0 + dt + 1)
                for v, ts in stream_slices(norm.tokens):
                    last = act.activation(hi[:, dt, ts], work[dt % 2][:, ts], ACT.Identity,
                                          bias=ada[:, norm.shift_row + dt, v:v + 1])
                last.then_inc(mod_hi, 1)

            act.dma_start(cond_sb[:], cond).then_inc(cond_landed, 16)
            consts = [(bias_sb, ada_bias), (gains_sb, gains), (pool_gain_sb, pool_gain), (rope_sb, rope),
                      (rot_sb, rotation), (ident, identity), (pairs_sb, pairs), (mask_sb, mask), (sinks_sb, sinks)]
            for dst, src in consts:
                act.dma_start(dst[:], src).then_inc(consts_landed, 16)
            act.dma_start(resid[:], x_in).then_inc(x_landed, 16)
            act.dma_start(counts[:], inv_counts).then_inc(counts_landed, 16)

            act.wait_ge(cond_landed, 16)
            act.activation(csilu[:], cond_sb[:], ACT.Silu).then_inc(cond_ready, 1)
            act.wait_ge(cond_ready, 1)
            act.activation(cparts[:, :, :, 0], csilu[:], ACT.Copy).then_inc(csilu_ready, 1)
            split_run(act, "hi", 0, 0, 16)
            act.wait_ge(x_landed, 16)
            for dt in range(DT):
                square(SQ_X0 + dt, resid[:, dt, :], TOK)
            with act.Fori(1, 4, 1) as t:
                for i in range(16):
                    split_piece(act, "hi", (i, 16, t), (i // 2, 8, t))
            act.wait_ge(consts_set, 1)
            std(PRE[0], 6, SQ_X0 + 16)

            def pooled_round(dt):
                act.wait_ge(diffed, dt + 1)
                if dt >= 8:
                    act.wait_ge(piece_used, first_piece[("pool", dt // 4 - 2)] + 2)
                act.activation(pooled_hi[dt // 4 % 2][:, dt % 4, :], work[2 + dt % 2][:], ACT.Copy) \
                   .then_inc(pooled_hi_done, 1)

            for kind, n in early:
                if kind == "ada":
                    s = first_piece[(kind, n)]
                    split_run(act, "hi", s, s // 2, 8)
                elif kind == "mix":
                    if n == 0:
                        act.wait_ge(ada_added, 8)
                        act.wait_ge(padding_set, 1)
                    act.wait_ge(scaled, SC_MIX + n + 1)
                    if n >= 2:
                        act.wait_ge(diffed, n - 1)
                    for v, ts in stream_slices(TOK):
                        last = act.activation(padded[n % 2][:, v, PAD:PAD + SEQ], work[n % 2][:, ts],
                                              ACT.Identity, bias=ada[:, n, v:v + 1])
                    last.then_inc(shifted, 1)
                    if n % 4:
                        pooled_round(n - 1)
                elif kind == "pool":
                    pooled_round(4 * n + 3)
                    s = first_piece[(kind, n)]
                    split_run(act, "hi", s, s // 2, 2)
                elif kind == "pool_out":
                    act.wait_ge(piece_used, first_piece[("pool", n)] + 2)
                    for i in range(4):
                        dt = 4 * n + i
                        act.activation(pool_y[:, dt, :], banks[i][:], ACT.Copy,
                                       scale=pool_gain_sb[:, dt:dt + 1])
                        square(SQ_Y0 + dt, banks[i][:], TOK, scale=pool_gain_sb[:, dt:dt + 1])
                elif kind == "post_rstd":
                    std(POST[0], 6, SQ_Y0 + 16)
                elif kind == "update":
                    act.wait_ge(updated, n + 1)
                    square(SQ_X1 + n, resid[:, n, :], TOK)

            split_run(act, "hi", S_FFN0, U_FFN0, 4)
            std(PRE[1], 6, SQ_X1 + 16)
            act.dma_start(spill, resid[:].rearrange("p a b -> p (a b)")).then_inc(spilled, 16)
            for dt in range(DT):
                modulate_hi(PRE[1], dt, h_hi)

            def silu_tile(layer, j, par, tokens):
                if par[1] >= 2 or not is_first(par[2]):
                    act.wait_ge(product[layer], j - 1)
                act.activation(work[par[0]][:, 0:tokens], banks[2 * par[0]][:, 0:tokens], ACT.Silu) \
                   .then_inc(gate_on[layer], 1)

            def round_tile(layer, j, slot, tokens):
                act.wait_ge(product[layer], j + 1)
                act.activation(g_hi[:, slot, 0:tokens], work[2 + slot % 2][:, 0:tokens], ACT.Copy) \
                   .then_inc(g_hi_done[layer], 1)

            def ffn_steps(layer, s_base, tokens):
                u_base, u_step, split_off, _ = ffn_units(layer)
                for i in range(4, 12):
                    if i == 7:
                        act.wait_ge(piece_used, s_base + 4)
                        silu_tile(layer, 0, (0, 0, 0), tokens)
                    if i == 11:
                        act.wait_ge(piece_used, s_base + 8)
                        silu_tile(layer, 1, (1, 1, 0), tokens)
                    split_piece(act, "hi", (s_base + i, 0, 0), (u_base - 6 + i // 2, 0, 0))
                    if i == 7:
                        round_tile(layer, 0, 0, tokens)
                    if i == 11:
                        round_tile(layer, 1, 1, tokens)

                def step(par, t):
                    q = s_base + 12 + 12 * par
                    for i in range(12):
                        side_tile = {3: 0, 7: 1}.get(i)
                        j = 2 * par + 2 + (side_tile or 0)
                        if side_tile is not None:
                            act.wait_ge(piece_used, q + i - 3 + t * 24)
                            silu_tile(layer, j + t * 4, (side_tile, j, t), tokens)
                        split_piece(act, "hi", (q + i, 24, t),
                                    (u_base + u_step * par + split_off[i // 2], 2 * u_step, t))
                        if side_tile is not None:
                            round_tile(layer, j + t * 4, 2 * ((par + 1) % 2) + side_tile, tokens)

                with act.Fori(0, CHUNKS // 2 - 1, 1) as t:
                    step(0, t)
                    step(1, t)
                step(0, CHUNKS // 2 - 1)

            ffn_steps(0, S_FFN0, TOK)
            act.wait_ge(piece_used, S_QKV - 8)
            act.dma_start(saved[:].rearrange("p a b -> p (a b)"), spill).then_inc(reloaded, 16)
            for dt in range(DT):
                act.wait_ge(y_added[0], 16 * (CHUNKS - 1) + dt + 1)
                square(SQ_Y2 + dt, resid[:, dt, :], TOK)
            std(POST[1], 7, SQ_Y2 + 16)
            for dt in range(DT):
                act.wait_ge(updated, 16 + dt + 1)
                square(SQ_X2 + dt, resid[:, dt, :], TOK)
            std(PRE[2], 6, SQ_X2 + 16)
            split_run(act, "hi", S_QKV, U_QKV, 4)
            for dt in range(DT):
                modulate_hi(PRE[2], dt, h_hi)

            split_run(act, "hi", S_QKV + 4, U_QKV + 2, 2)
            for m in range(2):
                act.wait_ge(piece_used, S_QKV + 2 * m + 2)
                act.activation(k32[:, m, :], banks[4 + m][:], ACT.Copy).then_inc(k_copied, 1)
                split_run(act, "hi", S_QKV + 6 + m, U_QKV + 3, 1)
            split_run(act, "hi", S_QKV + 8, U_QKV + 4, 4)
            act.wait_ge(piece_used, S_QKV + 8)
            for tt in range(4):
                act.activation(v32[:, tt, :], banks[tt][:, 0:KV], ACT.Copy).then_inc(v_copied, 1)

            def q_quad(t):
                for i in range(4):
                    for half in range(2):
                        split_piece(act, "hi", (S_QKV + 12 + 2 * i + half, 8, t), (U_QKV + 6 + i, 4, t))
                    act.wait_ge(piece_used, t * 8 + S_QKV + 10 + 2 * i)
                    if i >= 2 or not is_first(t):
                        act.wait_ge(q_ready, t * 4 + i - 1)
                    act.activation(work[i % 2][:, LAT], banks[i % 2][:, LAT], ACT.Copy).then_inc(q_copied, 1)

            repeat(act, Q_TILES // 4, q_quad)

            def kv_round(m):
                if m:
                    act.wait_ge(attended, 8)
                else:
                    act.wait_ge(k_ready, 2)
                    act.wait_ge(v_copied, 4)
                for b in range(2):
                    src = k32[64 * b:64 * b + 64, m, :]
                    for side_b in range(2):
                        act.activation(key_hi[64 * side_b:64 * side_b + 64, b, :], src, ACT.Copy)
                act.activation(val_hi[:], v32[:, :, m * P:(m + 1) * P], ACT.Copy).then_inc(kv_hi, 1)

            def q_round(n):
                pair, qt = n // 2, n % 2
                if n == 0:
                    act.wait_ge(q_ready, Q_TILES)
                if n >= 2:
                    act.wait_ge(scores, 4 * (n - 1))
                act.activation(q_hi[n % 2][:], side[:, 2 * pair:2 * pair + 2, qt * P:(qt + 1) * P], ACT.Copy) \
                   .then_inc(qs_hi, 1)

            def weigh(n):
                act.wait_ge(sink_step, n + 1)
                if n:
                    act.wait_ge(diag_ready, 4 * n)
                act.activation(sink_exp[:], sink_gap[:], ACT.Exp)
                for i in range(4):
                    last = act.activation(probs[:, i, :], probs[:, i, :], ACT.Exp, scale=Q_SCALE,
                                          bias=neg_top[:, i:i + 1], accum_out=row_sum[:, i:i + 1])
                    last.then_inc(weighed, 1)

            kv_round(0)
            q_round(0)
            weigh(0)
            q_round(1)
            for n in range(16):
                for i in range(4):
                    act.wait_ge(turned, 4 * n + i + 1)
                    if n and i == 0:
                        act.wait_ge(attended, n)
                    act.activation(pt_hi[:, :, i, :], banks[4 + i % 2][:].rearrange("p (k q) -> p k q", k=4),
                                   ACT.Copy).then_inc(pt_hi_done, 1)
                if n == 7:
                    kv_round(1)
                if n < 15:
                    weigh(n + 1)
                if n < 14:
                    q_round(n + 2)
                act.wait_ge(o_copied, n + 1)
                act.activation(o_hi[:, 2 * (n // 2):2 * (n // 2) + 2, (n % 2) * P:(n % 2 + 1) * P],
                               work[1][:, 0:SEQ].rearrange("p (a q) -> p a q", a=2), ACT.Copy) \
                   .then_inc(o_hi_done, 1)

            def out_quad(t):
                last_turn = isinstance(t, int) and t == DT // 4 - 1
                for i in range(4):
                    if i < 2 or not last_turn:
                        for half in range(2):
                            split_piece(act, "hi", (S_OUT + 4 + 2 * i + half, 8, t), (U_OUT + 2 + i, 4, t))
                    act.wait_ge(piece_used, t * 8 + S_OUT + 2 + 2 * i)
                    act.activation(side[:, bass.ds(t * 4 + i, 1), :].rearrange("p a b -> p (a b)"),
                                   banks[i % 2][:, LAT], ACT.Copy).then_inc(proj_copied, 1)
                    if i >= 2 or not is_first(t):
                        act.wait_ge(summed, t * 4 + SQ_Y3 + i - 1)
                    act.activation(squares[:, i % 2, LAT], banks[i % 2][:, LAT], ACT.Square) \
                       .then_inc(squared, 1)

            out_quad(0)
            with act.Fori(1, DT // 4 - 1, 1) as t:
                out_quad(t)
            out_quad(DT // 4 - 1)

            std(POST[2], 7, SQ_Y3 + 16)
            for dt in range(DT):
                act.wait_ge(updated, 32 + dt + 1)
                square(SQ_X3 + dt, resid[:, dt, LAT], SEQ)
            std(PRE[3], 7, SQ_X3 + 16)
            split_run(act, "hi", S_FFN1, U_FFN1, 4)
            for dt in range(DT):
                modulate_hi(PRE[3], dt, h1_hi)
            ffn_steps(1, S_FFN1, SEQ)
            for dt in range(DT):
                act.wait_ge(y_added[1], 16 * (CHUNKS - 1) + dt + 1)
                square(SQ_Y4 + dt, side[:, dt, :], SEQ)
            std(POST[3], 7, SQ_Y4 + 16)
            for half in range(2):
                act.wait_ge(updated, 48 + 8 * (half + 1))
                act.dma_start(out[:, 8 * half:8 * half + 8, :], resid[:, 8 * half:8 * half + 8, LAT]) \
                   .then_inc(stored, 16)

        @block.vector
        def _(dve):
            def rstd_of(norm):
                dve.wait_ge(std_ready, norm.std0 + 1)
                dve.reciprocal(rstd[:, 0:norm.tokens], rstd[:, 0:norm.tokens]).then_inc(rstd_ready, 1)
                dve.wait_ge(rstd_ready, norm.std0 + 1)

            def scale_tile(norm, dt, src, free):
                if free is not None:
                    dve.wait_ge(*free)
                for v, ts in stream_slices(norm.tokens):
                    last = dve.scalar_tensor_tensor(work[dt % 2][:, ts], src[:, dt, ts],
                                                    coef[:, norm.coef_row, dt, v:v + 1], rstd[:, ts],
                                                    ALU.mult, ALU.mult)
                last.then_inc(scaled, 1)

            def modulate(norm, hi, lo, src):
                def lo_part(dt):
                    dve.wait_ge(mod_hi, norm.mod0 + dt + 1)
                    for v, ts in stream_slices(norm.tokens):
                        last = dve.scalar_tensor_tensor(lo[:, dt, ts], work[dt % 2][:, ts],
                                                        ada[:, norm.shift_row + dt, v:v + 1],
                                                        hi[:, dt, ts].bitcast(F32), ALU.add, ALU.subtract)
                    last.then_inc(mod_lo, 1)

                for dt in range(DT + 1):
                    if dt < DT:
                        scale_tile(norm, dt, src, None if dt < 2 else (mod_lo, norm.mod0 + dt - 1))
                    if dt:
                        lo_part(dt - 1)

            def coefs(row, ada_row, chunks):
                dve.wait_ge(ada_added, chunks)
                src = ada[:, ada_row * DT:(ada_row + 1) * DT, :]
                dve.scalar_tensor_tensor(coef[:, row], src, 1.0 if row % 2 == 0 else 0.0, gains_sb[:, row],
                                         ALU.add, ALU.mult).then_inc(coef_ready, 1)

            def row_copy(j, pieces, bank):
                dve.wait_ge(piece_used, pieces)
                if not (isinstance(j, int) and j < 2):
                    dve.wait_ge(cols_done, j - 1)
                dve.tensor_copy(ada_rows[0:4, bank % 2, :], banks[bank][0:4, :]).then_inc(rows_copied, 1)

            def bias_add(j, n=1):
                dve.wait_ge(cols_done, j + n)
                where = slice(4 * j, 4 * (j + n)) if isinstance(j, int) else bass.ds(j * 4, 4 * n)
                dve.tensor_tensor(ada[:, where, :], banks[7][:, 0:8 * n].rearrange("p (a v) -> p a v", v=2),
                                  bias_sb[:, where, :], ALU.add).then_inc(ada_added, n)

            dve.memset(ones[:], 1.0)
            dve.memset(eps_sb[:], EPS).then_inc(consts_set, 1)
            dve.wait_ge(csilu_ready, 1)
            dve.tensor_tensor(cparts[:, :, :, 1], csilu[:], cparts[:, :, :, 0].bitcast(F32), ALU.subtract) \
               .then_inc(csilu_ready, 1)
            split_run(dve, "lo", 0, 0, 12)
            row_copy(0, 8, 4)
            split_run(dve, "lo", 12, 6, 4)
            dve.wait_ge(consts_landed, 16 * 9)
            bias_add(0)

            def ada_pair(t):
                for k in range(2):
                    for i in range(8):
                        split_piece(dve, "lo", (8 * k + i, 16, t), (4 * k + i // 2, 8, t))
                        if i == 3:
                            row_copy(t * 2 + k - 1, t * 16 + 8 * k, 4 + (k + 1) % 2)
                    bias_add(t * 2 + k - 1)

            with dve.Fori(1, 4, 1) as t:
                ada_pair(t)
            row_copy(7, 64, 5)
            bias_add(7)
            coefs(0, 1, 8)
            rstd_of(PRE[0])
            dve.wait_ge(coef_ready, 1)

            def pooled_rest(dt):
                dve.wait_ge(pooled_hi_done, dt + 1)
                dve.tensor_tensor(pooled_lo[dt // 4 % 2][:, dt % 4, :], work[2 + dt % 2][:],
                                  pooled_hi[dt // 4 % 2][:, dt % 4, :].bitcast(F32), ALU.subtract) \
                   .then_inc(pooled_lo_done, 1)

            for kind, n in early:
                if kind == "ada":
                    s = first_piece[(kind, n)]
                    split_run(dve, "lo", s, s // 2, 4)
                    if n > 8:
                        row_copy(n - 1, first_piece[("ada", n - 1)] + 8, 4 + (n - 1) % 2)
                    split_run(dve, "lo", s + 4, s // 2 + 2, 4)
                    if n > 8:
                        bias_add(n - 1)
                elif kind == "ada_flush":
                    row_copy(n, first_piece[("ada", n)] + 8, 4 + n % 2)
                    bias_add(n)
                elif kind == "mix":
                    scale_tile(PRE[0], n, resid, None if n < 2 else (shifted, n - 1))
                    if n % 4:
                        pooled_rest(n - 1)
                elif kind == "pool":
                    pooled_rest(4 * n + 3)
                    s = first_piece[(kind, n)]
                    split_run(dve, "lo", s, s // 2, 2)
                elif kind == "post_rstd":
                    coefs(1, 2, 12)
                    rstd_of(POST[0])
                    dve.wait_ge(coef_ready, 2)
                elif kind == "update":
                    scale_tile(POST[0], n, pool_y, (shifted, 16) if n < 2 else (updated, n - 1))

            coefs(2, 4, 20)
            split_run(dve, "lo", S_FFN0, U_FFN0, 4)
            rstd_of(PRE[1])
            dve.wait_ge(coef_ready, 3)
            dve.wait_ge(updated, 16)
            modulate(PRE[1], h_hi, h_lo, resid)

            def product_tile(layer, j, par, tokens):
                dve.wait_ge(gate_on[layer], j + 1)
                if not (isinstance(j, int) and j < 2):
                    dve.wait_ge(g_lo_done[layer], j - 1)
                dve.tensor_tensor(work[2 + par][:, 0:tokens], work[par][:, 0:tokens],
                                  banks[2 * par + 1][:, 0:tokens], ALU.mult).then_inc(product[layer], 1)

            def product_lo(layer, j, slot, tokens):
                dve.wait_ge(g_hi_done[layer], j + 1)
                dve.tensor_tensor(g_lo[:, slot, 0:tokens], work[2 + slot % 2][:, 0:tokens],
                                  g_hi[:, slot, 0:tokens].bitcast(F32), ALU.subtract).then_inc(g_lo_done[layer], 1)

            def mac_tile(n, par, t, u0):
                k = n % 4
                if k == 0:
                    dve.wait_ge(raw_landed[u0 % RAW], 16 * (u0 // RAW + 1) + t * 80)
                if n == 0:
                    dve.wait_ge(cols_done, ADA_EARLY + par + t * 2)
                else:
                    dve.wait_ge(mac_done, 32 * par + 2 * n + t * 64)
                for v in range(2):
                    w = raw[u0 % RAW][:, k * 512:(k + 1) * 512]
                    c = csilu[:, n, v:v + 1]
                    if n == 0:
                        dve.tensor_scalar(ada_acc[:, v, :], w, c, None, ALU.mult).then_inc(mac_done, 1)
                    else:
                        dve.scalar_tensor_tensor(ada_acc[:, v, :], w, c, ada_acc[:, v, :], ALU.mult, ALU.add) \
                           .then_inc(mac_done, 1)

            def ffn_steps(layer, s_base, tokens, y):
                u_base, u_step, split_off, mac_off = ffn_units(layer)
                for i in range(4, 12):
                    if i == 7:
                        product_tile(layer, 0, 0, tokens)
                    if i == 11:
                        product_tile(layer, 1, 1, tokens)
                    split_piece(dve, "lo", (s_base + i, 0, 0), (u_base - 6 + i // 2, 0, 0))
                    if i == 7:
                        product_lo(layer, 0, 0, tokens)
                    if i == 11:
                        product_lo(layer, 1, 1, tokens)

                def add_down(dt, q, parts, t):
                    if dt % 4 == 3:
                        dve.wait_ge(piece_used, q + dt // 4 + 1 + t * 24)
                    else:
                        dve.wait_ge(down_part[layer], parts + 3 * (dt // 4) + dt % 4 + 1 + t * 24)
                    dve.tensor_tensor(y[:, dt, :], y[:, dt, :], banks[4 + dt % 3][:, 0:tokens], ALU.add) \
                       .then_inc(y_added[layer], 1)

                def step(par, t):
                    q = s_base + 12 + 12 * par
                    ub = u_base + u_step * par
                    for i in range(12):
                        side_tile = {3: 0, 7: 1}.get(i)
                        j = 2 * par + 2 + (side_tile or 0)
                        if side_tile is not None:
                            product_tile(layer, j + t * 4, side_tile, tokens)
                        if i >= 8:
                            for dt in range(4 * (i - 8), 4 * (i - 8) + 4):
                                add_down(dt, q + 4, 12 * par, t)
                        split_piece(dve, "lo", (q + i, 24, t), (ub + split_off[i // 2], 2 * u_step, t))
                        if mac_off and i % 2 == 1 and i < 8:
                            for k in range(4):
                                mac_tile(4 * (i // 2) + k, par, t, ub + mac_off[i // 2])
                        if side_tile is not None:
                            product_lo(layer, j + t * 4, 2 * ((par + 1) % 2) + side_tile, tokens)
                        if mac_off and i == 11:
                            bias_add(ADA_EARLY + par + t * 2)

                dve.wait_ge(cleared, layer + 1)
                with dve.Fori(0, CHUNKS // 2 - 1, 1) as t:
                    step(0, t)
                    step(1, t)
                step(0, CHUNKS // 2 - 1)
                for dt in range(DT):
                    add_down(dt, s_base + 12 * (CHUNKS - 1) + 8, 12 * (CHUNKS - 1), 0)

            ffn_steps(0, S_FFN0, TOK, resid)

            coefs(3, 5, ADA_CHUNKS)
            coefs(4, 7, ADA_CHUNKS + 8)
            coefs(5, 8, ADA_CHUNKS + 12)
            rstd_of(POST[1])
            dve.wait_ge(coef_ready, 6)
            dve.wait_ge(reloaded, 16)
            for dt in range(DT):
                scale_tile(POST[1], dt, resid, None if dt < 2 else (updated, 16 + dt - 1))
            rstd_of(PRE[2])
            split_run(dve, "lo", S_QKV, U_QKV, 4)
            dve.wait_ge(updated, 32)
            modulate(PRE[2], h_hi, h_lo, resid)

            def gap_rows(n, units, chunks, bank):
                dve.wait_ge(gap_used, units)
                dve.wait_ge(cols_done, chunks)
                for i in range(n):
                    dve.tensor_copy(ada_rows[0:2, i, :], banks[bank + i][0:2, :]).then_inc(rows_copied, 1)

            gap_rows(ADA_GAP1, 4 * ADA_GAP1, ADA_EARLY + ADA_BESIDE, 0)

            cos, sin = rope_sb[:, 0, :], rope_sb[:, 1, :]
            split_run(dve, "lo", S_QKV + 4, U_QKV + 2, 4)
            bias_add(ADA_EARLY + ADA_BESIDE, ADA_GAP1)
            coefs(6, 10, ADA_CHUNKS + 20)
            for m in range(2):
                lat = k32[:, m, LAT]
                dve.wait_ge(k_turned, m + 1)
                dve.tensor_tensor(work[2 + m][:, LAT], banks[6 + m][:, LAT], sin, ALU.mult)
                dve.tensor_tensor(lat, lat, cos, ALU.mult).then_inc(k_rope, 1)
                dve.wait_ge(k_rope, m + 1)
                dve.tensor_tensor(lat, lat, work[2 + m][:, LAT], ALU.add).then_inc(k_ready, 1)
            split_run(dve, "lo", S_QKV + 8, U_QKV + 4, 4)

            def q_finish(j, i):
                dve.wait_ge(q_turned, j + 1)
                if isinstance(j, int) and j < 2:
                    dve.wait_ge(k_ready, 2)
                else:
                    dve.wait_ge(q_ready, j - 1)
                dst = side[:, bass.ds(j, 1), :].rearrange("p a b -> p (a b)")
                dve.tensor_tensor(work[2 + i % 2][:, LAT], banks[2 + i % 2][:, LAT], sin, ALU.mult)
                dve.tensor_tensor(dst, work[i % 2][:, LAT], cos, ALU.mult).then_inc(q_rope, 1)
                dve.wait_ge(q_rope, j + 1)
                dve.tensor_tensor(dst, dst, work[2 + i % 2][:, LAT], ALU.add).then_inc(q_ready, 1)

            def q_quad(t):
                for i in range(4):
                    if i or not is_first(t):
                        q_finish(t * 4 + i - 1, i + 3)
                    for half in range(2):
                        split_piece(dve, "lo", (S_QKV + 12 + 2 * i + half, 8, t), (U_QKV + 6 + i, 4, t))

            repeat(dve, Q_TILES // 4, q_quad)
            q_finish(Q_TILES - 1, 3)

            def kv_rest(m):
                dve.wait_ge(kv_hi, m + 1)
                for b in range(2):
                    own = slice(64 * b, 64 * b + 64)
                    dve.tensor_tensor(key_lo[own, b, :], k32[own, m, :], key_hi[own, b, :].bitcast(F32),
                                      ALU.subtract).then_inc(kv_lo, 1)
                dve.tensor_tensor(val_lo[:], v32[:, :, m * P:(m + 1) * P], val_hi[:].bitcast(F32),
                                  ALU.subtract)
                dve.wait_ge(kv_lo, 4 * m + 2)
                for b in range(2):
                    own, other = slice(64 * b, 64 * b + 64), slice(64 * (1 - b), 64 * (1 - b) + 64)
                    dve.tensor_copy(key_lo[other, b, :], key_lo[own, b, :].bitcast(F32)).then_inc(kv_lo, 1)

            def q_rest(n):
                pair, qt = n // 2, n % 2
                dve.wait_ge(qs_hi, n + 1)
                dve.tensor_tensor(q_lo[n % 2][:], side[:, 2 * pair:2 * pair + 2, qt * P:(qt + 1) * P],
                                  q_hi[n % 2][:].bitcast(F32), ALU.subtract).then_inc(qs_lo, 1)

            def head_max(n):
                pair, qt = n // 2, n % 2
                for i in range(4):
                    dve.wait_ge(scores, 4 * n + i + 1)
                    if n and i == 0:
                        dve.wait_ge(turned, 4 * n)
                    dve.tensor_tensor_reduce(probs[:, i, :], banks[i][:], mask_sb[:, qt, :], 1.0, 2 * MASKED,
                                             ALU.add, ALU.max, row_max[:, i:i + 1]).then_inc(masked, 1)
                own_sinks = sinks_sb[:, 4 * pair:4 * pair + 4]
                dve.wait_ge(masked, 4 * n + 4)
                dve.scalar_tensor_tensor(top[:], row_max[:], Q_SCALE, own_sinks, ALU.mult, ALU.max) \
                   .then_inc(small_step, 1)
                dve.wait_ge(small_step, 3 * n + 1)
                dve.tensor_scalar(neg_top[:], top[:], -1.0, None, ALU.mult)
                dve.tensor_tensor(sink_gap[:], own_sinks, top[:], ALU.subtract).then_inc(sink_step, 1)

            def normalisers(n):
                dve.wait_ge(weighed, 4 * n + 4)
                dve.tensor_tensor(denom[:], row_sum[:], sink_exp[:], ALU.add).then_inc(small_step, 1)
                dve.wait_ge(small_step, 3 * n + 2)
                dve.reciprocal(inv_denom[:], denom[:]).then_inc(small_step, 1)
                dve.wait_ge(small_step, 3 * n + 3)
                for i in range(4):
                    dve.tensor_scalar(work[0][:, i * P:(i + 1) * P], ident[:], inv_denom[:, i:i + 1], None,
                                      ALU.mult).then_inc(diag_ready, 1)

            kv_rest(0)
            q_rest(0)
            head_max(0)
            for n in range(16):
                if n < 15:
                    q_rest(n + 1) if n != 7 else None
                normalisers(n)
                for i in range(4):
                    dve.wait_ge(pt_hi_done, 4 * n + i + 1)
                    dve.tensor_tensor(pt_lo[:, :, i, :], banks[4 + i % 2][:].rearrange("p (k q) -> p k q", k=4),
                                      pt_hi[:, :, i, :].bitcast(F32), ALU.subtract).then_inc(pt_lo_done, 1)
                if n == 7:
                    kv_rest(1)
                    q_rest(8)
                if n < 15:
                    head_max(n + 1)
                dve.wait_ge(attended, n + 1)
                rows = slice(64 * (n // 4 % 2), 64 * (n // 4 % 2) + 64)
                got = banks[6 + n % 2][:].rearrange("p (a b q) -> p a b q", a=2, b=2)
                for b in range(2):
                    last = dve.tensor_copy(work[1][64 * b:64 * b + 64, 0:SEQ].rearrange("p (a q) -> p a q", a=2),
                                           got[rows, :, b, :])
                last.then_inc(o_copied, 1)
                dve.wait_ge(o_hi_done, n + 1)
                where = (slice(None), slice(2 * (n // 2), 2 * (n // 2) + 2), slice((n % 2) * P, (n % 2 + 1) * P))
                dve.tensor_tensor(o_lo[where], work[1][:, 0:SEQ].rearrange("p (a q) -> p a q", a=2),
                                  o_hi[where].bitcast(F32), ALU.subtract).then_inc(o_lo_done, 1)

            with dve.Fori(0, DT // 4 - 1, 1) as t:
                for i in range(8):
                    split_piece(dve, "lo", (S_OUT + 4 + i, 8, t), (U_OUT + 2 + i // 2, 4, t))
            split_run(dve, "lo", S_FFN1 - 4, U_GAP2 - 2, 4)
            rstd_of(POST[2])
            dve.wait_ge(proj_copied, 16)
            for dt in range(DT):
                scale_tile(POST[2], dt, side, None if dt < 2 else (updated, 32 + dt - 1))
            rstd_of(PRE[3])
            split_run(dve, "lo", S_FFN1, U_FFN1, 4)
            dve.wait_ge(coef_ready, 7)
            dve.wait_ge(updated, 48)
            modulate(PRE[3], h1_hi, h1_lo, resid)
            gap_rows(ADA_GAP2, 4 * (ADA_GAP1 + ADA_GAP2), 2 * ADA_CHUNKS - ADA_GAP2, 4)
            bias_add(2 * ADA_CHUNKS - ADA_GAP2, ADA_GAP2)
            coefs(7, 11, 2 * ADA_CHUNKS)
            ffn_steps(1, S_FFN1, SEQ, side)
            rstd_of(POST[3])
            dve.wait_ge(coef_ready, 8)
            for dt in range(DT):
                scale_tile(POST[3], dt, side, None if dt < 2 else (updated, 48 + dt - 1))

        @block.gpsimd
        def _(pool):
            for i in range(2):
                last = pool.memset(padded[i][:], 0.0)
            last.then_inc(padding_set, 1)
            pool.wait_ge(padding_set, 1)
            pool.wait_ge(counts_landed, 16)

            steps = [0]

            def step(ins):
                ins.then_inc(window_step, 1)
                steps[0] += 1
                pool.wait_ge(window_step, steps[0])

            def mix(dt):
                w = WINDOWS[dt // 4]
                pool.wait_ge(shifted, dt + 1)
                if dt:
                    pool.wait_ge(diffed, dt)
                src, n = padded[dt % 2], SEQ + 2 * PAD
                span = 1
                while span < w:
                    dst = window[0] if src is not window[0] else window[1]
                    n -= span
                    step(pool.tensor_tensor(dst[:, :, 0:n], src[:, :, 0:n], src[:, :, span:span + n], ALU.add))
                    src, span = dst, 2 * span
                other = window[0] if src is not window[0] else window[1]
                for v in range(2):
                    last = pool.tensor_tensor(other[:, v, 0:SEQ], src[:, v, PAD - w // 2:PAD - w // 2 + SEQ],
                                              counts[:, dt // 4, :], ALU.mult)
                step(last)
                if dt >= 2:
                    pool.wait_ge(pooled_lo_done, dt - 1)
                pool.tensor_tensor(work[2 + dt % 2][:].rearrange("p (v t) -> p v t", v=2), other[:, :, 0:SEQ],
                                   padded[dt % 2][:, :, PAD:PAD + SEQ], ALU.subtract).then_inc(diffed, 1)

            for dt in range(DT):
                mix(dt)

            def update(first, tokens, old):
                for dt in range(DT):
                    pool.wait_ge(scaled, first + dt + 1)
                    pool.tensor_tensor(resid[:, dt, 0:tokens], work[dt % 2][:, 0:tokens], old[:, dt, 0:tokens],
                                       ALU.add).then_inc(updated, 1)

            update(SC_U1, TOK, resid)
            pool.wait_ge(spilled, 16)
            pool.wait_ge(mod_lo, 16)
            pool.memset(resid[:], 0.0).then_inc(cleared, 1)
            pool.wait_ge(reloaded, 16)
            update(SC_U2, TOK, saved)
            update(SC_U3, SEQ, resid)
            pool.memset(side, 0.0).then_inc(cleared, 1)
            update(SC_U4, SEQ, resid)

        @block.tensor
        def _(pe):
            def piece_ready(s0, s_step=0, t=0):
                pe.wait_ge(lo_done, s0 + 1 + t * s_step)

            def three_passes(dst, wh, wl, xh, xl, start, stop):
                pe.matmul(dst, wh, xh, start=start, stop=False)
                pe.matmul(dst, wh, xl, start=False, stop=False)
                return pe.matmul(dst, wl, xh, start=False, stop=stop)

            def product_piece(dst, s0, xh, xl, tokens, k0, before=None, s_step=0, t=0):
                piece_ready(s0, s_step, t)
                slot = s0 % RING
                for i in range(8):
                    k = k0 + i
                    if before is not None:
                        before(k)
                    cols = slice(i * P, (i + 1) * P)
                    last = three_passes(dst, w_hi[slot][:, cols], w_lo[slot][:, cols], xh[:, k, 0:tokens],
                                        xl[:, k, 0:tokens], k == 0, k == DT - 1)
                last.then_inc(piece_used, 1)

            def add_squares(n, bank, tokens):
                pe.wait_ge(squared, n + 1)
                pe.matmul(banks[bank][:, 0:tokens], ones[:], squares[:, n % 2, 0:tokens],
                          start=(n % DT == 0), stop=(n % DT == DT - 1)).then_inc(summed, 1)

            def ada_piece(s0, q, bank, s_step=0, t=0):
                piece_ready(s0, s_step, t)
                slot = s0 % RING
                for i in range(2):
                    k = 2 * q + i
                    parts = cparts[:, k].rearrange("p v h -> p (v h)")
                    for n, w in enumerate((w_hi, w_lo)):
                        last = pe.matmul(banks[bank][0:4, :], parts, w[slot][:, i * 512:(i + 1) * 512],
                                         start=(k == 0 and n == 0), stop=(k == DT - 1 and n == 1))
                last.then_inc(piece_used, 1)

            def turn(row_tile, rows, columns, n=0):
                for i in range(4):
                    last = pe.matmul(banks[7][:, 8 * n + 2 * i:8 * n + 2 * i + 2],
                                     ada_rows[0:rows, row_tile, i * P:(i + 1) * P], columns, start=True, stop=True)
                return last

            def turn_rows(j, row_tile):
                pe.wait_ge(rows_copied, j + 1)
                if not is_first(j):
                    pe.wait_ge(ada_added, j)
                turn(row_tile, 4, pairs_sb[:]).then_inc(cols_done, 1)

            def ada_chunk(j, s0, bank, turned_chunk, s_step=0, t=0):
                if not (isinstance(j, int) and j < 2):
                    pe.wait_ge(rows_copied, j - 1)
                for q in range(8):
                    ada_piece(s0 + q, q, bank, s_step, t)
                    if q == 3 and turned_chunk is not None:
                        turn_rows(turned_chunk, (bank + 1) % 2)

            pe.wait_ge(csilu_ready, 2)
            pe.wait_ge(consts_set, 1)
            pe.wait_ge(consts_landed, 16 * 9)
            ada_chunk(0, 0, 4, None)
            ada_chunk(1, 8, 5, 0)
            for dt in range(DT):
                add_squares(SQ_X0 + dt, 6, TOK)
            with pe.Fori(1, 4, 1) as t:
                for k in range(2):
                    ada_chunk(t * 2 + k, 8 * k, 4 + k, t * 2 + k - 1, 16, t)
            turn_rows(7, 1)
            for kind, n in early:
                if kind == "ada":
                    ada_chunk(n, first_piece[(kind, n)], 4 + n % 2, n - 1 if n > 8 else None)
                elif kind == "ada_flush":
                    turn_rows(n, n % 2)
                elif kind == "pool":
                    pe.wait_ge(pooled_lo_done, 4 * n + 4)
                    if n:
                        pe.wait_ge(squared, SQ_Y0 + 4 * n)
                    for q in range(2):
                        s0 = first_piece[(kind, n)] + q
                        piece_ready(s0)
                        for i in range(2):
                            for k in range(4):
                                cols = slice((4 * i + k) * P, (4 * i + k + 1) * P)
                                last = three_passes(banks[2 * q + i][:], w_hi[s0 % RING][:, cols],
                                                    w_lo[s0 % RING][:, cols], pooled_hi[n % 2][:, k, :],
                                                    pooled_lo[n % 2][:, k, :], k == 0, k == 3)
                        last.then_inc(piece_used, 1)
                elif kind == "pool_out":
                    for i in range(4):
                        add_squares(SQ_Y0 + 4 * n + i, 6, TOK)
                elif kind == "update":
                    add_squares(SQ_X1 + n, 6, TOK)

            def ffn(layer, s_base, tokens, xh, xl, mod0, sq_first, after_first_tile=None):
                def gate_up(s0, j0, first, s_step=0, t=0):
                    for i in range(2):
                        if not first:
                            pe.wait_ge(product[layer], j0 + i - 1)
                        for n in range(2):
                            for half in range(2):
                                wait_x = None
                                if first and i == 0 and n == 0:
                                    wait_x = lambda k: pe.wait_ge(mod_lo, mod0 + k + 1)
                                product_piece(banks[2 * i + n][:, 0:tokens], s0 + 4 * i + 2 * n + half, xh, xl,
                                              tokens, 8 * half, wait_x, s_step, t)
                        if first and i == 0 and after_first_tile is not None:
                            after_first_tile()

                def down(s0, c0, slots, first, sq=None, s_step=0, t=0):
                    pe.wait_ge(g_lo_done[layer], 2 * c0 + 2 + t * 4)
                    for q in range(4):
                        piece_ready(s0 + q, s_step, t)
                        slot = (s0 + q) % RING
                        for i in range(4):
                            dt = 4 * q + i
                            if dt >= 3 or not first:
                                pe.wait_ge(y_added[layer], 16 * c0 + max(dt - 2, 0) + t * 32)
                            for k in range(2):
                                cols = slice((2 * i + k) * P, (2 * i + k + 1) * P)
                                last = three_passes(banks[4 + dt % 3][:, 0:tokens], w_hi[slot][:, cols],
                                                    w_lo[slot][:, cols], g_hi[:, slots + k, 0:tokens],
                                                    g_lo[:, slots + k, 0:tokens], k == 0, k == 1)
                            last.then_inc(piece_used if i == 3 else down_part[layer], 1)
                            if sq is not None and dt >= 2:
                                add_squares(sq + dt - 2, 7, tokens)
                    if sq is not None:
                        add_squares(sq + DT - 2, 7, tokens)
                        add_squares(sq + DT - 1, 7, tokens)

                def turn_beside(par, t):
                    pe.wait_ge(mac_done, 32 * (par + 1) + t * 64)
                    pe.wait_ge(ada_added, ADA_EARLY + par + t * 2)
                    for i in range(4):
                        for v in range(2):
                            last = pe.matmul(banks[7][:, 2 * i + v:2 * i + v + 1],
                                             ada_acc[:, v, i * P:(i + 1) * P], ones[:, 0:1], start=True, stop=True)
                    last.then_inc(cols_done, 1)

                def step(par, t):
                    gate_up(s_base + 8 + 12 * par, t * 4 + 2 * par + 2, False, 24, t)
                    down(s_base + 16 + 12 * par, par, 2 * par, par == 0 and is_first(t), None, 24, t)
                    if layer == 0:
                        turn_beside(par, t)

                gate_up(s_base, 0, True)

                def two_steps(t):
                    step(0, t)
                    step(1, t)

                repeat(pe, CHUNKS // 2 - 1, two_steps)
                step(0, CHUNKS // 2 - 1)
                if layer == 0:
                    pe.wait_ge(ada_added, ADA_EARLY + ADA_BESIDE)
                down(s_base + 12 * (CHUNKS - 1) + 8, CHUNKS - 1, 2, False, sq_first)

            ffn(0, S_FFN0, TOK, h_hi, h_lo, 0, SQ_Y2)

            def gap_chunks(u0, n, bank, sq_at):
                for i in range(n):
                    for k in range(DT):
                        u = u0 + 4 * i + k // 4
                        if k % 4 == 0:
                            pe.wait_ge(raw_landed[u % RAW], 16 * (u // RAW + 1))
                        last = pe.matmul(banks[bank + i][0:2, :], csilu[:, k, :],
                                         raw[u % RAW][:, (k % 4) * 512:(k % 4 + 1) * 512],
                                         start=(k == 0), stop=(k == DT - 1))
                        if k % 4 == 3:
                            last.then_inc(gap_used, 1)
                        if DT * i + k in sq_at:
                            add_squares(*sq_at[DT * i + k])

            def turn_gap(n, units_before):
                pe.wait_ge(rows_copied, units_before + n)
                for i in range(n):
                    last = turn(i, 2, ident[0:2, 0:2], i)
                last.then_inc(cols_done, n)

            pe.wait_ge(product[0], FT)
            gap_chunks(U_GAP1, ADA_GAP1, 0, {16 + 2 * i: (SQ_X2 + i, 6, TOK) for i in range(DT)})

            def key_tile(m):
                for half in range(2):
                    product_piece(banks[4 + m][:], S_QKV + 2 * m + half, h_hi, h_lo, TOK, 8 * half,
                                  (lambda k: pe.wait_ge(mod_lo, 16 + k + 1)) if m == 0 else None)

            def turn_key(m):
                pe.wait_ge(k_copied, m + 1)
                if m == 1:
                    pe.wait_ge(ada_added, ADA_EARLY + ADA_BESIDE + ADA_GAP1)
                pe.matmul(banks[6 + m][:, LAT], rot_sb[:], k32[:, m, LAT], start=True, stop=True) \
                  .then_inc(k_turned, 1)

            key_tile(0)
            turn_gap(ADA_GAP1, ADA_EARLY)
            key_tile(1)
            turn_key(0)
            for q in range(4):
                s0 = S_QKV + 4 + q
                piece_ready(s0)
                for i in range(4):
                    k = 4 * q + i
                    cols = slice(i * KV, (i + 1) * KV)
                    for tt in range(4):
                        ts = slice(tt * P, (tt + 1) * P)
                        last = three_passes(banks[tt][:, 0:KV], h_hi[:, k, ts], h_lo[:, k, ts],
                                            w_hi[s0 % RING][:, cols], w_lo[s0 % RING][:, cols],
                                            k == 0, k == DT - 1)
                last.then_inc(piece_used, 1)
            turn_key(1)
            pe.wait_ge(v_copied, 4)

            def turn_query(j, i):
                pe.wait_ge(q_copied, j + 1)
                pe.matmul(banks[2 + i % 2][:, LAT], rot_sb[:], work[i % 2][:, LAT], start=True, stop=True) \
                  .then_inc(q_turned, 1)

            def q_quad(t):
                for i in range(4):
                    if i >= 2 or not is_first(t):
                        pe.wait_ge(q_copied, t * 4 + i - 1)
                    for half in range(2):
                        product_piece(banks[i % 2][:, LAT], S_QKV + 8 + 2 * i + half, h_hi, h_lo, SEQ, 8 * half,
                                      None, 8, t)
                    if i or not is_first(t):
                        if i >= 3 or not is_first(t):
                            pe.wait_ge(q_ready, t * 4 + i - 2)
                        turn_query(t * 4 + i - 1, i + 3)

            repeat(pe, Q_TILES // 4, q_quad)
            pe.wait_ge(q_ready, Q_TILES - 2)
            turn_query(Q_TILES - 1, 3)

            def score_heads(n):
                b = n // 4 % 2
                pe.wait_ge(kv_lo, 4 * (n // 8) + 4)
                pe.wait_ge(qs_lo, n + 1)
                for i in range(4):
                    if n:
                        pe.wait_ge(masked, 4 * (n - 1) + i + 1)
                    rows = slice(64 * (i % 2), 64 * (i % 2) + 64)
                    qh, ql = q_hi[n % 2][rows, i // 2, :], q_lo[n % 2][rows, i // 2, :]
                    kh, kl = key_hi[rows, b, :], key_lo[rows, b, :]
                    pe.matmul(banks[i][:], qh, kh, start=True, stop=False)
                    pe.matmul(banks[i][:], ql, kh, start=False, stop=False)
                    pe.matmul(banks[i][:], qh, kl, start=False, stop=True).then_inc(scores, 1)

            def turn_probs(n):
                for i in range(4):
                    pe.wait_ge(diag_ready, 4 * n + i + 1)
                    if 4 * n + i >= 2:
                        pe.wait_ge(pt_lo_done, 4 * n + i - 1)
                    for kt in range(4):
                        last = pe.matmul(banks[4 + i % 2][:, kt * P:(kt + 1) * P],
                                         probs[:, i, kt * P:(kt + 1) * P], work[0][:, i * P:(i + 1) * P],
                                         start=True, stop=True)
                    last.then_inc(turned, 1)

            def attend(n):
                pe.wait_ge(pt_lo_done, 4 * n + 4)
                if n >= 2:
                    pe.wait_ge(o_copied, n - 1)
                for kt in range(4):
                    last = three_passes(banks[6 + n % 2][:], val_hi[:, kt, :], val_lo[:, kt, :],
                                        pt_hi[:, kt].rearrange("p h q -> p (h q)"),
                                        pt_lo[:, kt].rearrange("p h q -> p (h q)"), kt == 0, kt == 3)
                last.then_inc(attended, 1)

            score_heads(0)
            for n in range(16):
                turn_probs(n)
                if n < 15 and n != 7:
                    score_heads(n + 1)
                attend(n)
                if n == 7:
                    score_heads(8)

            pe.wait_ge(o_lo_done, 16)

            def out_quad(t):
                for i in range(4):
                    if i >= 2 or not is_first(t):
                        pe.wait_ge(squared, t * 4 + SQ_Y3 + i - 1)
                    for half in range(2):
                        product_piece(banks[i % 2][:, LAT], S_OUT + 2 * i + half, o_hi, o_lo, SEQ, 8 * half,
                                      None, 8, t)
                    if i or not is_first(t):
                        add_proj(t * 4 + i - 1, i + 3, i == 1 and is_first(t))

            def add_proj(dt, i, start, stop=False):
                pe.wait_ge(squared, dt + (SQ_Y3 + 1))
                pe.matmul(banks[7][:, LAT], ones[:], squares[:, i % 2, LAT], start=start,
                          stop=stop, skip_group_check=True).then_inc(summed, 1)

            repeat(pe, DT // 4, out_quad)
            add_proj(DT - 1, 3, False, True)
            gap_chunks(U_GAP2, ADA_GAP2, 4, {8 + i: (SQ_X3 + i, 7, SEQ) for i in range(DT)})
            ffn(1, S_FFN1, SEQ, h1_hi, h1_lo, 32, SQ_Y4, lambda: turn_gap(ADA_GAP2, ADA_EARLY + ADA_GAP1))


def tiles_of(w):
    return w.reshape(w.shape[0] // P, P, w.shape[1] // P, P)


def weight_stream(np, w_ada, w_pool, w_qkv, w_o, w_gate_up, w_down):
    units = np.empty((UNITS, P, UNIT), np.float32)

    def ada_chunk(u, j):
        w = w_ada[j // ADA_CHUNKS][:, j % ADA_CHUNKS * 512:(j % ADA_CHUNKS + 1) * 512]
        units[u:u + 4] = w.reshape(4, 4, P, 512).transpose(0, 2, 1, 3).reshape(4, P, UNIT)

    def column_tile(u, w, j):
        units[u] = w[:, j * P:(j + 1) * P].reshape(DT, P, P).transpose(1, 0, 2).reshape(P, UNIT)

    def swiglu(layer):
        u, u_step, split_off, mac_off = ((U_FFN0 + 6, 10, (0, 2, 4, 6, 8, 9), (1, 3, 5, 7)),
                                         (U_FFN1 + 6, 6, (0, 1, 2, 3, 4, 5), ()))[layer]
        gate_up, down = w_gate_up[layer], w_down[layer]

        def down_unit(at, c, h):
            w = down[c * 2 * P:(c + 1) * 2 * P, h * 1024:(h + 1) * 1024]
            units[at] = w.reshape(2, P, 8, P).transpose(1, 2, 0, 3).reshape(P, UNIT)

        for i, (j, up) in enumerate(((0, 0), (0, 1), (1, 0), (1, 1), (2, 0), (2, 1))):
            column_tile(u - 6 + i, gate_up, j + up * FT)
        for c in range(CHUNKS - 1):
            at = [u + c * u_step + off for off in split_off]
            column_tile(at[0], gate_up, 2 * c + 3)
            column_tile(at[1], gate_up, 2 * c + 3 + FT)
            down_unit(at[2], c, 0)
            down_unit(at[3], c, 1)
            if c < CHUNKS - 2:
                column_tile(at[4], gate_up, 2 * c + 4)
                column_tile(at[5], gate_up, 2 * c + 4 + FT)
            else:
                down_unit(at[4], c + 1, 0)
                down_unit(at[5], c + 1, 1)
            for n, off in enumerate(mac_off):
                j = ADA_EARLY + c
                w = w_ada[j // ADA_CHUNKS][n * 512:(n + 1) * 512, j % ADA_CHUNKS * 512:(j % ADA_CHUNKS + 1) * 512]
                units[u + c * u_step + off] = w.reshape(4, P, 512).transpose(1, 0, 2).reshape(P, UNIT)

    pieces = early_pieces()
    for (kind, n), s in pieces.items():
        if kind == "ada":
            ada_chunk(s // 2, n)
        else:
            units[s // 2] = w_pool[0, n].reshape(4, P, 4, P).transpose(1, 2, 0, 3).reshape(P, UNIT)
    swiglu(0)
    for i in range(ADA_GAP1):
        ada_chunk(U_GAP1 + 4 * i, ADA_EARLY + ADA_BESIDE + i)
    for m in range(2):
        column_tile(U_QKV + m, w_qkv[0], Q_TILES + m)
        w = w_qkv[0][m * 1024:(m + 1) * 1024, D + KV:]
        units[U_QKV + 2 + m] = w.reshape(8, P, KV).transpose(1, 0, 2).reshape(P, UNIT)
    for j in range(Q_TILES):
        column_tile(U_QKV + 4 + j, w_qkv[0], j)
    for j in range(DT):
        column_tile(U_OUT + j, w_o[0], j)
    for i in range(ADA_GAP2):
        ada_chunk(U_GAP2 + 4 * i, 2 * ADA_CHUNKS - ADA_GAP2 + i)
    swiglu(1)
    return units


def shape_tables(np):
    f = np.float32
    t = np.arange(SEQ)
    counts = np.stack([f(1) / (np.clip(t + w // 2, 0, SEQ) - np.clip(t - w // 2, 0, SEQ)).astype(f)
                       for w in WINDOWS])
    inv = f(1) / np.power(f(10000), np.arange(0, HEAD // 2, 2, dtype=f) / f(HEAD // 2))
    row, col = (t // 64).astype(f)[:, None] * inv, (t % 64).astype(f)[:, None] * inv
    angle = np.concatenate([row, row, col, col], axis=-1).T.astype(f)
    rope = np.stack([np.tile(np.cos(angle), (2, 1)), np.tile(np.sin(angle), (2, 1))], axis=1).astype(f)
    rotation = np.zeros((P, P), f)
    for m in range(P):
        half = m % (HEAD // 2) < HEAD // 4
        rotation[m + HEAD // 4 if half else m - HEAD // 4, m] = -1 if half else 1
    mask = np.zeros((P, 2, TOK), f)
    for qt in range(2):
        q = qt * P + np.arange(P)
        mask[:, qt, :SEQ] = np.where(np.abs(q[:, None] - t[None, :]) <= 128, 0, MASKED)
    pairs = np.array([[1, 0], [1, 0], [0, 1], [0, 1]], f)
    return (np.ascontiguousarray(np.broadcast_to(counts, (P, 4, SEQ))), np.ascontiguousarray(rope), rotation,
            np.eye(P, dtype=f), pairs, mask)


def kernel(x, c, ctx, c_ctx, w_ada, b_ada, norm_pre_mix, norm_post_mix, norm_pre_ffn, norm_post_ffn,
           w_pool, pool_scale, w_qkv, w_o, attn_sinks, w_gate_up, w_down):
    import numpy as np
    import concourse.bacc as bacc
    from concourse.bass_utils import run_bass_kernel_spmd

    def feature_major(a):
        return np.asarray(a).reshape(-1, DT, P).transpose(2, 1, 0)

    def twice(a):
        return np.repeat(a[..., None], 2, axis=-1)

    gains = np.stack([np.asarray(g)[layer] for layer in range(2)
                      for g in (norm_pre_mix, norm_post_mix, norm_pre_ffn, norm_post_ffn)])
    counts, rope, rotation, identity, pairs, mask = shape_tables(np)
    arrays = {
        "stream": weight_stream(np, *(np.asarray(a) for a in (w_ada, w_pool, w_qkv, w_o, w_gate_up, w_down))),
        "x_in": np.concatenate([feature_major(x), feature_major(ctx)], axis=2),
        "cond": np.concatenate([feature_major(c), feature_major(c_ctx)], axis=2),
        "ada_bias": twice(np.asarray(b_ada).reshape(12 * DT, P).T),
        "gains": twice(gains.reshape(8, DT, P).transpose(2, 0, 1)),
        "pool_gain": np.asarray(pool_scale)[0].reshape(DT, P).T,
        "inv_counts": counts, "rope": rope, "rotation": rotation, "identity": identity, "pairs": pairs,
        "mask": mask, "sinks": np.broadcast_to(np.asarray(attn_sinks)[0], (P, N_HEADS)),
    }
    arrays = {name: np.ascontiguousarray(a) for name, a in arrays.items()}
    nc = bacc.Bacc("TRN2", target_bir_lowering=False, num_devices=1)
    args = [nc.dram_tensor(name, a.shape, F32, kind="ExternalInput").ap() for name, a in arrays.items()]
    out = nc.dram_tensor("out", (P, DT, SEQ), F32, kind="ExternalOutput").ap()
    build_trunk(nc, *args, out)
    got = run_bass_kernel_spmd(nc, [arrays], core_ids=[0]).results[0]["out"]
    return got.transpose(2, 1, 0).reshape(1, SEQ, D)
```

```python
from contextlib import ExitStack

import concourse.bass as bass
from concourse import mybir

F32 = mybir.dt.float32
F32R = mybir.dt.float32r
ALU = mybir.AluOpType
ACT = mybir.ActivationFunctionType

P = 128
D = 2048
DT = D // P
SEQ = 256
TOK = 2 * SEQ
D_FF = 5632
FT = D_FF // P
CHUNKS = FT // 2
HEAD = 64
N_HEADS = D // HEAD
N_KV = N_HEADS // 8
KV = N_KV * HEAD
WINDOWS = (2, 4, 8, 16)
PAD = max(WINDOWS) // 2
EPS = 1e-6
Q_SCALE = HEAD ** -0.5
MASKED = -1e30

UNIT = 2048
PIECE = UNIT // 2
RAW = 4
RING = 4
ADA_CHUNKS = 6 * D // 512
ADA_EARLY = 20
ADA_BESIDE = CHUNKS - 1
ADA_GAP1 = 4
ADA_GAP2 = 3
assert ADA_EARLY + ADA_BESIDE + ADA_GAP1 + ADA_GAP2 == 2 * ADA_CHUNKS
Q_TILES = D // P
U_FFN0 = 4 * ADA_EARLY + 4
U_GAP1 = U_FFN0 + 3 * FT + 4 * ADA_BESIDE
U_QKV = U_GAP1 + 4 * ADA_GAP1
U_OUT = U_QKV + 4 + Q_TILES
U_GAP2 = U_OUT + DT
U_FFN1 = U_GAP2 + 4 * ADA_GAP2
UNITS = U_FFN1 + 3 * FT
S_FFN0 = 2 * U_FFN0
S_QKV = S_FFN0 + 6 * FT
S_OUT = S_QKV + 2 * (4 + Q_TILES)
S_FFN1 = S_OUT + 2 * DT


SPLIT_BEHIND = (11, 13)
STEPS = ((U_FFN0 + 6, 10, (1, 3, 5, 7, 8, 9), (0, 2, 4, 6)), (U_FFN1 + 6, 6, (0, 1, 2, 3, 4, 5), ()))


HALVES = 24


def early_order():
    order = []
    for h in range(HALVES):
        if h < DT:
            order.append(("scale", h))
        for i in range(4):
            order.append(("piece", 4 * h + i))
            if i == 0 and h < DT:
                order.append(("shift", h))
            if i == 1 and 1 <= h <= DT:
                order.append(("split", h - 1))
            if h % 4 == 2 and 6 <= h <= DT + 2:
                order.append(("evacuate", h - 6 + i))
            tile = 4 * (h - DT - 3) + i - 1
            if tile == -1:
                order.append(("post_rstd", 0))
            if 1 <= tile <= DT:
                order.append(("square", tile - 1))
            if 0 <= tile < DT:
                order.append(("update", tile))
        if h % 4 == 0 and 4 <= h <= DT:
            order.append(("pool", h // 4 - 1))
    return order + [("flush", 0)]


def early_pieces():
    at = {}
    s = 64
    for kind, n in early_order():
        if kind == "piece" and n % 4 == 0:
            at[("half", n // 4)] = s
            s += 4
        elif kind == "pool":
            at[(kind, n)] = s
            s += 2
    assert s == S_FFN0
    return at


def build_trunk(nc, stream, x_in, cond, ada_bias, gains, pool_gain, inv_counts, rope, rotation, identity,
                pairs, mask, sinks, out):
    ctx = ExitStack()
    with ctx:
        base = 16512
        RESID, HB, GB, RAWB = 0, 32768, 98304, 114688
        SPLITB, EXTRA = RAWB + RAW * UNIT * 4, RAWB + RAW * UNIT * 4 + 2 * RING * PIECE * 4
        extra = [EXTRA]

        def at(name, shape, offset, dt=F32):
            return nc.alloc_sbuf_tensor_at(name, shape, dt, offset=base + offset)

        def small(name, shape, dt=F32):
            size = 4
            for n in shape[1:]:
                size *= n
            t = at(name, shape, extra[0], dt)
            extra[0] += -(-size // 32) * 32
            assert base + extra[0] <= 229368
            return t

        resid = at("resid", [P, DT, TOK], RESID)
        side = resid[:, :, SEQ:TOK]
        h_hi = at("h_hi", [P, DT, TOK], HB, F32R)
        h_lo = at("h_lo", [P, DT, TOK], HB + 32768, F32R)
        pooled_hi = [at(f"pooled_hi{i}", [P, 4, TOK], HB + 8192 * i, F32R) for i in range(2)]
        pooled_lo = [at(f"pooled_lo{i}", [P, 4, TOK], HB + 16384 + 8192 * i, F32R) for i in range(2)]
        pool_y = at("pool_y", [P, DT, TOK], HB + 32768)
        saved = at("saved", [P, DT, TOK], HB)
        o_hi = at("o_hi", [P, DT, SEQ], HB, F32R)
        o_lo = at("o_lo", [P, DT, SEQ], HB + 16384, F32R)
        key_hi = at("key_hi", [P, 2, TOK], HB + 32768, F32R)
        key_lo = at("key_lo", [P, 2, TOK], HB + 36864, F32R)
        val_hi = at("val_hi", [P, 4, P], HB + 40960, F32R)
        val_lo = at("val_lo", [P, 4, P], HB + 43008, F32R)
        q_hi = [at(f"q_hi{i}", [P, 2, P], HB + 45056 + 1024 * i, F32R) for i in range(2)]
        q_lo = [at(f"q_lo{i}", [P, 2, P], HB + 47104 + 1024 * i, F32R) for i in range(2)]
        probs0 = at("probs0", [P, 4, TOK], HB + 49152)
        pt_hi = at("pt_hi", [P, 4, 4, P], HB + 57344, F32R)
        h1_hi = at("h1_hi", [P, DT, SEQ], HB, F32R)
        h1_lo = at("h1_lo", [P, DT, SEQ], HB + 16384, F32R)
        counts = at("counts", [P, 4, SEQ], GB)
        padded = [at(f"padded{i}", [P, 2, SEQ + 2 * PAD], GB + 4096 + 2176 * i) for i in range(2)]
        window = [at(f"window{i}", [P, 2, SEQ + 2 * PAD], GB + 8448 + 2176 * i) for i in range(2)]
        g_hi = at("g_hi", [P, 4, TOK], GB, F32R)
        g_lo = at("g_lo", [P, 4, TOK], GB + 8192, F32R)
        k32 = at("k32", [P, 2, TOK], GB)
        v32 = at("v32", [P, 4, KV], GB + 4096)
        pt_lo = at("pt_lo", [P, 4, 4, P], GB + 8192, F32R)

        raw = [at(f"raw{i}", [P, UNIT], RAWB + i * UNIT * 4) for i in range(RAW)]
        w_hi = [at(f"w_hi{i}", [P, PIECE], SPLITB + i * PIECE * 4, F32R) for i in range(RING)]
        w_lo = [at(f"w_lo{i}", [P, PIECE], SPLITB + (RING + i) * PIECE * 4, F32R) for i in range(RING)]

        work = [small(f"work{i}", [P, TOK]) for i in range(4)]
        rstd = small("rstd", [P, TOK])
        ada_rows = small("ada_rows", [P, 4, 512])
        ada_acc = ada_rows[:, 0:2, :]
        squares = ada_rows[:, 2:4, :]
        probs = [probs0, ada_rows]
        diag = [work[0], work[2]]
        mask_sb = small("mask_sb", [P, 2, TOK])
        rope_sb = small("rope_sb", [P, 2, SEQ])
        rot_sb = small("rot_sb", [P, P])
        ident = small("ident", [P, P])
        ones = small("ones", [P, P])
        bias_sb = small("bias_sb", [P, 12 * DT, 2])
        ada = small("ada", [P, 12 * DT, 2])
        gains_sb = small("gains_sb", [P, 8, DT, 2])
        coef = small("coef", [P, 8, DT, 2])
        pool_gain_sb = small("pool_gain_sb", [P, DT])
        sinks_sb = small("sinks_sb", [P, N_HEADS])
        cond_sb = small("cond_sb", [P, DT, 2])
        csilu = small("csilu", [P, DT, 2])
        cparts = small("cparts", [P, DT, 2, 2], F32R)
        pairs_sb = small("pairs_sb", [4, 2])
        eps_sb = small("eps_sb", [P, 1])
        row_max, top, neg_top, sink_gap, sink_exp, row_sum, denom, inv_denom = (
            [small(f"{name}{i}", [P, 4]) for i in range(2)]
            for name in ("row_max", "top", "neg_top", "sink_gap", "sink_exp", "row_sum", "denom", "inv_denom"))

        banks = [ctx.enter_context(nc.psum_tensor(f"bank{i}", [P, 512], F32)) for i in range(8)]
        spill = nc.dram_tensor("spill", (P, DT * TOK), F32).ap()

        def sem(name):
            return ctx.enter_context(nc.semaphore(name))

        raw_landed = [sem(f"raw_landed{i}") for i in range(RAW)]
        x_landed = sem("x_landed")
        cond_landed = sem("cond_landed")
        consts_landed = sem("consts_landed")
        counts_landed = sem("counts_landed")
        consts_set = sem("consts_set")
        padding_set = sem("padding_set")
        hi_done = sem("hi_done")
        lo_done = sem("lo_done")
        piece_used = sem("piece_used")
        cond_ready = sem("cond_ready")
        csilu_ready = sem("csilu_ready")
        rows_copied = sem("rows_copied")
        cols_done = sem("cols_done")
        ada_added = sem("ada_added")
        mac_done = sem("mac_done")
        gap_used = sem("gap_used")
        coef_ready = sem("coef_ready")
        squared = sem("squared")
        summed = sem("summed")
        std_ready = sem("std_ready")
        rstd_ready = sem("rstd_ready")
        scaled = sem("scaled")
        updated = sem("updated")
        mod_hi = sem("mod_hi")
        mod_lo = sem("mod_lo")
        shifted = sem("shifted")
        window_step = sem("window_step")
        diffed = sem("diffed")
        pooled_hi_done = sem("pooled_hi_done")
        pooled_lo_done = sem("pooled_lo_done")
        spilled = sem("spilled")
        reloaded = sem("reloaded")
        cleared = sem("cleared")
        gate_on = [sem("gate_on0"), sem("gate_on1")]
        product = [sem("product0"), sem("product1")]
        g_hi_done = [sem("g_hi_done0"), sem("g_hi_done1")]
        g_lo_done = [sem("g_lo_done0"), sem("g_lo_done1")]
        down_part = [sem("down_part0"), sem("down_part1")]
        y_added = [sem("y_added0"), sem("y_added1")]
        k_copied = sem("k_copied")
        k_turned = sem("k_turned")
        k_rope = sem("k_rope")
        k_ready = sem("k_ready")
        v_copied = sem("v_copied")
        q_copied = sem("q_copied")
        q_turned = sem("q_turned")
        q_rope = sem("q_rope")
        q_ready = sem("q_ready")
        key_hi_done = sem("key_hi_done")
        key_lo_done = sem("key_lo_done")
        val_hi_done = sem("val_hi_done")
        val_lo_done = sem("val_lo_done")
        qs_hi = sem("qs_hi")
        qs_lo = sem("qs_lo")
        scores = sem("scores")
        masked = sem("masked")
        small_step = sem("small_step")
        sink_step = sem("sink_step")
        weighed = sem("weighed")
        diag_ready = sem("diag_ready")
        turned = sem("turned")
        pt_hi_done = sem("pt_hi_done")
        pt_lo_done = sem("pt_lo_done")
        attended = sem("attended")
        o_copied = sem("o_copied")
        o_hi_done = sem("o_hi_done")
        o_lo_done = sem("o_lo_done")
        proj_copied = sem("proj_copied")
        stored = sem("stored")

        block = ctx.enter_context(nc.Block())
        early = early_order()
        first_piece = early_pieces()

        def is_first(t):
            return isinstance(t, int) and t == 0

        def repeat(eng, n, body):
            body(0)
            with eng.Fori(1, n, 1) as t:
                body(t)

        SQ_X0, SQ_Y0, SQ_X1, SQ_Y2, SQ_X2, SQ_Y3, SQ_X3, SQ_Y4 = (16 * i for i in range(8))
        SC_MIX, SC_U1, SC_M1, SC_U2, SC_M2, SC_U3, SC_M3, SC_U4 = (16 * i for i in range(8))

        def split_piece(eng, part, s, u):
            s0, s_step, t = s
            u0, u_step, _ = u
            slot, half = s0 % RING, s0 % 2
            src = raw[u0 % RAW][:, half * PIECE:(half + 1) * PIECE]
            if part == "hi":
                eng.wait_ge(raw_landed[u0 % RAW], 16 * (u0 // RAW + 1) + t * (4 * u_step))
                if s0 >= RING or not is_first(t):
                    eng.wait_ge(piece_used, s0 - RING + 1 + t * s_step)
                eng.activation(w_hi[slot][:], src, ACT.Copy).then_inc(hi_done, 1)
            else:
                eng.wait_ge(hi_done, s0 + 1 + t * s_step)
                eng.tensor_tensor(w_lo[slot][:], src, w_hi[slot][:].bitcast(F32), ALU.subtract).then_inc(lo_done, 1)

        def split_run(eng, part, s, u, n):
            for i in range(n):
                split_piece(eng, part, (s + i, 0, 0), (u + i // 2, 0, 0))

        def consumed(v):
            if v < U_FFN0 + 6:
                return lo_done, 2 * (v + 1)
            if v < U_GAP1:
                c, k = divmod(v - U_FFN0 - 6, 10)
                _, _, split_off, mac_off = STEPS[0]
                if k in mac_off:
                    return mac_done, 32 * c + 8 * (mac_off.index(k) + 1)
                return lo_done, S_FFN0 + 12 + 12 * c + 2 * (split_off.index(k) + 1)
            if v < U_QKV:
                return gap_used, v - U_GAP1 + 1
            if v < U_GAP2:
                return lo_done, S_QKV + 2 * (v - U_QKV + 1)
            if v < U_FFN1:
                return gap_used, 4 * ADA_GAP1 + v - U_GAP2 + 1
            return lo_done, S_FFN1 + 2 * (v - U_FFN1 + 1)

        @block.sync
        def _(sp):
            def load(u0, u_step, t):
                if u0 >= RAW:
                    which, value = consumed(u0 - RAW)
                    later = consumed(u0 - RAW + u_step)[1] - value if u_step else 0
                    sp.wait_ge(which, value + t * later)
                src = stream[u0] if isinstance(t, int) and t == 0 else stream[bass.ds(t * u_step + u0, 1)]
                sp.dma_start(raw[u0 % RAW][:], src).then_inc(raw_landed[u0 % RAW], 16)

            def load_range(lo, hi, step):
                turns = (hi - lo) // step
                if turns > 1:
                    with sp.Fori(0, turns, 1) as t:
                        for i in range(step):
                            load(lo + i, step, t)
                    lo += turns * step
                for u in range(lo, hi):
                    load(u, 0, 0)

            for u in range(RAW):
                load(u, 0, 0)
            load_range(RAW, U_FFN0 + 6 + RAW, RAW)
            load_range(U_FFN0 + 6 + RAW, U_FFN0 + 6 + RAW + 20 * (CHUNKS // 2 - 1), 20)
            load_range(U_FFN0 + 6 + RAW + 20 * (CHUNKS // 2 - 1), U_GAP1 + RAW, UNITS)
            for lo, hi in ((U_GAP1, U_QKV), (U_QKV, U_GAP2), (U_GAP2, U_FFN1), (U_FFN1, UNITS - RAW)):
                load_range(lo + RAW, hi + RAW, RAW)
            sp.wait_ge(stored, 32)

        def stream_slices(tokens):
            return [(v, slice(v * SEQ, (v + 1) * SEQ)) for v in range(tokens // SEQ)]

        LAT = slice(0, SEQ)

        class Norm:
            def __init__(self, tokens, coef_row, shift_row, scaled0, mod0, std0):
                self.tokens, self.coef_row, self.shift_row = tokens, coef_row, shift_row
                self.scaled0, self.mod0, self.std0 = scaled0, mod0, std0

        POST = [Norm(TOK, 1, None, SC_U1, None, 1), Norm(TOK, 3, None, SC_U2, None, 3),
                Norm(SEQ, 5, None, SC_U3, None, 5), Norm(SEQ, 7, None, SC_U4, None, 7)]
        PRE = [Norm(TOK, 0, 0, SC_MIX, None, 0), Norm(TOK, 2, 3 * DT, SC_M1, 0, 2),
               Norm(TOK, 4, 6 * DT, SC_M2, 16, 4), Norm(SEQ, 6, 9 * DT, SC_M3, 32, 6)]

        @block.scalar
        def _(act):
            def square(n, src, tokens, scale=None):
                if n >= 2:
                    act.wait_ge(summed, n - 1)
                kw = {} if scale is None else {"scale": scale}
                act.activation(squares[:, n % 2, 0:tokens], src, ACT.Square, **kw).then_inc(squared, 1)

            def std(norm, bank, sq_end):
                act.wait_ge(summed, sq_end)
                if norm.scaled0:
                    act.wait_ge(scaled, norm.scaled0)
                act.activation(rstd[:, 0:norm.tokens], banks[bank][:, 0:norm.tokens], ACT.Sqrt,
                               scale=1.0 / D, bias=eps_sb[:]).then_inc(std_ready, 1)

            def modulate_hi(norm, dt, hi):
                act.wait_ge(scaled, norm.scaled0 + dt + 1)
                for v, ts in stream_slices(norm.tokens):
                    last = act.activation(hi[:, dt, ts], work[dt % 2][:, ts], ACT.Identity,
                                          bias=ada[:, norm.shift_row + dt, v:v + 1])
                last.then_inc(mod_hi, 1)

            act.dma_start(cond_sb[:], cond).then_inc(cond_landed, 16)
            consts = [(bias_sb, ada_bias), (gains_sb, gains), (pool_gain_sb, pool_gain), (rope_sb, rope),
                      (rot_sb, rotation), (ident, identity), (pairs_sb, pairs), (mask_sb, mask), (sinks_sb, sinks)]
            for dst, src in consts:
                act.dma_start(dst[:], src).then_inc(consts_landed, 16)
            act.dma_start(resid[:], x_in).then_inc(x_landed, 16)
            act.dma_start(counts[:], inv_counts).then_inc(counts_landed, 16)

            act.wait_ge(cond_landed, 16)
            act.activation(csilu[:], cond_sb[:], ACT.Silu).then_inc(cond_ready, 1)
            act.wait_ge(cond_ready, 1)
            act.activation(cparts[:, :, :, 0], csilu[:], ACT.Copy).then_inc(csilu_ready, 1)
            split_run(act, "hi", 0, 0, 16)
            act.wait_ge(x_landed, 16)
            for dt in range(2):
                square(SQ_X0 + dt, resid[:, dt, :], TOK)
            with act.Fori(1, 4, 1) as t:
                for i in range(16):
                    split_piece(act, "hi", (i, 16, t), (i // 2, 8, t))
                    if i % 4 == 3:
                        act.wait_ge(summed, t * 4 + i // 4 - 3)
                        tile = resid[:, bass.ds(t * 4 + (i // 4 - 2), 1), :].rearrange("p a b -> p (a b)")
                        act.activation(squares[:, i // 4 % 2, :], tile, ACT.Square).then_inc(squared, 1)
            for dt in range(DT - 2, DT):
                square(SQ_X0 + dt, resid[:, dt, :], TOK)
            act.wait_ge(consts_set, 1)
            std(PRE[0], 6, SQ_X0 + 16)

            for kind, n in early:
                if kind == "piece":
                    h, i = divmod(n, 4)
                    s = first_piece[("half", h)]
                    split_piece(act, "hi", (s + i, 0, 0), ((s + i) // 2, 0, 0))
                elif kind == "shift":
                    if n == 0:
                        act.wait_ge(ada_added, 8)
                        act.wait_ge(padding_set, 1)
                    act.wait_ge(scaled, SC_MIX + n + 1)
                    if n >= 2:
                        act.wait_ge(diffed, n - 1)
                    for v, ts in stream_slices(TOK):
                        last = act.activation(padded[n % 2][:, v, PAD:PAD + SEQ], work[n % 2][:, ts],
                                              ACT.Identity, bias=ada[:, n, v:v + 1])
                    last.then_inc(shifted, 1)
                elif kind == "split":
                    act.wait_ge(diffed, n + 1)
                    if n >= 8:
                        act.wait_ge(piece_used, first_piece[("pool", n // 4 - 2)] + 2)
                    act.activation(pooled_hi[n // 4 % 2][:, n % 4, :], work[2 + n % 2][:], ACT.Copy) \
                       .then_inc(pooled_hi_done, 1)
                elif kind == "pool":
                    s = first_piece[(kind, n)]
                    split_run(act, "hi", s, s // 2, 2)
                elif kind == "evacuate":
                    act.wait_ge(piece_used, first_piece[("pool", n // 4)] + 2)
                    act.activation(pool_y[:, n, :], banks[n % 4][:], ACT.Copy, scale=pool_gain_sb[:, n:n + 1])
                    square(SQ_Y0 + n, banks[n % 4][:], TOK, scale=pool_gain_sb[:, n:n + 1])
                elif kind == "post_rstd":
                    std(POST[0], 6, SQ_Y0 + 16)
                elif kind == "square":
                    act.wait_ge(updated, n + 1)
                    square(SQ_X1 + n, resid[:, n, :], TOK)

            split_run(act, "hi", S_FFN0, U_FFN0, 4)
            std(PRE[1], 6, SQ_X1 + 16)
            act.dma_start(spill, resid[:].rearrange("p a b -> p (a b)")).then_inc(spilled, 16)
            for dt in range(DT):
                modulate_hi(PRE[1], dt, h_hi)

            def silu_tile(layer, j, par, tokens):
                if par[1] >= 2 or not is_first(par[2]):
                    act.wait_ge(product[layer], j - 1)
                act.activation(work[par[0]][:, 0:tokens], banks[2 * par[0]][:, 0:tokens], ACT.Silu) \
                   .then_inc(gate_on[layer], 1)

            def round_tile(layer, j, slot, tokens):
                act.wait_ge(product[layer], j + 1)
                act.activation(g_hi[:, slot, 0:tokens], work[2 + slot % 2][:, 0:tokens], ACT.Copy) \
                   .then_inc(g_hi_done[layer], 1)

            def ffn_steps(layer, s_base, tokens):
                u_base, u_step, split_off, _ = STEPS[layer]
                for i in range(4, 12):
                    if i == 7:
                        act.wait_ge(piece_used, s_base + 4)
                        silu_tile(layer, 0, (0, 0, 0), tokens)
                    if i == 11:
                        act.wait_ge(piece_used, s_base + 8)
                        silu_tile(layer, 1, (1, 1, 0), tokens)
                    split_piece(act, "hi", (s_base + i, 0, 0), (u_base - 6 + i // 2, 0, 0))
                    if i == 7:
                        round_tile(layer, 0, 0, tokens)
                    if i == 11:
                        round_tile(layer, 1, 1, tokens)

                def step(par, t):
                    q = s_base + 12 + 12 * par
                    for i in range(12):
                        side_tile = {3: 0, 7: 1}.get(i)
                        j = 2 * par + 2 + (side_tile or 0)
                        if side_tile is not None:
                            act.wait_ge(piece_used, q + i - 3 + t * 24)
                            silu_tile(layer, j + t * 4, (side_tile, j, t), tokens)
                        split_piece(act, "hi", (q + i, 24, t),
                                    (u_base + u_step * par + split_off[i // 2], 2 * u_step, t))
                        if side_tile is not None:
                            round_tile(layer, j + t * 4, 2 * ((par + 1) % 2) + side_tile, tokens)

                with act.Fori(0, CHUNKS // 2 - 1, 1) as t:
                    step(0, t)
                    step(1, t)
                step(0, CHUNKS // 2 - 1)

            ffn_steps(0, S_FFN0, TOK)
            act.wait_ge(piece_used, S_QKV - 8)
            act.dma_start(saved[:].rearrange("p a b -> p (a b)"), spill).then_inc(reloaded, 16)
            for dt in range(DT):
                act.wait_ge(y_added[0], 16 * (CHUNKS - 1) + dt + 1)
                square(SQ_Y2 + dt, resid[:, dt, :], TOK)
            std(POST[1], 7, SQ_Y2 + 16)
            for dt in range(DT):
                act.wait_ge(updated, 16 + dt + 1)
                square(SQ_X2 + dt, resid[:, dt, :], TOK)
            std(PRE[2], 6, SQ_X2 + 16)
            for dt in range(DT):
                modulate_hi(PRE[2], dt, h_hi)
                if dt in SPLIT_BEHIND:
                    i = 2 * SPLIT_BEHIND.index(dt)
                    split_run(act, "hi", S_QKV + i, U_QKV + i // 2, 2)

            split_run(act, "hi", S_QKV + 4, U_QKV + 2, 2)
            for m in range(2):
                act.wait_ge(piece_used, S_QKV + 2 * m + 2)
                act.activation(k32[:, m, :], banks[4 + m][:], ACT.Copy).then_inc(k_copied, 1)
                split_run(act, "hi", S_QKV + 6 + m, U_QKV + 3, 1)
            split_run(act, "hi", S_QKV + 8, U_QKV + 4, 4)
            act.wait_ge(piece_used, S_QKV + 8)
            for tt in range(4):
                act.activation(v32[:, tt, :], banks[tt][:, 0:KV], ACT.Copy).then_inc(v_copied, 1)

            def q_quad(t):
                for i in range(4):
                    for half in range(2):
                        split_piece(act, "hi", (S_QKV + 12 + 2 * i + half, 8, t), (U_QKV + 6 + i, 4, t))
                    act.wait_ge(piece_used, t * 8 + S_QKV + 10 + 2 * i)
                    if i >= 2 or not is_first(t):
                        act.wait_ge(q_ready, t * 4 + i - 1)
                    act.activation(work[i % 2][:, LAT], banks[i % 2][:, LAT], ACT.Copy).then_inc(q_copied, 1)

            repeat(act, Q_TILES // 4, q_quad)

            def key_round(m):
                if m:
                    act.wait_ge(scores, 32)
                else:
                    act.wait_ge(k_ready, 2)
                for b in range(2):
                    src = k32[64 * b:64 * b + 64, m, :]
                    for side_b in range(2):
                        last = act.activation(key_hi[64 * side_b:64 * side_b + 64, b, :], src, ACT.Copy)
                last.then_inc(key_hi_done, 1)

            def val_round(m):
                if m:
                    act.wait_ge(attended, 8)
                else:
                    act.wait_ge(v_copied, 4)
                act.activation(val_hi[:], v32[:, :, m * P:(m + 1) * P], ACT.Copy).then_inc(val_hi_done, 1)

            def q_round(n):
                pair, qt = n // 2, n % 2
                if n == 0:
                    act.wait_ge(q_ready, Q_TILES)
                if n >= 2:
                    act.wait_ge(scores, 4 * (n - 1))
                act.activation(q_hi[n % 2][:], side[:, 2 * pair:2 * pair + 2, qt * P:(qt + 1) * P], ACT.Copy) \
                   .then_inc(qs_hi, 1)

            def weigh(n):
                act.wait_ge(sink_step, n + 1)
                p = n % 2
                act.activation(sink_exp[p][:], sink_gap[p][:], ACT.Exp)
                for i in range(4):
                    act.activation(probs[p][:, i, :], probs[p][:, i, :], ACT.Exp, scale=Q_SCALE,
                                   bias=neg_top[p][:, i:i + 1], accum_out=row_sum[p][:, i:i + 1]) \
                       .then_inc(weighed, 1)

            key_round(0)
            q_round(0)
            q_round(1)
            weigh(0)
            val_round(0)
            for n in range(16):
                if n == 8:
                    val_round(1)
                for i in range(4):
                    act.wait_ge(turned, 4 * n + i + 1)
                    if n and i == 0:
                        act.wait_ge(attended, n)
                    act.activation(pt_hi[:, :, i, :], banks[4 + i % 2][:].rearrange("p (k q) -> p k q", k=4),
                                   ACT.Copy).then_inc(pt_hi_done, 1)
                if n < 15:
                    weigh(n + 1)
                if n == 6:
                    key_round(1)
                if n < 14:
                    q_round(n + 2)
                act.wait_ge(o_copied, n + 1)
                act.activation(o_hi[:, 2 * (n // 2):2 * (n // 2) + 2, (n % 2) * P:(n % 2 + 1) * P],
                               work[1][:, 0:SEQ].rearrange("p (a q) -> p a q", a=2), ACT.Copy) \
                   .then_inc(o_hi_done, 1)

            def out_quad(t):
                last_turn = isinstance(t, int) and t == DT // 4 - 1
                for i in range(4):
                    if i < 2 or not last_turn:
                        for half in range(2):
                            split_piece(act, "hi", (S_OUT + 4 + 2 * i + half, 8, t), (U_OUT + 2 + i, 4, t))
                    act.wait_ge(piece_used, t * 8 + S_OUT + 2 + 2 * i)
                    act.activation(side[:, bass.ds(t * 4 + i, 1), :].rearrange("p a b -> p (a b)"),
                                   banks[i % 2][:, LAT], ACT.Copy).then_inc(proj_copied, 1)
                    if i >= 2 or not is_first(t):
                        act.wait_ge(summed, t * 4 + SQ_Y3 + i - 1)
                    act.activation(squares[:, i % 2, LAT], banks[i % 2][:, LAT], ACT.Square) \
                       .then_inc(squared, 1)

            out_quad(0)
            with act.Fori(1, DT // 4 - 1, 1) as t:
                out_quad(t)
            out_quad(DT // 4 - 1)

            std(POST[2], 7, SQ_Y3 + 16)
            for dt in range(DT):
                act.wait_ge(updated, 32 + dt + 1)
                square(SQ_X3 + dt, resid[:, dt, LAT], SEQ)
            std(PRE[3], 7, SQ_X3 + 16)
            for dt in range(DT):
                modulate_hi(PRE[3], dt, h1_hi)
                if dt in SPLIT_BEHIND:
                    i = 2 * SPLIT_BEHIND.index(dt)
                    split_run(act, "hi", S_FFN1 + i, U_FFN1 + i // 2, 2)
            ffn_steps(1, S_FFN1, SEQ)
            for dt in range(DT):
                act.wait_ge(y_added[1], 16 * (CHUNKS - 1) + dt + 1)
                square(SQ_Y4 + dt, side[:, dt, :], SEQ)
            std(POST[3], 7, SQ_Y4 + 16)
            for half in range(2):
                act.wait_ge(updated, 48 + 8 * (half + 1))
                act.dma_start(out[:, 8 * half:8 * half + 8, :], resid[:, 8 * half:8 * half + 8, LAT]) \
                   .then_inc(stored, 16)

        @block.vector
        def _(dve):
            def rstd_of(norm):
                dve.wait_ge(std_ready, norm.std0 + 1)
                dve.reciprocal(rstd[:, 0:norm.tokens], rstd[:, 0:norm.tokens]).then_inc(rstd_ready, 1)
                dve.wait_ge(rstd_ready, norm.std0 + 1)

            def scale_tile(norm, dt, src, free):
                if free is not None:
                    dve.wait_ge(*free)
                for v, ts in stream_slices(norm.tokens):
                    last = dve.scalar_tensor_tensor(work[dt % 2][:, ts], src[:, dt, ts],
                                                    coef[:, norm.coef_row, dt, v:v + 1], rstd[:, ts],
                                                    ALU.mult, ALU.mult)
                last.then_inc(scaled, 1)

            def modulate(norm, hi, lo, src, s=None, u=None):
                def lo_part(dt):
                    dve.wait_ge(mod_hi, norm.mod0 + dt + 1)
                    for v, ts in stream_slices(norm.tokens):
                        last = dve.scalar_tensor_tensor(lo[:, dt, ts], work[dt % 2][:, ts],
                                                        ada[:, norm.shift_row + dt, v:v + 1],
                                                        hi[:, dt, ts].bitcast(F32), ALU.add, ALU.subtract)
                    last.then_inc(mod_lo, 1)

                for dt in range(DT + 1):
                    if dt < DT:
                        scale_tile(norm, dt, src, None if dt < 2 else (mod_lo, norm.mod0 + dt - 1))
                    if dt:
                        lo_part(dt - 1)
                    if s is not None and dt - 1 in SPLIT_BEHIND:
                        i = 2 * SPLIT_BEHIND.index(dt - 1)
                        split_run(dve, "lo", s + i, u + i // 2, 2)

            def coefs(row, ada_row, chunks):
                dve.wait_ge(ada_added, chunks)
                src = ada[:, ada_row * DT:(ada_row + 1) * DT, :]
                dve.scalar_tensor_tensor(coef[:, row], src, 1.0 if row % 2 == 0 else 0.0, gains_sb[:, row],
                                         ALU.add, ALU.mult).then_inc(coef_ready, 1)

            def row_copy(j, pieces, bank):
                dve.wait_ge(piece_used, pieces)
                if not (isinstance(j, int) and j < 2):
                    dve.wait_ge(cols_done, j - 1)
                dve.tensor_copy(ada_rows[0:4, bank % 2, :], banks[bank][0:4, :]).then_inc(rows_copied, 1)

            def bias_add(j, n=1):
                dve.wait_ge(cols_done, j + n)
                where = slice(4 * j, 4 * (j + n)) if isinstance(j, int) else bass.ds(j * 4, 4 * n)
                dve.tensor_tensor(ada[:, where, :], banks[7][:, 0:8 * n].rearrange("p (a v) -> p a v", v=2),
                                  bias_sb[:, where, :], ALU.add).then_inc(ada_added, n)

            dve.memset(ones[:], 1.0)
            dve.memset(eps_sb[:], EPS).then_inc(consts_set, 1)
            dve.wait_ge(csilu_ready, 1)
            dve.tensor_tensor(cparts[:, :, :, 1], csilu[:], cparts[:, :, :, 0].bitcast(F32), ALU.subtract) \
               .then_inc(csilu_ready, 1)
            split_run(dve, "lo", 0, 0, 12)
            row_copy(0, 8, 4)
            split_run(dve, "lo", 12, 6, 4)
            dve.wait_ge(consts_landed, 16 * 9)
            bias_add(0)

            def ada_pair(t):
                for k in range(2):
                    for i in range(8):
                        split_piece(dve, "lo", (8 * k + i, 16, t), (4 * k + i // 2, 8, t))
                        if i == 3:
                            row_copy(t * 2 + k - 1, t * 16 + 8 * k, 4 + (k + 1) % 2)
                    bias_add(t * 2 + k - 1)

            with dve.Fori(1, 4, 1) as t:
                ada_pair(t)
            row_copy(7, 64, 5)
            bias_add(7)
            coefs(0, 1, 8)
            rstd_of(PRE[0])
            dve.wait_ge(coef_ready, 1)

            for kind, n in early:
                if kind == "piece":
                    h, i = divmod(n, 4)
                    s, j = first_piece[("half", h)], 8 + h // 2
                    split_piece(dve, "lo", (s + i, 0, 0), ((s + i) // 2, 0, 0))
                    if h >= 2 and i == 3:
                        if h % 2 == 0:
                            row_copy(j - 1, first_piece[("half", h - 1)] + 4, 4 + (j - 1) % 2)
                        else:
                            bias_add(j - 1)
                elif kind == "scale":
                    scale_tile(PRE[0], n, resid, None if n < 2 else (shifted, n - 1))
                elif kind == "split":
                    dve.wait_ge(pooled_hi_done, n + 1)
                    dve.tensor_tensor(pooled_lo[n // 4 % 2][:, n % 4, :], work[2 + n % 2][:],
                                      pooled_hi[n // 4 % 2][:, n % 4, :].bitcast(F32), ALU.subtract) \
                       .then_inc(pooled_lo_done, 1)
                elif kind == "pool":
                    s = first_piece[(kind, n)]
                    split_run(dve, "lo", s, s // 2, 2)
                elif kind == "post_rstd":
                    coefs(1, 2, 12)
                    rstd_of(POST[0])
                    dve.wait_ge(coef_ready, 2)
                elif kind == "update":
                    scale_tile(POST[0], n, pool_y, (shifted, 16) if n < 2 else (updated, n - 1))
                elif kind == "flush":
                    row_copy(ADA_EARLY - 1, first_piece[("half", HALVES - 1)] + 4, 4 + (ADA_EARLY - 1) % 2)
                    bias_add(ADA_EARLY - 1)

            coefs(2, 4, 20)
            split_run(dve, "lo", S_FFN0, U_FFN0, 4)
            rstd_of(PRE[1])
            dve.wait_ge(coef_ready, 3)
            dve.wait_ge(updated, 16)
            modulate(PRE[1], h_hi, h_lo, resid)

            def product_tile(layer, j, par, tokens):
                dve.wait_ge(gate_on[layer], j + 1)
                if not (isinstance(j, int) and j < 2):
                    dve.wait_ge(g_lo_done[layer], j - 1)
                dve.tensor_tensor(work[2 + par][:, 0:tokens], work[par][:, 0:tokens],
                                  banks[2 * par + 1][:, 0:tokens], ALU.mult).then_inc(product[layer], 1)

            def product_lo(layer, j, slot, tokens):
                dve.wait_ge(g_hi_done[layer], j + 1)
                dve.tensor_tensor(g_lo[:, slot, 0:tokens], work[2 + slot % 2][:, 0:tokens],
                                  g_hi[:, slot, 0:tokens].bitcast(F32), ALU.subtract).then_inc(g_lo_done[layer], 1)

            def mac_tile(n, par, t, u0):
                k = n % 4
                if k == 0:
                    dve.wait_ge(raw_landed[u0 % RAW], 16 * (u0 // RAW + 1) + t * 80)
                if n == 0:
                    dve.wait_ge(cols_done, ADA_EARLY + par + t * 2)
                else:
                    dve.wait_ge(mac_done, 32 * par + 2 * n + t * 64)
                for v in range(2):
                    w = raw[u0 % RAW][:, k * 512:(k + 1) * 512]
                    c = csilu[:, n, v:v + 1]
                    if n == 0:
                        dve.tensor_scalar(ada_acc[:, v, :], w, c, None, ALU.mult).then_inc(mac_done, 1)
                    else:
                        dve.scalar_tensor_tensor(ada_acc[:, v, :], w, c, ada_acc[:, v, :], ALU.mult, ALU.add) \
                           .then_inc(mac_done, 1)

            def ffn_steps(layer, s_base, tokens, y):
                u_base, u_step, split_off, mac_off = STEPS[layer]
                for i in range(4, 12):
                    if i == 7:
                        product_tile(layer, 0, 0, tokens)
                    if i == 11:
                        product_tile(layer, 1, 1, tokens)
                    split_piece(dve, "lo", (s_base + i, 0, 0), (u_base - 6 + i // 2, 0, 0))
                    if i == 7:
                        product_lo(layer, 0, 0, tokens)
                    if i == 11:
                        product_lo(layer, 1, 1, tokens)

                def add_down(dt, q, parts, t):
                    if dt % 4 == 3:
                        dve.wait_ge(piece_used, q + dt // 4 + 1 + t * 24)
                    else:
                        dve.wait_ge(down_part[layer], parts + 3 * (dt // 4) + dt % 4 + 1 + t * 24)
                    dve.tensor_tensor(y[:, dt, :], y[:, dt, :], banks[4 + dt % 3][:, 0:tokens], ALU.add) \
                       .then_inc(y_added[layer], 1)

                def step(par, t):
                    q = s_base + 12 + 12 * par
                    ub = u_base + u_step * par
                    for i in range(12):
                        side_tile = {3: 0, 7: 1}.get(i)
                        j = 2 * par + 2 + (side_tile or 0)
                        if side_tile is not None:
                            product_tile(layer, j + t * 4, side_tile, tokens)
                        if i >= 8:
                            for dt in range(0 if i == 8 else 4 * i - 30, min(4 * i - 26, DT)):
                                add_down(dt, q + 4, 12 * par, t)
                        if mac_off and i % 2 == 0 and i < 8:
                            for k in range(4):
                                mac_tile(2 * i + k, par, t, ub + mac_off[i // 2])
                        split_piece(dve, "lo", (q + i, 24, t), (ub + split_off[i // 2], 2 * u_step, t))
                        if side_tile is not None:
                            product_lo(layer, j + t * 4, 2 * ((par + 1) % 2) + side_tile, tokens)
                        if mac_off and i == 11:
                            bias_add(ADA_EARLY + par + t * 2)

                dve.wait_ge(cleared, layer + 1)
                with dve.Fori(0, CHUNKS // 2 - 1, 1) as t:
                    step(0, t)
                    step(1, t)
                step(0, CHUNKS // 2 - 1)
                for dt in range(DT):
                    add_down(dt, s_base + 12 * (CHUNKS - 1) + 8, 12 * (CHUNKS - 1), 0)

            ffn_steps(0, S_FFN0, TOK, resid)

            coefs(3, 5, ADA_CHUNKS)
            coefs(4, 7, ADA_CHUNKS + 8)
            coefs(5, 8, ADA_CHUNKS + 12)
            rstd_of(POST[1])
            dve.wait_ge(coef_ready, 6)
            dve.wait_ge(reloaded, 16)
            for dt in range(DT):
                scale_tile(POST[1], dt, resid, None if dt < 2 else (updated, 16 + dt - 1))
            rstd_of(PRE[2])
            dve.wait_ge(updated, 32)
            modulate(PRE[2], h_hi, h_lo, resid, S_QKV, U_QKV)

            def gap_rows(n, units, chunks, bank):
                dve.wait_ge(gap_used, units)
                dve.wait_ge(cols_done, chunks)
                for i in range(n):
                    dve.tensor_copy(ada_rows[0:2, i, :], banks[bank + i][0:2, :]).then_inc(rows_copied, 1)

            gap_rows(ADA_GAP1, 4 * ADA_GAP1, ADA_EARLY + ADA_BESIDE, 0)

            cos, sin = rope_sb[:, 0, :], rope_sb[:, 1, :]
            split_run(dve, "lo", S_QKV + 4, U_QKV + 2, 4)
            bias_add(ADA_EARLY + ADA_BESIDE, ADA_GAP1)
            coefs(6, 10, ADA_CHUNKS + 20)
            for m in range(2):
                lat = k32[:, m, LAT]
                dve.wait_ge(k_turned, m + 1)
                dve.tensor_tensor(work[2 + m][:, LAT], banks[6 + m][:, LAT], sin, ALU.mult)
                dve.tensor_tensor(lat, lat, cos, ALU.mult).then_inc(k_rope, 1)
                dve.wait_ge(k_rope, m + 1)
                dve.tensor_tensor(lat, lat, work[2 + m][:, LAT], ALU.add).then_inc(k_ready, 1)
            split_run(dve, "lo", S_QKV + 8, U_QKV + 4, 4)

            def q_finish(j, i):
                dve.wait_ge(q_turned, j + 1)
                if isinstance(j, int) and j < 2:
                    dve.wait_ge(k_ready, 2)
                else:
                    dve.wait_ge(q_ready, j - 1)
                dst = side[:, bass.ds(j, 1), :].rearrange("p a b -> p (a b)")
                dve.tensor_tensor(work[2 + i % 2][:, LAT], banks[2 + i % 2][:, LAT], sin, ALU.mult)
                dve.tensor_tensor(dst, work[i % 2][:, LAT], cos, ALU.mult).then_inc(q_rope, 1)
                dve.wait_ge(q_rope, j + 1)
                dve.tensor_tensor(dst, dst, work[2 + i % 2][:, LAT], ALU.add).then_inc(q_ready, 1)

            def q_quad(t):
                for i in range(4):
                    if i or not is_first(t):
                        q_finish(t * 4 + i - 1, i + 3)
                    for half in range(2):
                        split_piece(dve, "lo", (S_QKV + 12 + 2 * i + half, 8, t), (U_QKV + 6 + i, 4, t))

            repeat(dve, Q_TILES // 4, q_quad)
            q_finish(Q_TILES - 1, 3)

            def key_rest(m):
                dve.wait_ge(key_hi_done, m + 1)
                for b in range(2):
                    own = slice(64 * b, 64 * b + 64)
                    dve.tensor_tensor(key_lo[own, b, :], k32[own, m, :], key_hi[own, b, :].bitcast(F32),
                                      ALU.subtract).then_inc(key_lo_done, 1)
                dve.wait_ge(key_lo_done, 4 * m + 2)
                for b in range(2):
                    own, other = slice(64 * b, 64 * b + 64), slice(64 * (1 - b), 64 * (1 - b) + 64)
                    dve.tensor_copy(key_lo[other, b, :], key_lo[own, b, :].bitcast(F32)) \
                       .then_inc(key_lo_done, 1)

            def val_rest(m):
                dve.wait_ge(val_hi_done, m + 1)
                dve.tensor_tensor(val_lo[:], v32[:, :, m * P:(m + 1) * P], val_hi[:].bitcast(F32),
                                  ALU.subtract).then_inc(val_lo_done, 1)

            def q_rest(n):
                pair, qt = n // 2, n % 2
                dve.wait_ge(qs_hi, n + 1)
                dve.tensor_tensor(q_lo[n % 2][:], side[:, 2 * pair:2 * pair + 2, qt * P:(qt + 1) * P],
                                  q_hi[n % 2][:].bitcast(F32), ALU.subtract).then_inc(qs_lo, 1)

            def head_max(n):
                pair, qt = n // 2, n % 2
                p = n % 2
                for i in range(4):
                    dve.wait_ge(scores, 4 * n + i + 1)
                    if n >= 2 and i == 0:
                        dve.wait_ge(turned, 4 * (n - 1))
                    dve.tensor_tensor_reduce(probs[p][:, i, :], banks[i][:], mask_sb[:, qt, :], 1.0, 2 * MASKED,
                                             ALU.add, ALU.max, row_max[p][:, i:i + 1]).then_inc(masked, 1)
                own_sinks = sinks_sb[:, 4 * pair:4 * pair + 4]
                dve.wait_ge(masked, 4 * n + 4)
                dve.scalar_tensor_tensor(top[p][:], row_max[p][:], Q_SCALE, own_sinks, ALU.mult, ALU.max) \
                   .then_inc(small_step, 1)
                dve.wait_ge(small_step, 3 * n + 1)
                dve.tensor_scalar(neg_top[p][:], top[p][:], -1.0, None, ALU.mult)
                dve.tensor_tensor(sink_gap[p][:], own_sinks, top[p][:], ALU.subtract).then_inc(sink_step, 1)

            def normalisers(n):
                p = n % 2
                dve.wait_ge(weighed, 4 * n + 4)
                dve.tensor_tensor(denom[p][:], row_sum[p][:], sink_exp[p][:], ALU.add).then_inc(small_step, 1)
                dve.wait_ge(small_step, 3 * n + 2)
                dve.reciprocal(inv_denom[p][:], denom[p][:]).then_inc(small_step, 1)
                dve.wait_ge(small_step, 3 * n + 3)
                for i in range(4):
                    dve.tensor_scalar(diag[p][:, i * P:(i + 1) * P], ident[:], inv_denom[p][:, i:i + 1], None,
                                      ALU.mult).then_inc(diag_ready, 1)

            key_rest(0)
            q_rest(0)
            q_rest(1)
            dve.wait_ge(q_ready, Q_TILES)
            head_max(0)
            val_rest(0)
            normalisers(0)
            for n in range(16):
                if n < 15:
                    head_max(n + 1)
                if n == 8:
                    val_rest(1)
                for i in range(4):
                    dve.wait_ge(pt_hi_done, 4 * n + i + 1)
                    dve.tensor_tensor(pt_lo[:, :, i, :], banks[4 + i % 2][:].rearrange("p (k q) -> p k q", k=4),
                                      pt_hi[:, :, i, :].bitcast(F32), ALU.subtract).then_inc(pt_lo_done, 1)
                if n < 15:
                    normalisers(n + 1)
                if n == 6:
                    key_rest(1)
                if n < 14:
                    q_rest(n + 2)
                dve.wait_ge(attended, n + 1)
                rows = slice(64 * (n // 4 % 2), 64 * (n // 4 % 2) + 64)
                got = banks[6 + n % 2][:].rearrange("p (a b q) -> p a b q", a=2, b=2)
                for b in range(2):
                    last = dve.tensor_copy(work[1][64 * b:64 * b + 64, 0:SEQ].rearrange("p (a q) -> p a q", a=2),
                                           got[rows, :, b, :])
                last.then_inc(o_copied, 1)
                dve.wait_ge(o_hi_done, n + 1)
                where = (slice(None), slice(2 * (n // 2), 2 * (n // 2) + 2), slice((n % 2) * P, (n % 2 + 1) * P))
                dve.tensor_tensor(o_lo[where], work[1][:, 0:SEQ].rearrange("p (a q) -> p a q", a=2),
                                  o_hi[where].bitcast(F32), ALU.subtract).then_inc(o_lo_done, 1)

            with dve.Fori(0, DT // 4 - 1, 1) as t:
                for i in range(8):
                    split_piece(dve, "lo", (S_OUT + 4 + i, 8, t), (U_OUT + 2 + i // 2, 4, t))
            split_run(dve, "lo", S_FFN1 - 4, U_GAP2 - 2, 4)
            rstd_of(POST[2])
            dve.wait_ge(proj_copied, 16)
            for dt in range(DT):
                scale_tile(POST[2], dt, side, None if dt < 2 else (updated, 32 + dt - 1))
            rstd_of(PRE[3])
            dve.wait_ge(coef_ready, 7)
            dve.wait_ge(updated, 48)
            modulate(PRE[3], h1_hi, h1_lo, resid, S_FFN1, U_FFN1)
            gap_rows(ADA_GAP2, 4 * (ADA_GAP1 + ADA_GAP2), 2 * ADA_CHUNKS - ADA_GAP2, 4)
            bias_add(2 * ADA_CHUNKS - ADA_GAP2, ADA_GAP2)
            coefs(7, 11, 2 * ADA_CHUNKS)
            ffn_steps(1, S_FFN1, SEQ, side)
            rstd_of(POST[3])
            dve.wait_ge(coef_ready, 8)
            for dt in range(DT):
                scale_tile(POST[3], dt, side, None if dt < 2 else (updated, 48 + dt - 1))

        @block.gpsimd
        def _(pool):
            for i in range(2):
                last = pool.memset(padded[i][:], 0.0)
            last.then_inc(padding_set, 1)
            pool.wait_ge(padding_set, 1)
            pool.wait_ge(counts_landed, 16)

            steps = [0]

            def step(ins):
                ins.then_inc(window_step, 1)
                steps[0] += 1
                pool.wait_ge(window_step, steps[0])

            def mix(dt):
                w = WINDOWS[dt // 4]
                pool.wait_ge(shifted, dt + 1)
                if dt:
                    pool.wait_ge(diffed, dt)
                src, n = padded[dt % 2], SEQ + 2 * PAD
                span = 1
                while span < w:
                    dst = window[0] if src is not window[0] else window[1]
                    n -= span
                    step(pool.tensor_tensor(dst[:, :, 0:n], src[:, :, 0:n], src[:, :, span:span + n], ALU.add))
                    src, span = dst, 2 * span
                other = window[0] if src is not window[0] else window[1]
                for v in range(2):
                    last = pool.tensor_tensor(other[:, v, 0:SEQ], src[:, v, PAD - w // 2:PAD - w // 2 + SEQ],
                                              counts[:, dt // 4, :], ALU.mult)
                step(last)
                if dt >= 2:
                    pool.wait_ge(pooled_lo_done, dt - 1)
                pool.tensor_tensor(work[2 + dt % 2][:].rearrange("p (v t) -> p v t", v=2), other[:, :, 0:SEQ],
                                   padded[dt % 2][:, :, PAD:PAD + SEQ], ALU.subtract).then_inc(diffed, 1)

            for dt in range(DT):
                mix(dt)

            def update(first, tokens, old):
                for dt in range(DT):
                    pool.wait_ge(scaled, first + dt + 1)
                    pool.tensor_tensor(resid[:, dt, 0:tokens], work[dt % 2][:, 0:tokens], old[:, dt, 0:tokens],
                                       ALU.add).then_inc(updated, 1)

            update(SC_U1, TOK, resid)
            pool.wait_ge(spilled, 16)
            pool.wait_ge(mod_lo, 16)
            pool.memset(resid[:], 0.0).then_inc(cleared, 1)
            pool.wait_ge(reloaded, 16)
            update(SC_U2, TOK, saved)
            update(SC_U3, SEQ, resid)
            pool.memset(side, 0.0).then_inc(cleared, 1)
            update(SC_U4, SEQ, resid)

        @block.tensor
        def _(pe):
            def piece_ready(s0, s_step=0, t=0):
                pe.wait_ge(lo_done, s0 + 1 + t * s_step)

            def three_passes(dst, wh, wl, xh, xl, start, stop):
                pe.matmul(dst, wh, xh, start=start, stop=False)
                pe.matmul(dst, wh, xl, start=False, stop=False)
                return pe.matmul(dst, wl, xh, start=False, stop=stop)

            def product_piece(dst, s0, xh, xl, tokens, k0, before=None, s_step=0, t=0):
                piece_ready(s0, s_step, t)
                slot = s0 % RING
                for i in range(8):
                    k = k0 + i
                    if before is not None:
                        before(k)
                    cols = slice(i * P, (i + 1) * P)
                    last = three_passes(dst, w_hi[slot][:, cols], w_lo[slot][:, cols], xh[:, k, 0:tokens],
                                        xl[:, k, 0:tokens], k == 0, k == DT - 1)
                last.then_inc(piece_used, 1)

            def add_squares(n, bank, tokens):
                pe.wait_ge(squared, n + 1)
                pe.matmul(banks[bank][:, 0:tokens], ones[:], squares[:, n % 2, 0:tokens],
                          start=(n % DT == 0), stop=(n % DT == DT - 1)).then_inc(summed, 1)

            def ada_piece(s0, q, bank, s_step=0, t=0):
                piece_ready(s0, s_step, t)
                slot = s0 % RING
                for i in range(2):
                    k = 2 * q + i
                    parts = cparts[:, k].rearrange("p v h -> p (v h)")
                    for n, w in enumerate((w_hi, w_lo)):
                        last = pe.matmul(banks[bank][0:4, :], parts, w[slot][:, i * 512:(i + 1) * 512],
                                         start=(k == 0 and n == 0), stop=(k == DT - 1 and n == 1))
                last.then_inc(piece_used, 1)

            def turn(row_tile, rows, columns, n=0):
                for i in range(4):
                    last = pe.matmul(banks[7][:, 8 * n + 2 * i:8 * n + 2 * i + 2],
                                     ada_rows[0:rows, row_tile, i * P:(i + 1) * P], columns, start=True, stop=True)
                return last

            def turn_rows(j, row_tile):
                pe.wait_ge(rows_copied, j + 1)
                if not is_first(j):
                    pe.wait_ge(ada_added, j)
                turn(row_tile, 4, pairs_sb[:]).then_inc(cols_done, 1)

            def ada_chunk(j, s0, bank, turned_chunk, s_step=0, t=0):
                if not (isinstance(j, int) and j < 2):
                    pe.wait_ge(rows_copied, j - 1)
                for q in range(8):
                    ada_piece(s0 + q, q, bank, s_step, t)
                    if s_step and q % 4 == 3:
                        i = 2 * (bank % 2) + q // 4
                        pe.wait_ge(squared, t * 4 + i - 1)
                        pe.matmul(banks[6][:], ones[:], squares[:, i % 2, :], start=False, stop=False,
                                  skip_group_check=True).then_inc(summed, 1)
                    if q == 3 and turned_chunk is not None:
                        turn_rows(turned_chunk, (bank + 1) % 2)

            pe.wait_ge(csilu_ready, 2)
            pe.wait_ge(consts_set, 1)
            pe.wait_ge(consts_landed, 16 * 9)
            ada_chunk(0, 0, 4, None)
            ada_chunk(1, 8, 5, 0)
            for dt in range(2):
                add_squares(SQ_X0 + dt, 6, TOK)
            with pe.Fori(1, 4, 1) as t:
                for k in range(2):
                    ada_chunk(t * 2 + k, 8 * k, 4 + k, t * 2 + k - 1, 16, t)
            for dt in range(DT - 2, DT):
                add_squares(SQ_X0 + dt, 6, TOK)
            turn_rows(7, 1)
            for kind, n in early:
                if kind == "piece":
                    h, i = divmod(n, 4)
                    j = 8 + h // 2
                    if h % 2 == 0 and i == 0:
                        pe.wait_ge(rows_copied, j - 1)
                    ada_piece(first_piece[("half", h)] + i, 4 * (h % 2) + i, 4 + j % 2)
                    if h % 2 == 1 and h >= 3 and i == 0:
                        turn_rows(j - 1, (j - 1) % 2)
                elif kind == "flush":
                    turn_rows(ADA_EARLY - 1, (ADA_EARLY - 1) % 2)
                elif kind == "pool":
                    pe.wait_ge(pooled_lo_done, 4 * n + 4)
                    if n:
                        pe.wait_ge(squared, SQ_Y0 + 4 * n)
                    for q in range(2):
                        s0 = first_piece[(kind, n)] + q
                        piece_ready(s0)
                        for i in range(2):
                            for k in range(4):
                                cols = slice((4 * i + k) * P, (4 * i + k + 1) * P)
                                last = three_passes(banks[2 * q + i][:], w_hi[s0 % RING][:, cols],
                                                    w_lo[s0 % RING][:, cols], pooled_hi[n % 2][:, k, :],
                                                    pooled_lo[n % 2][:, k, :], k == 0, k == 3)
                        last.then_inc(piece_used, 1)
                elif kind == "evacuate":
                    add_squares(SQ_Y0 + n, 6, TOK)
                elif kind == "square":
                    add_squares(SQ_X1 + n, 6, TOK)

            def ffn(layer, s_base, tokens, xh, xl, mod0, sq_first, after_first_tile=None):
                def gate_up(s0, j0, first, s_step=0, t=0):
                    for i in range(2):
                        if not first:
                            pe.wait_ge(product[layer], j0 + i - 1)
                        for n in range(2):
                            for half in range(2):
                                wait_x = None
                                if first and i == 0 and n == 0:
                                    wait_x = lambda k: pe.wait_ge(mod_lo, mod0 + k + 1)
                                product_piece(banks[2 * i + n][:, 0:tokens], s0 + 4 * i + 2 * n + half, xh, xl,
                                              tokens, 8 * half, wait_x, s_step, t)
                        if first and i == 0 and after_first_tile is not None:
                            after_first_tile()

                def down(s0, c0, slots, first, sq=None, s_step=0, t=0):
                    pe.wait_ge(g_lo_done[layer], 2 * c0 + 2 + t * 4)
                    for q in range(4):
                        piece_ready(s0 + q, s_step, t)
                        slot = (s0 + q) % RING
                        for i in range(4):
                            dt = 4 * q + i
                            if dt >= 3 or not first:
                                pe.wait_ge(y_added[layer], 16 * c0 + max(dt - 2, 0) + t * 32)
                            for k in range(2):
                                cols = slice((2 * i + k) * P, (2 * i + k + 1) * P)
                                last = three_passes(banks[4 + dt % 3][:, 0:tokens], w_hi[slot][:, cols],
                                                    w_lo[slot][:, cols], g_hi[:, slots + k, 0:tokens],
                                                    g_lo[:, slots + k, 0:tokens], k == 0, k == 1)
                            last.then_inc(piece_used if i == 3 else down_part[layer], 1)
                            if sq is not None and dt >= 2:
                                add_squares(sq + dt - 2, 7, tokens)
                    if sq is not None:
                        add_squares(sq + DT - 2, 7, tokens)
                        add_squares(sq + DT - 1, 7, tokens)

                def turn_beside(par, t):
                    pe.wait_ge(mac_done, 32 * (par + 1) + t * 64)
                    pe.wait_ge(ada_added, ADA_EARLY + par + t * 2)
                    for i in range(4):
                        for v in range(2):
                            last = pe.matmul(banks[7][:, 2 * i + v:2 * i + v + 1],
                                             ada_acc[:, v, i * P:(i + 1) * P], ones[:, 0:1], start=True, stop=True)
                    last.then_inc(cols_done, 1)

                def step(par, t):
                    gate_up(s_base + 8 + 12 * par, t * 4 + 2 * par + 2, False, 24, t)
                    down(s_base + 16 + 12 * par, par, 2 * par, par == 0 and is_first(t), None, 24, t)
                    if layer == 0:
                        turn_beside(par, t)

                gate_up(s_base, 0, True)

                def two_steps(t):
                    step(0, t)
                    step(1, t)

                repeat(pe, CHUNKS // 2 - 1, two_steps)
                step(0, CHUNKS // 2 - 1)
                if layer == 0:
                    pe.wait_ge(ada_added, ADA_EARLY + ADA_BESIDE)
                down(s_base + 12 * (CHUNKS - 1) + 8, CHUNKS - 1, 2, False, sq_first)

            ffn(0, S_FFN0, TOK, h_hi, h_lo, 0, SQ_Y2)

            def gap_chunks(u0, n, bank, sq_at):
                for i in range(n):
                    for k in range(DT):
                        u = u0 + 4 * i + k // 4
                        if k % 4 == 0:
                            pe.wait_ge(raw_landed[u % RAW], 16 * (u // RAW + 1))
                        last = pe.matmul(banks[bank + i][0:2, :], csilu[:, k, :],
                                         raw[u % RAW][:, (k % 4) * 512:(k % 4 + 1) * 512],
                                         start=(k == 0), stop=(k == DT - 1))
                        if k % 4 == 3:
                            last.then_inc(gap_used, 1)
                        if DT * i + k in sq_at:
                            add_squares(*sq_at[DT * i + k])

            def turn_gap(n, units_before):
                pe.wait_ge(rows_copied, units_before + n)
                for i in range(n):
                    last = turn(i, 2, ident[0:2, 0:2], i)
                last.then_inc(cols_done, n)

            pe.wait_ge(product[0], FT)
            gap_chunks(U_GAP1, ADA_GAP1, 0, {9 + i: (SQ_X2 + i, 6, TOK) for i in range(DT)})

            def key_tile(m):
                for half in range(2):
                    product_piece(banks[4 + m][:], S_QKV + 2 * m + half, h_hi, h_lo, TOK, 8 * half,
                                  (lambda k: pe.wait_ge(mod_lo, 16 + k + 1)) if m == 0 else None)

            def turn_key(m):
                pe.wait_ge(k_copied, m + 1)
                if m == 1:
                    pe.wait_ge(ada_added, ADA_EARLY + ADA_BESIDE + ADA_GAP1)
                pe.matmul(banks[6 + m][:, LAT], rot_sb[:], k32[:, m, LAT], start=True, stop=True) \
                  .then_inc(k_turned, 1)

            key_tile(0)
            turn_gap(ADA_GAP1, ADA_EARLY)
            key_tile(1)
            turn_key(0)
            for q in range(4):
                s0 = S_QKV + 4 + q
                piece_ready(s0)
                for i in range(4):
                    k = 4 * q + i
                    cols = slice(i * KV, (i + 1) * KV)
                    for tt in range(4):
                        ts = slice(tt * P, (tt + 1) * P)
                        last = three_passes(banks[tt][:, 0:KV], h_hi[:, k, ts], h_lo[:, k, ts],
                                            w_hi[s0 % RING][:, cols], w_lo[s0 % RING][:, cols],
                                            k == 0, k == DT - 1)
                last.then_inc(piece_used, 1)
            turn_key(1)
            pe.wait_ge(v_copied, 4)

            def turn_query(j, i):
                pe.wait_ge(q_copied, j + 1)
                pe.matmul(banks[2 + i % 2][:, LAT], rot_sb[:], work[i % 2][:, LAT], start=True, stop=True) \
                  .then_inc(q_turned, 1)

            def q_quad(t):
                for i in range(4):
                    if i >= 2 or not is_first(t):
                        pe.wait_ge(q_copied, t * 4 + i - 1)
                    for half in range(2):
                        product_piece(banks[i % 2][:, LAT], S_QKV + 8 + 2 * i + half, h_hi, h_lo, SEQ, 8 * half,
                                      None, 8, t)
                    if i or not is_first(t):
                        if i >= 3 or not is_first(t):
                            pe.wait_ge(q_ready, t * 4 + i - 2)
                        turn_query(t * 4 + i - 1, i + 3)

            repeat(pe, Q_TILES // 4, q_quad)
            pe.wait_ge(q_ready, Q_TILES - 2)
            turn_query(Q_TILES - 1, 3)

            def score_heads(n):
                b = n // 4 % 2
                pe.wait_ge(key_lo_done, 4 * (n // 8) + 4)
                pe.wait_ge(qs_lo, n + 1)
                for i in range(4):
                    if n:
                        pe.wait_ge(masked, 4 * (n - 1) + i + 1)
                    rows = slice(64 * (i % 2), 64 * (i % 2) + 64)
                    qh, ql = q_hi[n % 2][rows, i // 2, :], q_lo[n % 2][rows, i // 2, :]
                    kh, kl = key_hi[rows, b, :], key_lo[rows, b, :]
                    pe.matmul(banks[i][:], qh, kh, start=True, stop=False)
                    pe.matmul(banks[i][:], ql, kh, start=False, stop=False)
                    pe.matmul(banks[i][:], qh, kl, start=False, stop=True).then_inc(scores, 1)

            def turn_probs(n):
                for i in range(4):
                    pe.wait_ge(diag_ready, 4 * n + i + 1)
                    if 4 * n + i >= 2:
                        pe.wait_ge(pt_lo_done, 4 * n + i - 1)
                    for kt in range(4):
                        last = pe.matmul(banks[4 + i % 2][:, kt * P:(kt + 1) * P],
                                         probs[n % 2][:, i, kt * P:(kt + 1) * P], diag[n % 2][:, i * P:(i + 1) * P],
                                         start=True, stop=True)
                    last.then_inc(turned, 1)

            def attend(n):
                pe.wait_ge(val_lo_done, n // 8 + 1)
                pe.wait_ge(pt_lo_done, 4 * n + 4)
                if n >= 2:
                    pe.wait_ge(o_copied, n - 1)
                for kt in range(4):
                    last = three_passes(banks[6 + n % 2][:], val_hi[:, kt, :], val_lo[:, kt, :],
                                        pt_hi[:, kt].rearrange("p h q -> p (h q)"),
                                        pt_lo[:, kt].rearrange("p h q -> p (h q)"), kt == 0, kt == 3)
                last.then_inc(attended, 1)

            score_heads(0)
            for n in range(16):
                if n < 15:
                    score_heads(n + 1)
                turn_probs(n)
                attend(n)

            pe.wait_ge(o_lo_done, 16)

            def out_quad(t):
                for i in range(4):
                    if i >= 2 or not is_first(t):
                        pe.wait_ge(squared, t * 4 + SQ_Y3 + i - 1)
                    for half in range(2):
                        product_piece(banks[i % 2][:, LAT], S_OUT + 2 * i + half, o_hi, o_lo, SEQ, 8 * half,
                                      None, 8, t)
                    if i or not is_first(t):
                        add_proj(t * 4 + i - 1, i + 3, i == 1 and is_first(t))

            def add_proj(dt, i, start, stop=False):
                pe.wait_ge(squared, dt + (SQ_Y3 + 1))
                pe.matmul(banks[7][:, LAT], ones[:], squares[:, i % 2, LAT], start=start,
                          stop=stop, skip_group_check=True).then_inc(summed, 1)

            repeat(pe, DT // 4, out_quad)
            add_proj(DT - 1, 3, False, True)
            gap_chunks(U_GAP2, ADA_GAP2, 4, {8 + i: (SQ_X3 + i, 7, SEQ) for i in range(DT)})
            ffn(1, S_FFN1, SEQ, h1_hi, h1_lo, 32, SQ_Y4, lambda: turn_gap(ADA_GAP2, ADA_EARLY + ADA_GAP1))


def tiles_of(w):
    return w.reshape(w.shape[0] // P, P, w.shape[1] // P, P)


def weight_stream(np, w_ada, w_pool, w_qkv, w_o, w_gate_up, w_down):
    units = np.empty((UNITS, P, UNIT), np.float32)

    def ada_chunk(u, j):
        w = w_ada[j // ADA_CHUNKS][:, j % ADA_CHUNKS * 512:(j % ADA_CHUNKS + 1) * 512]
        units[u:u + 4] = w.reshape(4, 4, P, 512).transpose(0, 2, 1, 3).reshape(4, P, UNIT)

    def column_tile(u, w, j):
        units[u] = w[:, j * P:(j + 1) * P].reshape(DT, P, P).transpose(1, 0, 2).reshape(P, UNIT)

    def swiglu(layer):
        u, u_step, split_off, mac_off = STEPS[layer]
        gate_up, down = w_gate_up[layer], w_down[layer]

        def down_unit(at, c, h):
            w = down[c * 2 * P:(c + 1) * 2 * P, h * 1024:(h + 1) * 1024]
            units[at] = w.reshape(2, P, 8, P).transpose(1, 2, 0, 3).reshape(P, UNIT)

        for i, (j, up) in enumerate(((0, 0), (0, 1), (1, 0), (1, 1), (2, 0), (2, 1))):
            column_tile(u - 6 + i, gate_up, j + up * FT)
        for c in range(CHUNKS - 1):
            at = [u + c * u_step + off for off in split_off]
            column_tile(at[0], gate_up, 2 * c + 3)
            column_tile(at[1], gate_up, 2 * c + 3 + FT)
            down_unit(at[2], c, 0)
            down_unit(at[3], c, 1)
            if c < CHUNKS - 2:
                column_tile(at[4], gate_up, 2 * c + 4)
                column_tile(at[5], gate_up, 2 * c + 4 + FT)
            else:
                down_unit(at[4], c + 1, 0)
                down_unit(at[5], c + 1, 1)
            for n, off in enumerate(mac_off):
                j = ADA_EARLY + c
                w = w_ada[j // ADA_CHUNKS][n * 512:(n + 1) * 512, j % ADA_CHUNKS * 512:(j % ADA_CHUNKS + 1) * 512]
                units[u + c * u_step + off] = w.reshape(4, P, 512).transpose(1, 0, 2).reshape(P, UNIT)

    pieces = early_pieces()
    for j in range(8):
        ada_chunk(4 * j, j)
    for (kind, n), s in pieces.items():
        if kind == "half":
            j = 8 + n // 2
            w = w_ada[0][n % 2 * 1024:(n % 2 + 1) * 1024, j * 512:(j + 1) * 512]
            units[s // 2:s // 2 + 2] = w.reshape(2, 4, P, 512).transpose(0, 2, 1, 3).reshape(2, P, UNIT)
        else:
            units[s // 2] = w_pool[0, n].reshape(4, P, 4, P).transpose(1, 2, 0, 3).reshape(P, UNIT)
    swiglu(0)
    for i in range(ADA_GAP1):
        ada_chunk(U_GAP1 + 4 * i, ADA_EARLY + ADA_BESIDE + i)
    for m in range(2):
        column_tile(U_QKV + m, w_qkv[0], Q_TILES + m)
        w = w_qkv[0][m * 1024:(m + 1) * 1024, D + KV:]
        units[U_QKV + 2 + m] = w.reshape(8, P, KV).transpose(1, 0, 2).reshape(P, UNIT)
    for j in range(Q_TILES):
        column_tile(U_QKV + 4 + j, w_qkv[0], j)
    for j in range(DT):
        column_tile(U_OUT + j, w_o[0], j)
    for i in range(ADA_GAP2):
        ada_chunk(U_GAP2 + 4 * i, 2 * ADA_CHUNKS - ADA_GAP2 + i)
    swiglu(1)
    return units


def shape_tables(np):
    f = np.float32
    t = np.arange(SEQ)
    counts = np.stack([f(1) / (np.clip(t + w // 2, 0, SEQ) - np.clip(t - w // 2, 0, SEQ)).astype(f)
                       for w in WINDOWS])
    inv = f(1) / np.power(f(10000), np.arange(0, HEAD // 2, 2, dtype=f) / f(HEAD // 2))
    row, col = (t // 64).astype(f)[:, None] * inv, (t % 64).astype(f)[:, None] * inv
    angle = np.concatenate([row, row, col, col], axis=-1).T.astype(f)
    rope = np.stack([np.tile(np.cos(angle), (2, 1)), np.tile(np.sin(angle), (2, 1))], axis=1).astype(f)
    rotation = np.zeros((P, P), f)
    for m in range(P):
        half = m % (HEAD // 2) < HEAD // 4
        rotation[m + HEAD // 4 if half else m - HEAD // 4, m] = -1 if half else 1
    mask = np.zeros((P, 2, TOK), f)
    for qt in range(2):
        q = qt * P + np.arange(P)
        mask[:, qt, :SEQ] = np.where(np.abs(q[:, None] - t[None, :]) <= 128, 0, MASKED)
    pairs = np.array([[1, 0], [1, 0], [0, 1], [0, 1]], f)
    return (np.ascontiguousarray(np.broadcast_to(counts, (P, 4, SEQ))), np.ascontiguousarray(rope), rotation,
            np.eye(P, dtype=f), pairs, mask)


def kernel(x, c, ctx, c_ctx, w_ada, b_ada, norm_pre_mix, norm_post_mix, norm_pre_ffn, norm_post_ffn,
           w_pool, pool_scale, w_qkv, w_o, attn_sinks, w_gate_up, w_down):
    import numpy as np
    import concourse.bacc as bacc
    from concourse.bass_utils import run_bass_kernel_spmd

    def feature_major(a):
        return np.asarray(a).reshape(-1, DT, P).transpose(2, 1, 0)

    def twice(a):
        return np.repeat(a[..., None], 2, axis=-1)

    gains = np.stack([np.asarray(g)[layer] for layer in range(2)
                      for g in (norm_pre_mix, norm_post_mix, norm_pre_ffn, norm_post_ffn)])
    counts, rope, rotation, identity, pairs, mask = shape_tables(np)
    arrays = {
        "stream": weight_stream(np, *(np.asarray(a) for a in (w_ada, w_pool, w_qkv, w_o, w_gate_up, w_down))),
        "x_in": np.concatenate([feature_major(x), feature_major(ctx)], axis=2),
        "cond": np.concatenate([feature_major(c), feature_major(c_ctx)], axis=2),
        "ada_bias": twice(np.asarray(b_ada).reshape(12 * DT, P).T),
        "gains": twice(gains.reshape(8, DT, P).transpose(2, 0, 1)),
        "pool_gain": np.asarray(pool_scale)[0].reshape(DT, P).T,
        "inv_counts": counts, "rope": rope, "rotation": rotation, "identity": identity, "pairs": pairs,
        "mask": mask, "sinks": np.broadcast_to(np.asarray(attn_sinks)[0], (P, N_HEADS)),
    }
    arrays = {name: np.ascontiguousarray(a) for name, a in arrays.items()}
    nc = bacc.Bacc("TRN2", target_bir_lowering=False, num_devices=1)
    args = [nc.dram_tensor(name, a.shape, F32, kind="ExternalInput").ap() for name, a in arrays.items()]
    out = nc.dram_tensor("out", (P, DT, SEQ), F32, kind="ExternalOutput").ap()
    build_trunk(nc, *args, out)
    got = run_bass_kernel_spmd(nc, [arrays], core_ids=[0]).results[0]["out"]
    return got.transpose(2, 1, 0).reshape(1, SEQ, D)
```

```python
from contextlib import ExitStack

import concourse.bass as bass
from concourse import mybir

F32 = mybir.dt.float32
F32R = mybir.dt.float32r
ALU = mybir.AluOpType
ACT = mybir.ActivationFunctionType

P = 128
D = 2048
DT = D // P
SEQ = 256
TOK = 2 * SEQ
D_FF = 5632
FT = D_FF // P
CHUNKS = FT // 2
HEAD = 64
N_HEADS = D // HEAD
N_KV = N_HEADS // 8
KV = N_KV * HEAD
WINDOWS = (2, 4, 8, 16)
PAD = max(WINDOWS) // 2
EPS = 1e-6
Q_SCALE = HEAD ** -0.5
MASKED = -1e30

UNIT = 2048
PIECE = UNIT // 2
RAW = 4
RING = 4
ADA_CHUNKS = 6 * D // 512
ADA_EARLY = 20
ADA_BESIDE = CHUNKS - 1
ADA_GAP1 = 4
ADA_GAP2 = 3
assert ADA_EARLY + ADA_BESIDE + ADA_GAP1 + ADA_GAP2 == 2 * ADA_CHUNKS
Q_TILES = D // P
STEPS_ATT = N_HEADS // 4 * (SEQ // P)
U_FFN0 = 4 * ADA_EARLY + 4
U_GAP1 = U_FFN0 + 3 * FT + 4 * ADA_BESIDE
U_QKV = U_GAP1 + 4 * ADA_GAP1
U_OUT = U_QKV + 4 + Q_TILES
U_GAP2 = U_OUT + DT
U_FFN1 = U_GAP2 + 4 * ADA_GAP2
UNITS = U_FFN1 + 3 * FT
S_FFN0 = 2 * U_FFN0
S_QKV = S_FFN0 + 6 * FT
S_OUT = S_QKV + 2 * (4 + Q_TILES)
S_FFN1 = S_OUT + 2 * DT


SPLIT_BEHIND = (11, 12)
STEPS = ((U_FFN0 + 6, 10, (1, 3, 5, 7, 8, 9), (0, 2, 4, 6)), (U_FFN1 + 6, 6, (0, 1, 2, 3, 4, 5), ()))


HALVES = 24


def on_vector(dt):
    return dt % 3 == 2


def early_order():
    order = []
    for h in range(HALVES):
        if h < DT:
            order.append(("scale", h))
        for i in range(4):
            order.append(("piece", 4 * h + i))
            if i == 1 and h < DT:
                order.append(("shift", h))
            if i == 2 and 1 <= h <= DT:
                order.append(("split", h - 1))
            if h % 4 == 2 and 6 <= h <= DT + 2:
                order.append(("evacuate", h - 6 + i))
            tile = 4 * (h - DT - 3) + i - 1
            if tile == -1:
                order.append(("post_rstd", 0))
            if 2 <= tile < DT + 2:
                order.append(("square", tile - 2))
            if 0 <= tile < DT:
                order.append(("update", tile))
        if h % 4 <= 1 and 4 <= h <= DT + 1:
            order.append(("pool", 2 * (h // 4 - 1) + h % 4))
    return order + [("next", 0), ("next", 1), ("pre_rstd", 0), ("flush", 0), ("next", 2), ("next", 3)]


def early_pieces():
    at = {}
    s = 64
    for item in early_order():
        if item[0] in ("piece", "pool"):
            at[item] = s
            s += 1
    assert s == S_FFN0
    at.update({("next", i): s + i for i in range(4)})
    return at


def build_trunk(nc, stream, x_in, cond, ada_bias, gains, pool_gain, inv_counts, rope, rotation, identity,
                pairs, mask, sinks, out):
    ctx = ExitStack()
    with ctx:
        base = 16512
        RESID, HB, GB, RAWB = 0, 32768, 98304, 114688
        SPLITB, EXTRA = RAWB + RAW * UNIT * 4, RAWB + RAW * UNIT * 4 + 2 * RING * PIECE * 4
        extra = [EXTRA]

        def at(name, shape, offset, dt=F32):
            return nc.alloc_sbuf_tensor_at(name, shape, dt, offset=base + offset)

        def small(name, shape, dt=F32):
            size = 4
            for n in shape[1:]:
                size *= n
            t = at(name, shape, extra[0], dt)
            extra[0] += -(-size // 32) * 32
            assert base + extra[0] <= 229368
            return t

        resid = at("resid", [P, DT, TOK], RESID)
        side = resid[:, :, SEQ:TOK]
        h_hi = at("h_hi", [P, DT, TOK], HB, F32R)
        h_lo = at("h_lo", [P, DT, TOK], HB + 32768, F32R)
        pooled_hi = [at(f"pooled_hi{i}", [P, 4, TOK], HB + 8192 * i, F32R) for i in range(2)]
        pooled_lo = [at(f"pooled_lo{i}", [P, 4, TOK], HB + 16384 + 8192 * i, F32R) for i in range(2)]
        pool_y = at("pool_y", [P, DT, TOK], HB + 32768)
        saved = at("saved", [P, DT, TOK], HB)
        o_hi = at("o_hi", [P, DT, SEQ], HB, F32R)
        o_lo = at("o_lo", [P, DT, SEQ], HB + 16384, F32R)
        key_hi = at("key_hi", [P, 2, TOK], HB + 32768, F32R)
        key_lo = at("key_lo", [P, 2, TOK], HB + 36864, F32R)
        val_hi = at("val_hi", [P, 4, P], HB + 40960, F32R)
        val_lo = at("val_lo", [P, 4, P], HB + 43008, F32R)
        q_hi = [at(f"q_hi{i}", [P, 2, P], HB + 45056 + 1024 * i, F32R) for i in range(2)]
        q_lo = [at(f"q_lo{i}", [P, 2, P], HB + 47104 + 1024 * i, F32R) for i in range(2)]
        probs0 = at("probs0", [P, 4, TOK], HB + 49152)
        pt_hi = at("pt_hi", [P, 4, 4, P], HB + 57344, F32R)
        h1_hi = at("h1_hi", [P, DT, SEQ], HB, F32R)
        h1_lo = at("h1_lo", [P, DT, SEQ], HB + 16384, F32R)
        counts = at("counts", [P, 4, SEQ], GB)
        padded = [at(f"padded{i}", [P, 2, SEQ + 2 * PAD], GB + 4096 + 2176 * i) for i in range(2)]
        window = [at(f"window{i}", [P, 2, SEQ + 2 * PAD], GB + 8448 + 2176 * i) for i in range(2)]
        g_hi = at("g_hi", [P, 4, TOK], GB, F32R)
        g_lo = at("g_lo", [P, 4, TOK], GB + 8192, F32R)
        k32 = at("k32", [P, 2, TOK], GB)
        v32 = at("v32", [P, 4, KV], GB + 4096)
        pt_lo = at("pt_lo", [P, 4, 4, P], GB + 8192, F32R)

        raw = [at(f"raw{i}", [P, UNIT], RAWB + i * UNIT * 4) for i in range(RAW)]
        w_hi = [at(f"w_hi{i}", [P, PIECE], SPLITB + i * PIECE * 4, F32R) for i in range(RING)]
        w_lo = [at(f"w_lo{i}", [P, PIECE], SPLITB + (RING + i) * PIECE * 4, F32R) for i in range(RING)]

        work = [small(f"work{i}", [P, TOK]) for i in range(4)]
        rstd = small("rstd", [P, TOK])
        ada_rows = small("ada_rows", [P, 4, 512])
        ada_acc = ada_rows[:, 0:2, :]
        squares = ada_rows[:, 2:4, :]
        probs = [probs0, ada_rows]
        diag = [work[0], work[2]]
        square_sum = work[3]
        mask_sb = small("mask_sb", [P, 2, TOK])
        rope_sb = small("rope_sb", [P, 2, SEQ])
        rot_sb = small("rot_sb", [P, P])
        ident = small("ident", [P, P])
        ones = small("ones", [P, P])
        bias_sb = small("bias_sb", [P, 12 * DT, 2])
        ada = small("ada", [P, 12 * DT, 2])
        gains_sb = small("gains_sb", [P, 8, DT, 2])
        coef = small("coef", [P, 8, DT, 2])
        pool_gain_sb = small("pool_gain_sb", [P, DT])
        sinks_sb = small("sinks_sb", [P, N_HEADS])
        cond_sb = small("cond_sb", [P, DT, 2])
        csilu = small("csilu", [P, DT, 2])
        cparts = small("cparts", [P, DT, 2, 2], F32R)
        pairs_sb = small("pairs_sb", [4, 2])
        eps_sb = small("eps_sb", [P, 1])
        row_max, top, neg_top, sink_gap, sink_exp, row_sum, denom, inv_denom = (
            [small(f"{name}{i}", [P, 4]) for i in range(2)]
            for name in ("row_max", "top", "neg_top", "sink_gap", "sink_exp", "row_sum", "denom", "inv_denom"))

        banks = [ctx.enter_context(nc.psum_tensor(f"bank{i}", [P, 512], F32)) for i in range(8)]
        spill = nc.dram_tensor("spill", (P, DT * TOK), F32).ap()

        def sem(name):
            return ctx.enter_context(nc.semaphore(name))

        raw_landed = [sem(f"raw_landed{i}") for i in range(RAW)]
        x_landed = sem("x_landed")
        cond_landed = sem("cond_landed")
        consts_landed = sem("consts_landed")
        counts_landed = sem("counts_landed")
        consts_set = sem("consts_set")
        padding_set = sem("padding_set")
        hi_done = sem("hi_done")
        lo_done = sem("lo_done")
        piece_used = sem("piece_used")
        cond_ready = sem("cond_ready")
        csilu_ready = sem("csilu_ready")
        rows_copied = sem("rows_copied")
        cols_done = sem("cols_done")
        ada_added = sem("ada_added")
        mac_done = sem("mac_done")
        gap_used = sem("gap_used")
        coef_ready = sem("coef_ready")
        squared = sem("squared")
        summed = sem("summed")
        totalled = sem("totalled")
        std_ready = sem("std_ready")
        rstd_ready = sem("rstd_ready")
        scaled = sem("scaled")
        finished = sem("finished")
        updated = sem("updated")
        mod_full = sem("mod_full")
        mod_hi = sem("mod_hi")
        mod_lo = sem("mod_lo")
        shifted = sem("shifted")
        window_step = sem("window_step")
        diffed = sem("diffed")
        pooled_hi_done = sem("pooled_hi_done")
        pooled_lo_done = sem("pooled_lo_done")
        spilled = sem("spilled")
        reloaded = sem("reloaded")
        cleared = sem("cleared")
        gate_on = [sem("gate_on0"), sem("gate_on1")]
        product = [sem("product0"), sem("product1")]
        g_hi_done = [sem("g_hi_done0"), sem("g_hi_done1")]
        g_lo_done = [sem("g_lo_done0"), sem("g_lo_done1")]
        down_part = [sem("down_part0"), sem("down_part1")]
        y_added = [sem("y_added0"), sem("y_added1")]
        k_copied = sem("k_copied")
        k_turned = sem("k_turned")
        k_rope = sem("k_rope")
        k_ready = sem("k_ready")
        v_copied = sem("v_copied")
        q_copied = sem("q_copied")
        q_turned = sem("q_turned")
        q_rope = sem("q_rope")
        q_ready = sem("q_ready")
        key_hi_done = sem("key_hi_done")
        key_lo_done = sem("key_lo_done")
        val_hi_done = sem("val_hi_done")
        val_lo_done = sem("val_lo_done")
        qs_hi = sem("qs_hi")
        qs_lo = sem("qs_lo")
        scores = sem("scores")
        masked = sem("masked")
        top_ready = sem("top_ready")
        denom_step = sem("denom_step")
        sink_step = sem("sink_step")
        weighed = sem("weighed")
        diag_ready = sem("diag_ready")
        turned = sem("turned")
        pt_hi_done = sem("pt_hi_done")
        pt_lo_done = sem("pt_lo_done")
        attended = sem("attended")
        o_copied = sem("o_copied")
        o_hi_done = sem("o_hi_done")
        o_lo_done = sem("o_lo_done")
        proj_copied = sem("proj_copied")
        stored = sem("stored")

        block = ctx.enter_context(nc.Block())
        early = early_order()

        def turn_bank(n, i):
            return 4 + (4 * n + i) % 3

        piece_at = early_pieces()

        def is_first(t):
            return isinstance(t, int) and t == 0

        def repeat(eng, n, body):
            body(0)
            with eng.Fori(1, n, 1) as t:
                body(t)

        SQ_X0, SQ_Y0, SQ_X1, SQ_Y2, SQ_X2, SQ_Y3, SQ_X3, SQ_Y4 = (16 * i for i in range(8))
        SC_MIX, SC_U1, SC_M1, SC_U2, SC_M2, SC_U3, SC_M3, SC_U4 = (16 * i for i in range(8))

        def split_piece(eng, part, s, u):
            s0, s_step, t = s
            u0, u_step, _ = u
            slot, half = s0 % RING, s0 % 2
            src = raw[u0 % RAW][:, half * PIECE:(half + 1) * PIECE]
            if part == "hi":
                eng.wait_ge(raw_landed[u0 % RAW], 16 * (u0 // RAW + 1) + t * (4 * u_step))
                if s0 >= RING or not is_first(t):
                    eng.wait_ge(piece_used, s0 - RING + 1 + t * s_step)
                eng.activation(w_hi[slot][:], src, ACT.Copy).then_inc(hi_done, 1)
            else:
                eng.wait_ge(hi_done, s0 + 1 + t * s_step)
                eng.tensor_tensor(w_lo[slot][:], src, w_hi[slot][:].bitcast(F32), ALU.subtract).then_inc(lo_done, 1)

        def split_run(eng, part, s, u, n):
            for i in range(n):
                split_piece(eng, part, (s + i, 0, 0), (u + i // 2, 0, 0))

        def consumed(v):
            if v < U_FFN0 + 6:
                return lo_done, 2 * (v + 1)
            if v < U_GAP1:
                c, k = divmod(v - U_FFN0 - 6, 10)
                _, _, split_off, mac_off = STEPS[0]
                if k in mac_off:
                    return mac_done, 32 * c + 8 * (mac_off.index(k) + 1)
                return lo_done, S_FFN0 + 12 + 12 * c + 2 * (split_off.index(k) + 1)
            if v < U_QKV:
                return gap_used, v - U_GAP1 + 1
            if v < U_GAP2:
                return lo_done, S_QKV + 2 * (v - U_QKV + 1)
            if v < U_FFN1:
                return gap_used, 4 * ADA_GAP1 + v - U_GAP2 + 1
            return lo_done, S_FFN1 + 2 * (v - U_FFN1 + 1)

        @block.sync
        def _(sp):
            def load(u0, u_step, t):
                if u0 >= RAW:
                    which, value = consumed(u0 - RAW)
                    later = consumed(u0 - RAW + u_step)[1] - value if u_step else 0
                    sp.wait_ge(which, value + t * later)
                src = stream[u0] if isinstance(t, int) and t == 0 else stream[bass.ds(t * u_step + u0, 1)]
                sp.dma_start(raw[u0 % RAW][:], src).then_inc(raw_landed[u0 % RAW], 16)

            def load_range(lo, hi, step):
                turns = (hi - lo) // step
                if turns > 1:
                    with sp.Fori(0, turns, 1) as t:
                        for i in range(step):
                            load(lo + i, step, t)
                    lo += turns * step
                for u in range(lo, hi):
                    load(u, 0, 0)

            for u in range(RAW):
                load(u, 0, 0)
            load_range(RAW, U_FFN0 + 6 + RAW, RAW)
            load_range(U_FFN0 + 6 + RAW, U_FFN0 + 6 + RAW + 20 * (CHUNKS // 2 - 1), 20)
            load_range(U_FFN0 + 6 + RAW + 20 * (CHUNKS // 2 - 1), U_GAP1 + RAW, UNITS)
            for lo, hi in ((U_GAP1, U_QKV), (U_QKV, U_GAP2), (U_GAP2, U_FFN1), (U_FFN1, UNITS - RAW)):
                load_range(lo + RAW, hi + RAW, RAW)
            sp.wait_ge(stored, 16 * (DT // 4))

        def stream_slices(tokens):
            return [(v, slice(v * SEQ, (v + 1) * SEQ)) for v in range(tokens // SEQ)]

        LAT = slice(0, SEQ)

        class Norm:
            def __init__(self, tokens, coef_row, shift_row, scaled0, mod0, std0):
                self.tokens, self.coef_row, self.shift_row = tokens, coef_row, shift_row
                self.scaled0, self.mod0, self.std0 = scaled0, mod0, std0

        POST = [Norm(TOK, 1, None, SC_U1, None, 1), Norm(TOK, 3, None, SC_U2, None, 3),
                Norm(SEQ, 5, None, SC_U3, None, 5), Norm(SEQ, 7, None, SC_U4, None, 7)]
        PRE = [Norm(TOK, 0, 0, SC_MIX, None, 0), Norm(TOK, 2, 3 * DT, SC_M1, 0, 2),
               Norm(TOK, 4, 6 * DT, SC_M2, 16, 4), Norm(SEQ, 6, 9 * DT, SC_M3, 32, 6)]

        @block.scalar
        def _(act):
            def square(n, src, tokens, scale=None):
                if n >= 2:
                    act.wait_ge(summed, n - 1)
                kw = {} if scale is None else {"scale": scale}
                act.activation(squares[:, n % 2, 0:tokens], src, ACT.Square, **kw).then_inc(squared, 1)

            def std(norm, bank, sums, count):
                act.wait_ge(sums, count)
                if norm.scaled0:
                    act.wait_ge(scaled, norm.scaled0)
                act.activation(rstd[:, 0:norm.tokens], banks[bank][:, 0:norm.tokens], ACT.Sqrt,
                               scale=1.0 / D, bias=eps_sb[:]).then_inc(std_ready, 1)

            def modulate_hi(norm, dt, hi):
                tile = work[dt % 4]
                act.wait_ge(scaled, norm.scaled0 + dt + 1)
                for v, ts in stream_slices(norm.tokens):
                    last = act.activation(tile[:, ts], tile[:, ts], ACT.Identity,
                                          scale=coef[:, norm.coef_row, dt, v:v + 1],
                                          bias=ada[:, norm.shift_row + dt, v:v + 1])
                last.then_inc(mod_full, 1)
                act.wait_ge(mod_full, norm.mod0 + dt + 1)
                act.activation(hi[:, dt, 0:norm.tokens], tile[:, 0:norm.tokens], ACT.Copy).then_inc(mod_hi, 1)

            act.dma_start(cond_sb[:], cond).then_inc(cond_landed, 16)
            consts = [(bias_sb, ada_bias), (gains_sb, gains), (pool_gain_sb, pool_gain), (rope_sb, rope),
                      (rot_sb, rotation), (ident, identity), (pairs_sb, pairs), (mask_sb, mask), (sinks_sb, sinks)]
            for dst, src in consts:
                act.dma_start(dst[:], src).then_inc(consts_landed, 16)
            act.dma_start(resid[:], x_in).then_inc(x_landed, 16)
            act.dma_start(counts[:], inv_counts).then_inc(counts_landed, 16)

            act.wait_ge(cond_landed, 16)
            act.activation(csilu[:], cond_sb[:], ACT.Silu).then_inc(cond_ready, 1)
            act.wait_ge(cond_ready, 1)
            act.activation(cparts[:, :, :, 0], csilu[:], ACT.Copy).then_inc(csilu_ready, 1)
            split_run(act, "hi", 0, 0, 16)
            act.wait_ge(x_landed, 16)
            for dt in range(2):
                square(SQ_X0 + dt, resid[:, dt, :], TOK)
            with act.Fori(1, 4, 1) as t:
                for i in range(16):
                    split_piece(act, "hi", (i, 16, t), (i // 2, 8, t))
                    if i % 4 == 3:
                        act.wait_ge(summed, t * 4 + i // 4 - 3)
                        tile = resid[:, bass.ds(t * 4 + (i // 4 - 2), 1), :].rearrange("p a b -> p (a b)")
                        act.activation(squares[:, i // 4 % 2, :], tile, ACT.Square).then_inc(squared, 1)
            for dt in range(DT - 2, DT):
                square(SQ_X0 + dt, resid[:, dt, :], TOK)
            act.wait_ge(consts_set, 1)
            std(PRE[0], 6, summed, SQ_X0 + 16)

            for kind, n in early:
                if kind in ("piece", "pool", "next"):
                    s = piece_at[(kind, n)]
                    split_piece(act, "hi", (s, 0, 0), (s // 2, 0, 0))
                elif kind == "shift":
                    if n == 0:
                        act.wait_ge(ada_added, 8)
                        act.wait_ge(padding_set, 1)
                    act.wait_ge(scaled, SC_MIX + n + 1)
                    if n >= 2:
                        act.wait_ge(diffed, n - 1)
                    for v, ts in stream_slices(TOK):
                        last = act.activation(padded[n % 2][:, v, PAD:PAD + SEQ], work[n % 2][:, ts],
                                              ACT.Identity, bias=ada[:, n, v:v + 1])
                    last.then_inc(shifted, 1)
                elif kind == "split":
                    act.wait_ge(diffed, n + 1)
                    if n >= 8:
                        act.wait_ge(piece_used, piece_at[("pool", 2 * (n // 4) - 3)] + 1)
                    act.activation(pooled_hi[n // 4 % 2][:, n % 4, :], work[2 + n % 2][:], ACT.Copy) \
                       .then_inc(pooled_hi_done, 1)
                elif kind == "evacuate":
                    act.wait_ge(piece_used, piece_at[("pool", n // 2)] + 1)
                    act.activation(pool_y[:, n, :], banks[n % 4][:], ACT.Copy, scale=pool_gain_sb[:, n:n + 1])
                    square(SQ_Y0 + n, banks[n % 4][:], TOK, scale=pool_gain_sb[:, n:n + 1])
                elif kind == "post_rstd":
                    std(POST[0], 6, summed, SQ_Y0 + 16)
                elif kind == "square":
                    act.wait_ge(updated, n + 1)
                    square(SQ_X1 + n, resid[:, n, :], TOK)
                elif kind == "pre_rstd":
                    std(PRE[1], 6, summed, SQ_X1 + 16)

            act.dma_start(spill, resid[:].rearrange("p a b -> p (a b)")).then_inc(spilled, 16)
            for dt in range(DT):
                modulate_hi(PRE[1], dt, h_hi)

            def silu_tile(layer, j, par, tokens):
                if par[1] >= 2 or not is_first(par[2]):
                    act.wait_ge(product[layer], j - 1)
                act.activation(work[par[0]][:, 0:tokens], banks[2 * par[0]][:, 0:tokens], ACT.Silu) \
                   .then_inc(gate_on[layer], 1)

            def round_tile(layer, j, slot, tokens):
                act.wait_ge(product[layer], j + 1)
                act.activation(g_hi[:, slot, 0:tokens], work[2 + slot % 2][:, 0:tokens], ACT.Copy) \
                   .then_inc(g_hi_done[layer], 1)

            def ffn_steps(layer, s_base, tokens):
                u_base, u_step, split_off, _ = STEPS[layer]
                for i in range(4, 12):
                    if i == 7:
                        act.wait_ge(piece_used, s_base + 4)
                        silu_tile(layer, 0, (0, 0, 0), tokens)
                    if i == 11:
                        act.wait_ge(piece_used, s_base + 8)
                        silu_tile(layer, 1, (1, 1, 0), tokens)
                    split_piece(act, "hi", (s_base + i, 0, 0), (u_base - 6 + i // 2, 0, 0))
                    if i == 7:
                        round_tile(layer, 0, 0, tokens)
                    if i == 11:
                        round_tile(layer, 1, 1, tokens)

                def step(par, t):
                    q = s_base + 12 + 12 * par
                    for i in range(12):
                        side_tile = {3: 0, 7: 1}.get(i)
                        j = 2 * par + 2 + (side_tile or 0)
                        if side_tile is not None:
                            act.wait_ge(piece_used, q + i - 3 + t * 24)
                            silu_tile(layer, j + t * 4, (side_tile, j, t), tokens)
                        split_piece(act, "hi", (q + i, 24, t),
                                    (u_base + u_step * par + split_off[i // 2], 2 * u_step, t))
                        if side_tile is not None:
                            round_tile(layer, j + t * 4, 2 * ((par + 1) % 2) + side_tile, tokens)

                with act.Fori(0, CHUNKS // 2 - 1, 1) as t:
                    step(0, t)
                    step(1, t)
                step(0, CHUNKS // 2 - 1)

            ffn_steps(0, S_FFN0, TOK)
            act.wait_ge(piece_used, S_QKV - 8)
            act.dma_start(saved[:].rearrange("p a b -> p (a b)"), spill).then_inc(reloaded, 16)
            for dt in range(DT):
                act.wait_ge(y_added[0], 16 * (CHUNKS - 1) + dt + 1)
                square(SQ_Y2 + dt, resid[:, dt, :], TOK)
            std(POST[1], 7, totalled, 1)
            for dt in range(DT):
                act.wait_ge(updated, 16 + dt + 1)
                square(SQ_X2 + dt, resid[:, dt, :], TOK)
            std(PRE[2], 6, totalled, 2)
            for dt in range(DT):
                modulate_hi(PRE[2], dt, h_hi)
                if dt in SPLIT_BEHIND:
                    i = 2 * SPLIT_BEHIND.index(dt)
                    split_run(act, "hi", S_QKV + i, U_QKV + i // 2, 2)

            split_run(act, "hi", S_QKV + 4, U_QKV + 2, 2)
            for m in range(2):
                act.wait_ge(piece_used, S_QKV + 2 * m + 2)
                act.activation(k32[:, m, :], banks[4 + m][:], ACT.Copy).then_inc(k_copied, 1)
                split_run(act, "hi", S_QKV + 6 + m, U_QKV + 3, 1)
            split_run(act, "hi", S_QKV + 8, U_QKV + 4, 4)
            act.wait_ge(piece_used, S_QKV + 8)
            for tt in range(4):
                act.activation(v32[:, tt, :], banks[tt][:, 0:KV], ACT.Copy).then_inc(v_copied, 1)

            def q_quad(t):
                for i in range(4):
                    for half in range(2):
                        split_piece(act, "hi", (S_QKV + 12 + 2 * i + half, 8, t), (U_QKV + 6 + i, 4, t))
                    act.wait_ge(piece_used, t * 8 + S_QKV + 10 + 2 * i)
                    if i >= 2 or not is_first(t):
                        act.wait_ge(q_ready, t * 4 + i - 1)
                    act.activation(work[i % 2][:, LAT], banks[i % 2][:, LAT], ACT.Copy).then_inc(q_copied, 1)

            repeat(act, Q_TILES // 4, q_quad)

            def key_round(m):
                if m:
                    act.wait_ge(scores, 32)
                else:
                    act.wait_ge(k_ready, 2)
                for b in range(2):
                    src = k32[64 * b:64 * b + 64, m, :]
                    for side_b in range(2):
                        last = act.activation(key_hi[64 * side_b:64 * side_b + 64, b, :], src, ACT.Copy)
                last.then_inc(key_hi_done, 1)

            def val_round(m):
                if m:
                    act.wait_ge(attended, 8)
                else:
                    act.wait_ge(v_copied, 4)
                act.activation(val_hi[:], v32[:, :, m * P:(m + 1) * P], ACT.Copy).then_inc(val_hi_done, 1)

            def q_round(n):
                pair, qt = n // 2, n % 2
                if n == 0:
                    act.wait_ge(q_ready, Q_TILES)
                if n >= 2:
                    act.wait_ge(scores, 4 * (n - 1))
                act.activation(q_hi[n % 2][:], side[:, 2 * pair:2 * pair + 2, qt * P:(qt + 1) * P], ACT.Copy) \
                   .then_inc(qs_hi, 1)

            def weigh(n, i):
                p = n % 2
                if i == 0:
                    act.wait_ge(sink_step, n + 1)
                    act.activation(sink_exp[p][:], sink_gap[p][:], ACT.Exp)
                act.activation(probs[p][:, i, :], probs[p][:, i, :], ACT.Exp, scale=Q_SCALE,
                               bias=neg_top[p][:, i:i + 1], accum_out=row_sum[p][:, i:i + 1]) \
                   .then_inc(weighed, 1)

            key_round(0)
            q_round(0)
            q_round(1)
            for i in range(4):
                weigh(0, i)
            val_round(0)
            q_round(2)
            for n in range(STEPS_ATT):
                if n == STEPS_ATT // 2 - 2:
                    key_round(1)
                if n == STEPS_ATT // 2:
                    val_round(1)
                for i in range(4):
                    act.wait_ge(turned, 4 * n + i + 1)
                    if n and i == 0:
                        act.wait_ge(attended, n)
                    act.activation(pt_hi[:, :, i, :],
                                   banks[turn_bank(n, i)][:].rearrange("p (k q) -> p k q", k=4),
                                   ACT.Copy).then_inc(pt_hi_done, 1)
                if n < STEPS_ATT - 1:
                    for i in range(4):
                        weigh(n + 1, i)
                if n < STEPS_ATT - 3:
                    q_round(n + 3)
                act.wait_ge(o_copied, n + 1)
                act.activation(o_hi[:, 2 * (n // 2):2 * (n // 2) + 2, (n % 2) * P:(n % 2 + 1) * P],
                               work[1][:, 0:SEQ].rearrange("p (a q) -> p a q", a=2), ACT.Copy) \
                   .then_inc(o_hi_done, 1)

            def out_quad(t):
                last_turn = isinstance(t, int) and t == DT // 4 - 1
                for i in range(4):
                    if i < 2 or not last_turn:
                        for half in range(2):
                            split_piece(act, "hi", (S_OUT + 4 + 2 * i + half, 8, t), (U_OUT + 2 + i, 4, t))
                    act.wait_ge(piece_used, t * 8 + S_OUT + 2 + 2 * i)
                    act.activation(side[:, bass.ds(t * 4 + i, 1), :].rearrange("p a b -> p (a b)"),
                                   banks[i % 2][:, LAT], ACT.Copy).then_inc(proj_copied, 1)
                    if i >= 2 or not is_first(t):
                        act.wait_ge(summed, t * 4 + SQ_Y3 + i - 1)
                    act.activation(squares[:, i % 2, LAT], banks[i % 2][:, LAT], ACT.Square) \
                       .then_inc(squared, 1)

            out_quad(0)
            with act.Fori(1, DT // 4 - 1, 1) as t:
                out_quad(t)
            out_quad(DT // 4 - 1)

            std(POST[2], 7, totalled, 3)
            for dt in range(DT):
                act.wait_ge(updated, 32 + dt + 1)
                square(SQ_X3 + dt, resid[:, dt, LAT], SEQ)
            std(PRE[3], 7, totalled, 4)
            for dt in range(DT):
                modulate_hi(PRE[3], dt, h1_hi)
                if dt in SPLIT_BEHIND:
                    i = 2 * SPLIT_BEHIND.index(dt)
                    split_run(act, "hi", S_FFN1 + i, U_FFN1 + i // 2, 2)
            ffn_steps(1, S_FFN1, SEQ)
            for dt in range(DT):
                act.wait_ge(y_added[1], 16 * (CHUNKS - 1) + dt + 1)
                square(SQ_Y4 + dt, side[:, dt, :], SEQ)
            std(POST[3], 7, totalled, 5)
            for dt in range(4, DT + 1, 4):
                own = sum(on_vector(i) for i in range(dt))
                act.wait_ge(updated, 48 + dt - own)
                act.wait_ge(finished, own)
                act.dma_start(out[:, dt - 4:dt, :], resid[:, dt - 4:dt, LAT]).then_inc(stored, 16)

        @block.vector
        def _(dve):
            def rstd_of(norm):
                dve.wait_ge(std_ready, norm.std0 + 1)
                dve.reciprocal(rstd[:, 0:norm.tokens], rstd[:, 0:norm.tokens]).then_inc(rstd_ready, 1)
                dve.wait_ge(rstd_ready, norm.std0 + 1)

            def scale_tile(norm, dt, src, free):
                if free is not None:
                    dve.wait_ge(*free)
                for v, ts in stream_slices(norm.tokens):
                    last = dve.scalar_tensor_tensor(work[dt % 2][:, ts], src[:, dt, ts],
                                                    coef[:, norm.coef_row, dt, v:v + 1], rstd[:, ts],
                                                    ALU.mult, ALU.mult)
                last.then_inc(scaled, 1)

            def modulate(norm, hi, lo, src, s=None, u=None):
                def normalise(dt):
                    if dt >= 4:
                        dve.wait_ge(mod_lo, norm.mod0 + dt - 3)
                    dve.tensor_tensor(work[dt % 4][:, 0:norm.tokens], src[:, dt, 0:norm.tokens],
                                      rstd[:, 0:norm.tokens], ALU.mult).then_inc(scaled, 1)

                def lo_part(dt):
                    dve.wait_ge(mod_hi, norm.mod0 + dt + 1)
                    dve.tensor_tensor(lo[:, dt, 0:norm.tokens], work[dt % 4][:, 0:norm.tokens],
                                      hi[:, dt, 0:norm.tokens].bitcast(F32), ALU.subtract).then_inc(mod_lo, 1)

                normalise(0)
                normalise(1)
                for dt in range(1, DT + 1):
                    if dt + 1 < DT:
                        normalise(dt + 1)
                    lo_part(dt - 1)
                    if s is not None and dt - 1 in SPLIT_BEHIND:
                        i = 2 * SPLIT_BEHIND.index(dt - 1)
                        split_run(dve, "lo", s + i, u + i // 2, 2)

            def coefs(row, ada_row, chunks):
                dve.wait_ge(ada_added, chunks)
                src = ada[:, ada_row * DT:(ada_row + 1) * DT, :]
                dve.scalar_tensor_tensor(coef[:, row], src, 1.0 if row % 2 == 0 else 0.0, gains_sb[:, row],
                                         ALU.add, ALU.mult).then_inc(coef_ready, 1)

            def row_copy(j, pieces, bank):
                dve.wait_ge(piece_used, pieces)
                if not (isinstance(j, int) and j < 2):
                    dve.wait_ge(cols_done, j - 1)
                dve.tensor_copy(ada_rows[0:4, bank % 2, :], banks[bank][0:4, :]).then_inc(rows_copied, 1)

            def bias_add(j, n=1):
                dve.wait_ge(cols_done, j + n)
                where = slice(4 * j, 4 * (j + n)) if isinstance(j, int) else bass.ds(j * 4, 4 * n)
                dve.tensor_tensor(ada[:, where, :], banks[7][:, 0:8 * n].rearrange("p (a v) -> p a v", v=2),
                                  bias_sb[:, where, :], ALU.add).then_inc(ada_added, n)

            dve.memset(ones[:], 1.0)
            dve.memset(eps_sb[:], EPS).then_inc(consts_set, 1)
            dve.wait_ge(csilu_ready, 1)
            dve.tensor_tensor(cparts[:, :, :, 1], csilu[:], cparts[:, :, :, 0].bitcast(F32), ALU.subtract) \
               .then_inc(csilu_ready, 1)
            split_run(dve, "lo", 0, 0, 12)
            row_copy(0, 8, 4)
            split_run(dve, "lo", 12, 6, 4)
            dve.wait_ge(consts_landed, 16 * 9)
            bias_add(0)

            def ada_pair(t):
                for k in range(2):
                    for i in range(8):
                        split_piece(dve, "lo", (8 * k + i, 16, t), (4 * k + i // 2, 8, t))
                        if i == 3:
                            row_copy(t * 2 + k - 1, t * 16 + 8 * k, 4 + (k + 1) % 2)
                    bias_add(t * 2 + k - 1)

            with dve.Fori(1, 4, 1) as t:
                ada_pair(t)
            row_copy(7, 64, 5)
            bias_add(7)
            coefs(0, 1, 8)
            rstd_of(PRE[0])
            dve.wait_ge(coef_ready, 1)

            for kind, n in early:
                if kind in ("piece", "pool", "next"):
                    s = piece_at[(kind, n)]
                    split_piece(dve, "lo", (s, 0, 0), (s // 2, 0, 0))
                if kind == "piece":
                    h, j = n // 4, 8 + n // 8
                    if h >= 2 and n % 4 == 3:
                        if h % 2 == 0:
                            row_copy(j - 1, piece_at[("piece", 4 * h - 1)] + 1, 4 + (j - 1) % 2)
                        else:
                            bias_add(j - 1)
                elif kind == "scale":
                    scale_tile(PRE[0], n, resid, None if n < 2 else (shifted, n - 1))
                elif kind == "split":
                    dve.wait_ge(pooled_hi_done, n + 1)
                    dve.tensor_tensor(pooled_lo[n // 4 % 2][:, n % 4, :], work[2 + n % 2][:],
                                      pooled_hi[n // 4 % 2][:, n % 4, :].bitcast(F32), ALU.subtract) \
                       .then_inc(pooled_lo_done, 1)
                elif kind == "post_rstd":
                    coefs(1, 2, 12)
                    rstd_of(POST[0])
                    dve.wait_ge(coef_ready, 2)
                elif kind == "update":
                    scale_tile(POST[0], n, pool_y, (shifted, 16) if n < 2 else (updated, n - 1))
                elif kind == "flush":
                    row_copy(ADA_EARLY - 1, piece_at[("piece", 4 * HALVES - 1)] + 1, 4 + (ADA_EARLY - 1) % 2)
                    bias_add(ADA_EARLY - 1)
                    coefs(2, 4, ADA_EARLY)
                elif kind == "pre_rstd":
                    rstd_of(PRE[1])

            dve.wait_ge(coef_ready, 3)
            dve.wait_ge(updated, 16)
            modulate(PRE[1], h_hi, h_lo, resid)

            def product_tile(layer, j, par, tokens):
                dve.wait_ge(gate_on[layer], j + 1)
                if not (isinstance(j, int) and j < 2):
                    dve.wait_ge(g_lo_done[layer], j - 1)
                dve.tensor_tensor(work[2 + par][:, 0:tokens], work[par][:, 0:tokens],
                                  banks[2 * par + 1][:, 0:tokens], ALU.mult).then_inc(product[layer], 1)

            def product_lo(layer, j, slot, tokens):
                dve.wait_ge(g_hi_done[layer], j + 1)
                dve.tensor_tensor(g_lo[:, slot, 0:tokens], work[2 + slot % 2][:, 0:tokens],
                                  g_hi[:, slot, 0:tokens].bitcast(F32), ALU.subtract).then_inc(g_lo_done[layer], 1)

            def mac_tile(n, par, t, u0):
                k = n % 4
                if k == 0:
                    dve.wait_ge(raw_landed[u0 % RAW], 16 * (u0 // RAW + 1) + t * 80)
                if n == 0:
                    dve.wait_ge(cols_done, ADA_EARLY + par + t * 2)
                else:
                    dve.wait_ge(mac_done, 32 * par + 2 * n + t * 64)
                for v in range(2):
                    w = raw[u0 % RAW][:, k * 512:(k + 1) * 512]
                    c = csilu[:, n, v:v + 1]
                    if n == 0:
                        dve.tensor_scalar(ada_acc[:, v, :], w, c, None, ALU.mult).then_inc(mac_done, 1)
                    else:
                        dve.scalar_tensor_tensor(ada_acc[:, v, :], w, c, ada_acc[:, v, :], ALU.mult, ALU.add) \
                           .then_inc(mac_done, 1)

            def add_square(base, dt, tokens, t=0):
                if dt == 0 and is_first(t):
                    return
                dve.wait_ge(squared, base + dt + 1 + t * 4)
                total = square_sum[:, 0:tokens]
                if dt == 1 and is_first(t):
                    dve.tensor_tensor(total, squares[:, 0, 0:tokens], squares[:, 1, 0:tokens], ALU.add) \
                       .then_inc(summed, 2)
                else:
                    dve.wait_ge(summed, base + dt + t * 4)
                    dve.tensor_tensor(total, total, squares[:, dt % 2, 0:tokens], ALU.add).then_inc(summed, 1)

            def update_tiles(norm, src, updates, sq):
                for dt in range(DT + 3):
                    if dt < DT:
                        scale_tile(norm, dt, src, None if dt < 2 else (updated, updates + dt - 1))
                    if dt >= 3:
                        add_square(sq, dt - 3, norm.tokens)

            def ffn_steps(layer, s_base, tokens, y, sq):
                u_base, u_step, split_off, mac_off = STEPS[layer]
                for i in range(4, 12):
                    if i == 7:
                        product_tile(layer, 0, 0, tokens)
                    if i == 11:
                        product_tile(layer, 1, 1, tokens)
                    split_piece(dve, "lo", (s_base + i, 0, 0), (u_base - 6 + i // 2, 0, 0))
                    if i == 7:
                        product_lo(layer, 0, 0, tokens)
                    if i == 11:
                        product_lo(layer, 1, 1, tokens)

                def add_down(dt, q, parts, t):
                    if dt % 4 == 3:
                        dve.wait_ge(piece_used, q + dt // 4 + 1 + t * 24)
                    else:
                        dve.wait_ge(down_part[layer], parts + 3 * (dt // 4) + dt % 4 + 1 + t * 24)
                    dve.tensor_tensor(y[:, dt, :], y[:, dt, :], banks[4 + dt % 3][:, 0:tokens], ALU.add) \
                       .then_inc(y_added[layer], 1)

                def step(par, t):
                    q = s_base + 12 + 12 * par
                    ub = u_base + u_step * par
                    for i in range(12):
                        side_tile = {3: 0, 7: 1}.get(i)
                        j = 2 * par + 2 + (side_tile or 0)
                        if side_tile is not None:
                            product_tile(layer, j + t * 4, side_tile, tokens)
                        for dt in {7: (0, 1), 8: (3, 4, 5), 9: (6, 7, 8, 9), 10: (10, 11, 12, 13),
                                   11: (14, 15)}.get(i, ()):
                            add_down(dt, q + 4, 12 * par, t)
                        if mac_off and i % 2 == 0 and i < 8:
                            for k in range(4):
                                mac_tile(2 * i + k, par, t, ub + mac_off[i // 2])
                        split_piece(dve, "lo", (q + i, 24, t), (ub + split_off[i // 2], 2 * u_step, t))
                        if i == 7:
                            add_down(2, q + 4, 12 * par, t)
                        if side_tile is not None:
                            product_lo(layer, j + t * 4, 2 * ((par + 1) % 2) + side_tile, tokens)
                        if mac_off and i == 11:
                            bias_add(ADA_EARLY + par + t * 2)

                dve.wait_ge(cleared, layer + 1)
                with dve.Fori(0, CHUNKS // 2 - 1, 1) as t:
                    step(0, t)
                    step(1, t)
                step(0, CHUNKS // 2 - 1)
                dve.wait_ge(g_lo_done[layer], FT)
                for dt in range(DT):
                    add_down(dt, s_base + 12 * (CHUNKS - 1) + 8, 12 * (CHUNKS - 1), 0)
                    if dt:
                        add_square(sq, dt - 1, tokens)
                add_square(sq, DT - 1, tokens)

            ffn_steps(0, S_FFN0, TOK, resid, SQ_Y2)

            coefs(3, 5, ADA_CHUNKS)
            coefs(4, 7, ADA_CHUNKS + 8)
            coefs(5, 8, ADA_CHUNKS + 12)
            rstd_of(POST[1])
            dve.wait_ge(coef_ready, 6)
            dve.wait_ge(reloaded, 16)
            update_tiles(POST[1], resid, 16, SQ_X2)
            rstd_of(PRE[2])
            dve.wait_ge(updated, 32)
            modulate(PRE[2], h_hi, h_lo, resid, S_QKV, U_QKV)

            def gap_rows(n, units, chunks, bank):
                dve.wait_ge(gap_used, units)
                dve.wait_ge(cols_done, chunks)
                for i in range(n):
                    dve.tensor_copy(ada_rows[0:2, i, :], banks[bank + i][0:2, :]).then_inc(rows_copied, 1)

            gap_rows(ADA_GAP1, 4 * ADA_GAP1, ADA_EARLY + ADA_BESIDE, 0)

            cos, sin = rope_sb[:, 0, :], rope_sb[:, 1, :]
            split_run(dve, "lo", S_QKV + 4, U_QKV + 2, 4)
            bias_add(ADA_EARLY + ADA_BESIDE, ADA_GAP1)
            coefs(6, 10, ADA_CHUNKS + 20)
            for m in range(2):
                lat = k32[:, m, LAT]
                dve.wait_ge(k_turned, m + 1)
                dve.tensor_tensor(work[2 + m][:, LAT], banks[6 + m][:, LAT], sin, ALU.mult)
                dve.tensor_tensor(lat, lat, cos, ALU.mult).then_inc(k_rope, 1)
                dve.wait_ge(k_rope, m + 1)
                dve.tensor_tensor(lat, lat, work[2 + m][:, LAT], ALU.add).then_inc(k_ready, 1)
            split_run(dve, "lo", S_QKV + 8, U_QKV + 4, 4)

            def q_finish(j, i):
                dve.wait_ge(q_turned, j + 1)
                if isinstance(j, int) and j < 2:
                    dve.wait_ge(k_ready, 2)
                else:
                    dve.wait_ge(q_ready, j - 1)
                dst = side[:, bass.ds(j, 1), :].rearrange("p a b -> p (a b)")
                dve.tensor_tensor(work[2 + i % 2][:, LAT], banks[2 + i % 2][:, LAT], sin, ALU.mult)
                dve.tensor_tensor(dst, work[i % 2][:, LAT], cos, ALU.mult).then_inc(q_rope, 1)
                dve.wait_ge(q_rope, j + 1)
                dve.tensor_tensor(dst, dst, work[2 + i % 2][:, LAT], ALU.add).then_inc(q_ready, 1)

            def q_quad(t):
                for i in range(4):
                    if i or not is_first(t):
                        q_finish(t * 4 + i - 1, i + 3)
                    for half in range(2):
                        split_piece(dve, "lo", (S_QKV + 12 + 2 * i + half, 8, t), (U_QKV + 6 + i, 4, t))

            repeat(dve, Q_TILES // 4, q_quad)
            q_finish(Q_TILES - 1, 3)

            def key_rest(m):
                dve.wait_ge(key_hi_done, m + 1)
                for b in range(2):
                    own = slice(64 * b, 64 * b + 64)
                    dve.tensor_tensor(key_lo[own, b, :], k32[own, m, :], key_hi[own, b, :].bitcast(F32),
                                      ALU.subtract).then_inc(key_lo_done, 1)
                dve.wait_ge(key_lo_done, 4 * m + 2)
                for b in range(2):
                    own, other = slice(64 * b, 64 * b + 64), slice(64 * (1 - b), 64 * (1 - b) + 64)
                    dve.tensor_copy(key_lo[other, b, :], key_lo[own, b, :].bitcast(F32)) \
                       .then_inc(key_lo_done, 1)

            def val_rest(m):
                dve.wait_ge(val_hi_done, m + 1)
                dve.tensor_tensor(val_lo[:], v32[:, :, m * P:(m + 1) * P], val_hi[:].bitcast(F32),
                                  ALU.subtract).then_inc(val_lo_done, 1)

            def q_rest(n):
                pair, qt = n // 2, n % 2
                dve.wait_ge(qs_hi, n + 1)
                dve.tensor_tensor(q_lo[n % 2][:], side[:, 2 * pair:2 * pair + 2, qt * P:(qt + 1) * P],
                                  q_hi[n % 2][:].bitcast(F32), ALU.subtract).then_inc(qs_lo, 1)

            def head_max(n):
                pair, qt = n // 2, n % 2
                p = n % 2
                for i in range(4):
                    dve.wait_ge(scores, 4 * n + i + 1)
                    if n >= 2 and i == 0:
                        dve.wait_ge(turned, 4 * (n - 1))
                    dve.tensor_tensor_reduce(probs[p][:, i, :], banks[i][:], mask_sb[:, qt, :], 1.0, 2 * MASKED,
                                             ALU.add, ALU.max, row_max[p][:, i:i + 1]).then_inc(masked, 1)
                own_sinks = sinks_sb[:, 4 * pair:4 * pair + 4]
                dve.wait_ge(masked, 4 * n + 4)
                dve.scalar_tensor_tensor(top[p][:], row_max[p][:], Q_SCALE, own_sinks, ALU.mult, ALU.max) \
                   .then_inc(top_ready, 1)
                dve.wait_ge(top_ready, n + 1)
                dve.tensor_scalar(neg_top[p][:], top[p][:], -1.0, None, ALU.mult)
                dve.tensor_tensor(sink_gap[p][:], own_sinks, top[p][:], ALU.subtract).then_inc(sink_step, 1)

            def normalisers(n):
                p = n % 2
                dve.wait_ge(weighed, 4 * n + 4)
                dve.tensor_tensor(denom[p][:], row_sum[p][:], sink_exp[p][:], ALU.add).then_inc(denom_step, 1)
                dve.wait_ge(denom_step, 2 * n + 1)
                dve.reciprocal(inv_denom[p][:], denom[p][:]).then_inc(denom_step, 1)
                dve.wait_ge(denom_step, 2 * n + 2)
                for i in range(4):
                    dve.tensor_scalar(diag[p][:, i * P:(i + 1) * P], ident[:], inv_denom[p][:, i:i + 1], None,
                                      ALU.mult).then_inc(diag_ready, 1)

            key_rest(0)
            q_rest(0)
            q_rest(1)
            dve.wait_ge(q_ready, Q_TILES)
            head_max(0)
            head_max(1)
            normalisers(0)
            val_rest(0)
            q_rest(2)
            for n in range(STEPS_ATT):
                if n == STEPS_ATT // 2 - 2:
                    key_rest(1)
                if n == STEPS_ATT // 2:
                    val_rest(1)
                for i in range(4):
                    dve.wait_ge(pt_hi_done, 4 * n + i + 1)
                    dve.tensor_tensor(pt_lo[:, :, i, :],
                                      banks[turn_bank(n, i)][:].rearrange("p (k q) -> p k q", k=4),
                                      pt_hi[:, :, i, :].bitcast(F32), ALU.subtract).then_inc(pt_lo_done, 1)
                if n < STEPS_ATT - 2:
                    head_max(n + 2)
                if n < STEPS_ATT - 1:
                    normalisers(n + 1)
                if n < STEPS_ATT - 3:
                    q_rest(n + 3)
                dve.wait_ge(attended, n + 1)
                rows = slice(64 * (n // 4 % 2), 64 * (n // 4 % 2) + 64)
                got = banks[7][:].rearrange("p (a b q) -> p a b q", a=2, b=2)
                for b in range(2):
                    last = dve.tensor_copy(work[1][64 * b:64 * b + 64, 0:SEQ].rearrange("p (a q) -> p a q", a=2),
                                           got[rows, :, b, :])
                last.then_inc(o_copied, 1)
                dve.wait_ge(o_hi_done, n + 1)
                where = (slice(None), slice(2 * (n // 2), 2 * (n // 2) + 2), slice((n % 2) * P, (n % 2 + 1) * P))
                dve.tensor_tensor(o_lo[where], work[1][:, 0:SEQ].rearrange("p (a q) -> p a q", a=2),
                                  o_hi[where].bitcast(F32), ALU.subtract).then_inc(o_lo_done, 1)

            def out_quad(t):
                for i in range(4):
                    for half in range(2):
                        split_piece(dve, "lo", (S_OUT + 4 + 2 * i + half, 8, t), (U_OUT + 2 + i, 4, t))
                    add_square(SQ_Y3, i, SEQ, t)

            repeat(dve, DT // 4 - 1, out_quad)
            for i in range(2):
                split_run(dve, "lo", S_FFN1 - 4 + 2 * i, U_GAP2 - 2 + i, 2)
                add_square(SQ_Y3, DT - 4 + i, SEQ)
            for i in range(2, 4):
                add_square(SQ_Y3, DT - 4 + i, SEQ)
            rstd_of(POST[2])
            dve.wait_ge(proj_copied, 16)
            update_tiles(POST[2], side, 32, SQ_X3)
            rstd_of(PRE[3])
            dve.wait_ge(coef_ready, 7)
            dve.wait_ge(updated, 48)
            modulate(PRE[3], h1_hi, h1_lo, resid, S_FFN1, U_FFN1)
            gap_rows(ADA_GAP2, 4 * (ADA_GAP1 + ADA_GAP2), 2 * ADA_CHUNKS - ADA_GAP2, 4)
            bias_add(2 * ADA_CHUNKS - ADA_GAP2, ADA_GAP2)
            coefs(7, 11, 2 * ADA_CHUNKS)
            ffn_steps(1, S_FFN1, SEQ, side, SQ_Y4)
            rstd_of(POST[3])
            dve.wait_ge(coef_ready, 8)
            for dt in range(DT):
                if dt >= 4 and on_vector(dt - 4):
                    dve.wait_ge(finished, sum(on_vector(i) for i in range(dt - 3)))
                elif dt >= 4:
                    dve.wait_ge(updated, 48 + dt - 3 - sum(on_vector(i) for i in range(dt - 3)))
                dve.scalar_tensor_tensor(work[dt % 4][:, LAT], side[:, dt, :], coef[:, POST[3].coef_row, dt, 0:1],
                                         rstd[:, LAT], ALU.mult, ALU.mult).then_inc(scaled, 1)
                if on_vector(dt):
                    dve.wait_ge(scaled, SC_U4 + dt + 1)
                    dve.tensor_tensor(resid[:, dt, LAT], work[dt % 4][:, LAT], resid[:, dt, LAT], ALU.add) \
                       .then_inc(finished, 1)

        @block.gpsimd
        def _(pool):
            for i in range(2):
                last = pool.memset(padded[i][:], 0.0)
            last.then_inc(padding_set, 1)
            pool.wait_ge(padding_set, 1)
            pool.wait_ge(counts_landed, 16)

            steps = [0]

            def step(ins):
                ins.then_inc(window_step, 1)
                steps[0] += 1
                pool.wait_ge(window_step, steps[0])

            def mix(dt):
                w = WINDOWS[dt // 4]
                pool.wait_ge(shifted, dt + 1)
                if dt:
                    pool.wait_ge(diffed, dt)
                src, n = padded[dt % 2], SEQ + 2 * PAD
                span = 1
                while span < w:
                    dst = window[0] if src is not window[0] else window[1]
                    n -= span
                    step(pool.tensor_tensor(dst[:, :, 0:n], src[:, :, 0:n], src[:, :, span:span + n], ALU.add))
                    src, span = dst, 2 * span
                other = window[0] if src is not window[0] else window[1]
                for v in range(2):
                    last = pool.tensor_tensor(other[:, v, 0:SEQ], src[:, v, PAD - w // 2:PAD - w // 2 + SEQ],
                                              counts[:, dt // 4, :], ALU.mult)
                step(last)
                if dt >= 2:
                    pool.wait_ge(pooled_lo_done, dt - 1)
                pool.tensor_tensor(work[2 + dt % 2][:].rearrange("p (v t) -> p v t", v=2), other[:, :, 0:SEQ],
                                   padded[dt % 2][:, :, PAD:PAD + SEQ], ALU.subtract).then_inc(diffed, 1)

            for dt in range(DT):
                mix(dt)

            def update(first, tokens, old):
                for dt in range(DT):
                    pool.wait_ge(scaled, first + dt + 1)
                    pool.tensor_tensor(resid[:, dt, 0:tokens], work[dt % 2][:, 0:tokens], old[:, dt, 0:tokens],
                                       ALU.add).then_inc(updated, 1)

            update(SC_U1, TOK, resid)
            pool.wait_ge(spilled, 16)
            pool.wait_ge(mod_lo, 16)
            pool.memset(resid[:], 0.0).then_inc(cleared, 1)
            pool.wait_ge(reloaded, 16)
            update(SC_U2, TOK, saved)
            update(SC_U3, SEQ, resid)
            pool.memset(side, 0.0).then_inc(cleared, 1)
            for dt in range(DT):
                if not on_vector(dt):
                    pool.wait_ge(scaled, SC_U4 + dt + 1)
                    pool.tensor_tensor(resid[:, dt, LAT], work[dt % 4][:, LAT], resid[:, dt, LAT],
                                       ALU.add).then_inc(updated, 1)

        @block.tensor
        def _(pe):
            def piece_ready(s0, s_step=0, t=0):
                pe.wait_ge(lo_done, s0 + 1 + t * s_step)

            def three_passes(dst, wh, wl, xh, xl, start, stop):
                pe.matmul(dst, wh, xh, start=start, stop=False)
                pe.matmul(dst, wh, xl, start=False, stop=False)
                return pe.matmul(dst, wl, xh, start=False, stop=stop)

            def product_piece(dst, s0, xh, xl, tokens, k0, s_step=0, t=0):
                piece_ready(s0, s_step, t)
                slot = s0 % RING
                for i in range(8):
                    k = k0 + i
                    cols = slice(i * P, (i + 1) * P)
                    last = three_passes(dst, w_hi[slot][:, cols], w_lo[slot][:, cols], xh[:, k, 0:tokens],
                                        xl[:, k, 0:tokens], k == 0, k == DT - 1)
                last.then_inc(piece_used, 1)

            def product_pair(dsts, s0, xh, xl, tokens, mod0):
                for k in range(DT):
                    pe.wait_ge(mod_lo, mod0 + k + 1)
                    for n, dst in enumerate(dsts):
                        s = s0 + 2 * n + k // 8
                        if k % 8 == 0:
                            piece_ready(s)
                        cols = slice(k % 8 * P, (k % 8 + 1) * P)
                        last = three_passes(dst, w_hi[s % RING][:, cols], w_lo[s % RING][:, cols],
                                            xh[:, k, 0:tokens], xl[:, k, 0:tokens], k == 0, k == DT - 1)
                last.then_inc(piece_used, 4)

            def add_squares(n, bank, tokens):
                pe.wait_ge(squared, n + 1)
                pe.matmul(banks[bank][:, 0:tokens], ones[:], squares[:, n % 2, 0:tokens],
                          start=(n % DT == 0), stop=(n % DT == DT - 1)).then_inc(summed, 1)

            def total_squares(base, bank, tokens):
                pe.wait_ge(summed, base + DT)
                pe.matmul(banks[bank][:, 0:tokens], ones[:], square_sum[:, 0:tokens], start=True, stop=True) \
                  .then_inc(totalled, 1)

            def ada_piece(s0, q, bank, s_step=0, t=0):
                piece_ready(s0, s_step, t)
                slot = s0 % RING
                for i in range(2):
                    k = 2 * q + i
                    parts = cparts[:, k].rearrange("p v h -> p (v h)")
                    for n, w in enumerate((w_hi, w_lo)):
                        last = pe.matmul(banks[bank][0:4, :], parts, w[slot][:, i * 512:(i + 1) * 512],
                                         start=(k == 0 and n == 0), stop=(k == DT - 1 and n == 1))
                last.then_inc(piece_used, 1)

            def turn(row_tile, rows, columns, n=0):
                for i in range(4):
                    last = pe.matmul(banks[7][:, 8 * n + 2 * i:8 * n + 2 * i + 2],
                                     ada_rows[0:rows, row_tile, i * P:(i + 1) * P], columns, start=True, stop=True)
                return last

            def turn_rows(j, row_tile):
                pe.wait_ge(rows_copied, j + 1)
                if not is_first(j):
                    pe.wait_ge(ada_added, j)
                turn(row_tile, 4, pairs_sb[:]).then_inc(cols_done, 1)

            def ada_chunk(j, s0, bank, turned_chunk, s_step=0, t=0):
                if not (isinstance(j, int) and j < 2):
                    pe.wait_ge(rows_copied, j - 1)
                for q in range(8):
                    ada_piece(s0 + q, q, bank, s_step, t)
                    if s_step and q % 4 == 3:
                        i = 2 * (bank % 2) + q // 4
                        pe.wait_ge(squared, t * 4 + i - 1)
                        pe.matmul(banks[6][:], ones[:], squares[:, i % 2, :], start=False, stop=False,
                                  skip_group_check=True).then_inc(summed, 1)
                    if q == 3 and turned_chunk is not None:
                        turn_rows(turned_chunk, (bank + 1) % 2)

            pe.wait_ge(csilu_ready, 2)
            pe.wait_ge(consts_set, 1)
            pe.wait_ge(consts_landed, 16 * 9)
            ada_chunk(0, 0, 4, None)
            ada_chunk(1, 8, 5, 0)
            for dt in range(2):
                add_squares(SQ_X0 + dt, 6, TOK)
            with pe.Fori(1, 4, 1) as t:
                for k in range(2):
                    ada_chunk(t * 2 + k, 8 * k, 4 + k, t * 2 + k - 1, 16, t)
            for dt in range(DT - 2, DT):
                add_squares(SQ_X0 + dt, 6, TOK)
            turn_rows(7, 1)
            for kind, n in early:
                if kind == "piece":
                    h, i = divmod(n, 4)
                    j = 8 + h // 2
                    if h % 2 == 0 and i == 0:
                        pe.wait_ge(rows_copied, j - 1)
                    ada_piece(piece_at[(kind, n)], 4 * (h % 2) + i, 4 + j % 2)
                    if h % 2 == 1 and h >= 3 and i == 0:
                        turn_rows(j - 1, (j - 1) % 2)
                elif kind == "flush":
                    turn_rows(ADA_EARLY - 1, (ADA_EARLY - 1) % 2)
                elif kind == "pool":
                    group, q = divmod(n, 2)
                    pe.wait_ge(pooled_lo_done, 4 * group + 4)
                    if group:
                        pe.wait_ge(squared, SQ_Y0 + 4 * group)
                    s = piece_at[(kind, n)]
                    piece_ready(s)
                    for i in range(2):
                        for k in range(4):
                            cols = slice((4 * i + k) * P, (4 * i + k + 1) * P)
                            last = three_passes(banks[2 * q + i][:], w_hi[s % RING][:, cols],
                                                w_lo[s % RING][:, cols], pooled_hi[group % 2][:, k, :],
                                                pooled_lo[group % 2][:, k, :], k == 0, k == 3)
                    last.then_inc(piece_used, 1)
                elif kind == "evacuate":
                    add_squares(SQ_Y0 + n, 6, TOK)
                elif kind == "square":
                    add_squares(SQ_X1 + n, 6, TOK)

            def ffn(layer, s_base, tokens, xh, xl, mod0, after_first_tile=None):
                def gate_up(s0, j0, s_step=0, t=0):
                    for i in range(2):
                        pe.wait_ge(product[layer], j0 + i - 1)
                        tile_pair(s0, i, s_step, t)

                def tile_pair(s0, i, s_step=0, t=0):
                    for n in range(2):
                        for half in range(2):
                            product_piece(banks[2 * i + n][:, 0:tokens], s0 + 4 * i + 2 * n + half, xh, xl,
                                          tokens, 8 * half, s_step, t)

                def down(s0, c0, slots, first, s_step=0, t=0):
                    pe.wait_ge(g_lo_done[layer], 2 * c0 + 2 + t * 4)
                    for q in range(4):
                        piece_ready(s0 + q, s_step, t)
                        slot = (s0 + q) % RING
                        for i in range(4):
                            dt = 4 * q + i
                            if dt >= 3 or not first:
                                pe.wait_ge(y_added[layer], 16 * c0 + max(dt - 2, 0) + t * 32)
                            for k in range(2):
                                cols = slice((2 * i + k) * P, (2 * i + k + 1) * P)
                                last = three_passes(banks[4 + dt % 3][:, 0:tokens], w_hi[slot][:, cols],
                                                    w_lo[slot][:, cols], g_hi[:, slots + k, 0:tokens],
                                                    g_lo[:, slots + k, 0:tokens], k == 0, k == 1)
                            last.then_inc(piece_used if i == 3 else down_part[layer], 1)

                def turn_beside(par, t):
                    pe.wait_ge(mac_done, 32 * (par + 1) + t * 64)
                    pe.wait_ge(ada_added, ADA_EARLY + par + t * 2)
                    for i in range(4):
                        for v in range(2):
                            last = pe.matmul(banks[7][:, 2 * i + v:2 * i + v + 1],
                                             ada_acc[:, v, i * P:(i + 1) * P], ones[:, 0:1], start=True, stop=True)
                    last.then_inc(cols_done, 1)

                def step(par, t):
                    gate_up(s_base + 8 + 12 * par, t * 4 + 2 * par + 2, 24, t)
                    down(s_base + 16 + 12 * par, par, 2 * par, par == 0 and is_first(t), 24, t)
                    if layer == 0:
                        turn_beside(par, t)

                product_pair([banks[0][:, 0:tokens], banks[1][:, 0:tokens]], s_base, xh, xl, tokens, mod0)
                if after_first_tile is not None:
                    after_first_tile()
                tile_pair(s_base, 1)

                def two_steps(t):
                    step(0, t)
                    step(1, t)

                repeat(pe, CHUNKS // 2 - 1, two_steps)
                step(0, CHUNKS // 2 - 1)
                if layer == 0:
                    pe.wait_ge(ada_added, ADA_EARLY + ADA_BESIDE)
                down(s_base + 12 * (CHUNKS - 1) + 8, CHUNKS - 1, 2, False)

            ffn(0, S_FFN0, TOK, h_hi, h_lo, 0)

            def gap_chunks(u0, n, bank, sq_at):
                for i in range(n):
                    for k in range(DT):
                        u = u0 + 4 * i + k // 4
                        if k % 4 == 0:
                            pe.wait_ge(raw_landed[u % RAW], 16 * (u // RAW + 1))
                        last = pe.matmul(banks[bank + i][0:2, :], csilu[:, k, :],
                                         raw[u % RAW][:, (k % 4) * 512:(k % 4 + 1) * 512],
                                         start=(k == 0), stop=(k == DT - 1))
                        if k % 4 == 3:
                            last.then_inc(gap_used, 1)
                        if DT * i + k in sq_at:
                            total_squares(*sq_at[DT * i + k])

            def turn_gap(n, units_before):
                pe.wait_ge(rows_copied, units_before + n)
                for i in range(n):
                    last = turn(i, 2, ident[0:2, 0:2], i)
                last.then_inc(cols_done, n)

            pe.wait_ge(product[0], FT)
            gap_chunks(U_GAP1, ADA_GAP1, 0, {1: (SQ_Y2, 7, TOK), 34: (SQ_X2, 6, TOK)})

            def turn_key(m):
                pe.wait_ge(k_copied, m + 1)
                if m == 1:
                    pe.wait_ge(ada_added, ADA_EARLY + ADA_BESIDE + ADA_GAP1)
                pe.matmul(banks[6 + m][:, LAT], rot_sb[:], k32[:, m, LAT], start=True, stop=True) \
                  .then_inc(k_turned, 1)

            product_pair([banks[4][:], banks[5][:]], S_QKV, h_hi, h_lo, TOK, 16)
            turn_gap(ADA_GAP1, ADA_EARLY)
            turn_key(0)
            for q in range(4):
                s0 = S_QKV + 4 + q
                piece_ready(s0)
                for i in range(4):
                    k = 4 * q + i
                    cols = slice(i * KV, (i + 1) * KV)
                    for tt in range(4):
                        ts = slice(tt * P, (tt + 1) * P)
                        last = three_passes(banks[tt][:, 0:KV], h_hi[:, k, ts], h_lo[:, k, ts],
                                            w_hi[s0 % RING][:, cols], w_lo[s0 % RING][:, cols],
                                            k == 0, k == DT - 1)
                last.then_inc(piece_used, 1)
            turn_key(1)
            pe.wait_ge(v_copied, 4)

            def turn_query(j, i):
                pe.wait_ge(q_copied, j + 1)
                pe.matmul(banks[2 + i % 2][:, LAT], rot_sb[:], work[i % 2][:, LAT], start=True, stop=True) \
                  .then_inc(q_turned, 1)

            def q_quad(t):
                for i in range(4):
                    if i >= 2 or not is_first(t):
                        pe.wait_ge(q_copied, t * 4 + i - 1)
                    for half in range(2):
                        product_piece(banks[i % 2][:, LAT], S_QKV + 8 + 2 * i + half, h_hi, h_lo, SEQ, 8 * half,
                                      8, t)
                    if i or not is_first(t):
                        if i >= 3 or not is_first(t):
                            pe.wait_ge(q_ready, t * 4 + i - 2)
                        turn_query(t * 4 + i - 1, i + 3)

            repeat(pe, Q_TILES // 4, q_quad)
            pe.wait_ge(q_ready, Q_TILES - 2)
            turn_query(Q_TILES - 1, 3)

            def score_heads(n):
                b = n // 4 % 2
                pe.wait_ge(key_lo_done, 4 * (n // 8) + 4)
                pe.wait_ge(qs_lo, n + 1)
                for i in range(4):
                    if n:
                        pe.wait_ge(masked, 4 * (n - 1) + i + 1)
                    rows = slice(64 * (i % 2), 64 * (i % 2) + 64)
                    qh, ql = q_hi[n % 2][rows, i // 2, :], q_lo[n % 2][rows, i // 2, :]
                    kh, kl = key_hi[rows, b, :], key_lo[rows, b, :]
                    pe.matmul(banks[i][:], qh, kh, start=True, stop=False)
                    pe.matmul(banks[i][:], ql, kh, start=False, stop=False)
                    pe.matmul(banks[i][:], qh, kl, start=False, stop=True).then_inc(scores, 1)

            def turn_probs(n):
                for i in range(4):
                    pe.wait_ge(diag_ready, 4 * n + i + 1)
                    if 4 * n + i >= 3:
                        pe.wait_ge(pt_lo_done, 4 * n + i - 2)
                    for kt in range(4):
                        last = pe.matmul(banks[turn_bank(n, i)][:, kt * P:(kt + 1) * P],
                                         probs[n % 2][:, i, kt * P:(kt + 1) * P], diag[n % 2][:, i * P:(i + 1) * P],
                                         start=True, stop=True)
                    last.then_inc(turned, 1)

            def attend(n):
                pe.wait_ge(val_lo_done, n // 8 + 1)
                pe.wait_ge(pt_lo_done, 4 * n + 4)
                if n:
                    pe.wait_ge(o_copied, n)
                for kt in range(4):
                    last = three_passes(banks[7][:], val_hi[:, kt, :], val_lo[:, kt, :],
                                        pt_hi[:, kt].rearrange("p h q -> p (h q)"),
                                        pt_lo[:, kt].rearrange("p h q -> p (h q)"), kt == 0, kt == 3)
                last.then_inc(attended, 1)

            score_heads(0)
            score_heads(1)
            for n in range(STEPS_ATT):
                turn_probs(n)
                if n < STEPS_ATT - 2:
                    score_heads(n + 2)
                attend(n)

            pe.wait_ge(o_lo_done, 16)

            def out_quad(t):
                for i in range(4):
                    if i >= 2 or not is_first(t):
                        pe.wait_ge(squared, t * 4 + SQ_Y3 + i - 1)
                    for half in range(2):
                        product_piece(banks[i % 2][:, LAT], S_OUT + 2 * i + half, o_hi, o_lo, SEQ, 8 * half,
                                      8, t)
            repeat(pe, DT // 4, out_quad)
            gap_chunks(U_GAP2, ADA_GAP2, 4, {1: (SQ_Y3, 7, SEQ), 20: (SQ_X3, 7, SEQ)})
            ffn(1, S_FFN1, SEQ, h1_hi, h1_lo, 32, lambda: turn_gap(ADA_GAP2, ADA_EARLY + ADA_GAP1))
            total_squares(SQ_Y4, 7, SEQ)


def weight_stream(np, w_ada, w_pool, w_qkv, w_o, w_gate_up, w_down):
    units = np.empty((UNITS, P, UNIT), np.float32)

    def ada_chunk(u, j):
        w = w_ada[j // ADA_CHUNKS][:, j % ADA_CHUNKS * 512:(j % ADA_CHUNKS + 1) * 512]
        units[u:u + 4] = w.reshape(4, 4, P, 512).transpose(0, 2, 1, 3).reshape(4, P, UNIT)

    def column_tile(u, w, j):
        units[u] = w[:, j * P:(j + 1) * P].reshape(DT, P, P).transpose(1, 0, 2).reshape(P, UNIT)

    def swiglu(layer):
        u, u_step, split_off, mac_off = STEPS[layer]
        gate_up, down = w_gate_up[layer], w_down[layer]

        def down_unit(at, c, h):
            w = down[c * 2 * P:(c + 1) * 2 * P, h * 1024:(h + 1) * 1024]
            units[at] = w.reshape(2, P, 8, P).transpose(1, 2, 0, 3).reshape(P, UNIT)

        for i, (j, up) in enumerate(((0, 0), (0, 1), (1, 0), (1, 1), (2, 0), (2, 1))):
            column_tile(u - 6 + i, gate_up, j + up * FT)
        for c in range(CHUNKS - 1):
            at = [u + c * u_step + off for off in split_off]
            column_tile(at[0], gate_up, 2 * c + 3)
            column_tile(at[1], gate_up, 2 * c + 3 + FT)
            down_unit(at[2], c, 0)
            down_unit(at[3], c, 1)
            if c < CHUNKS - 2:
                column_tile(at[4], gate_up, 2 * c + 4)
                column_tile(at[5], gate_up, 2 * c + 4 + FT)
            else:
                down_unit(at[4], c + 1, 0)
                down_unit(at[5], c + 1, 1)
            for n, off in enumerate(mac_off):
                j = ADA_EARLY + c
                w = w_ada[j // ADA_CHUNKS][n * 512:(n + 1) * 512, j % ADA_CHUNKS * 512:(j % ADA_CHUNKS + 1) * 512]
                units[u + c * u_step + off] = w.reshape(4, P, 512).transpose(1, 0, 2).reshape(P, UNIT)

    for j in range(8):
        ada_chunk(4 * j, j)
    for (kind, n), s in early_pieces().items():
        if kind == "piece":
            j, q = 8 + n // 8, n % 8
            w = w_ada[0][2 * q * P:(2 * q + 2) * P, j * 512:(j + 1) * 512].reshape(2, P, 512).transpose(1, 0, 2)
        elif kind == "pool":
            w = w_pool[0, n // 2].reshape(4, P, 4, P).transpose(1, 2, 0, 3)[:, n % 2 * 2:n % 2 * 2 + 2]
        else:
            continue
        units[s // 2, :, s % 2 * PIECE:(s % 2 + 1) * PIECE] = w.reshape(P, PIECE)
    swiglu(0)
    for i in range(ADA_GAP1):
        ada_chunk(U_GAP1 + 4 * i, ADA_EARLY + ADA_BESIDE + i)
    for m in range(2):
        column_tile(U_QKV + m, w_qkv[0], Q_TILES + m)
        w = w_qkv[0][m * 1024:(m + 1) * 1024, D + KV:]
        units[U_QKV + 2 + m] = w.reshape(8, P, KV).transpose(1, 0, 2).reshape(P, UNIT)
    for j in range(Q_TILES):
        column_tile(U_QKV + 4 + j, w_qkv[0], j)
    for j in range(DT):
        column_tile(U_OUT + j, w_o[0], j)
    for i in range(ADA_GAP2):
        ada_chunk(U_GAP2 + 4 * i, 2 * ADA_CHUNKS - ADA_GAP2 + i)
    swiglu(1)
    return units


def shape_tables(np):
    f = np.float32
    t = np.arange(SEQ)
    counts = np.stack([f(1) / (np.clip(t + w // 2, 0, SEQ) - np.clip(t - w // 2, 0, SEQ)).astype(f)
                       for w in WINDOWS])
    inv = f(1) / np.power(f(10000), np.arange(0, HEAD // 2, 2, dtype=f) / f(HEAD // 2))
    row, col = (t // 64).astype(f)[:, None] * inv, (t % 64).astype(f)[:, None] * inv
    angle = np.concatenate([row, row, col, col], axis=-1).T.astype(f)
    rope = np.stack([np.tile(np.cos(angle), (2, 1)), np.tile(np.sin(angle), (2, 1))], axis=1).astype(f)
    rotation = np.zeros((P, P), f)
    for m in range(P):
        half = m % (HEAD // 2) < HEAD // 4
        rotation[m + HEAD // 4 if half else m - HEAD // 4, m] = -1 if half else 1
    mask = np.zeros((P, 2, TOK), f)
    for qt in range(2):
        q = qt * P + np.arange(P)
        mask[:, qt, :SEQ] = np.where(np.abs(q[:, None] - t[None, :]) <= 128, 0, MASKED)
    pairs = np.array([[1, 0], [1, 0], [0, 1], [0, 1]], f)
    return (np.ascontiguousarray(np.broadcast_to(counts, (P, 4, SEQ))), np.ascontiguousarray(rope), rotation,
            np.eye(P, dtype=f), pairs, mask)


def kernel(x, c, ctx, c_ctx, w_ada, b_ada, norm_pre_mix, norm_post_mix, norm_pre_ffn, norm_post_ffn,
           w_pool, pool_scale, w_qkv, w_o, attn_sinks, w_gate_up, w_down):
    import numpy as np
    import concourse.bacc as bacc
    from concourse.bass_utils import run_bass_kernel_spmd

    def feature_major(a):
        return np.asarray(a).reshape(-1, DT, P).transpose(2, 1, 0)

    def twice(a):
        return np.repeat(a[..., None], 2, axis=-1)

    gains = np.stack([np.asarray(g)[layer] for layer in range(2)
                      for g in (norm_pre_mix, norm_post_mix, norm_pre_ffn, norm_post_ffn)])
    counts, rope, rotation, identity, pairs, mask = shape_tables(np)
    arrays = {
        "stream": weight_stream(np, *(np.asarray(a) for a in (w_ada, w_pool, w_qkv, w_o, w_gate_up, w_down))),
        "x_in": np.concatenate([feature_major(x), feature_major(ctx)], axis=2),
        "cond": np.concatenate([feature_major(c), feature_major(c_ctx)], axis=2),
        "ada_bias": twice(np.asarray(b_ada).reshape(12 * DT, P).T),
        "gains": twice(gains.reshape(8, DT, P).transpose(2, 0, 1)),
        "pool_gain": np.asarray(pool_scale)[0].reshape(DT, P).T,
        "inv_counts": counts, "rope": rope, "rotation": rotation, "identity": identity, "pairs": pairs,
        "mask": mask, "sinks": np.broadcast_to(np.asarray(attn_sinks)[0], (P, N_HEADS)),
    }
    arrays = {name: np.ascontiguousarray(a) for name, a in arrays.items()}
    nc = bacc.Bacc("TRN2", target_bir_lowering=False, num_devices=1)
    args = [nc.dram_tensor(name, a.shape, F32, kind="ExternalInput").ap() for name, a in arrays.items()]
    out = nc.dram_tensor("out", (P, DT, SEQ), F32, kind="ExternalOutput").ap()
    build_trunk(nc, *args, out)
    got = run_bass_kernel_spmd(nc, [arrays], core_ids=[0]).results[0]["out"]
    return got.transpose(2, 1, 0).reshape(1, SEQ, D)
```
